# Optimizing a Trainium2 kernel written in Bass

```python
import math
import jax, jax.numpy as jnp
from jax import lax
import numpy as np

D_MODEL = 1024
BATCH = 1
SEQ = 256
DEPTH = 2

CHUNK = 64
N_MIXERS = 2
MIX_WIDTH = D_MODEL // 2
SGU_CHUNK = 128
SGU_HEADS = 4
SGU_HEAD_DIM = MIX_WIDTH // SGU_HEADS
CONV_WIDTH = 3
N_MEM = 256
XA_HEADS = 4
XA_HEAD_DIM = MIX_WIDTH // XA_HEADS
N_EXPERTS = 16
N_GROUPS = 4
GROUP_SIZE = N_EXPERTS // N_GROUPS
TOP_K = 2
D_EXPERT = D_MODEL // 2
N_A = (DEPTH + 1) // 2
N_B = DEPTH // 2
ALPHA = (2 * DEPTH) ** 0.25
BETA = (8 * DEPTH) ** -0.25
LN_EPS = 1e-5


def layer_norm(x, g, b):
    xf = x.astype(jnp.float32)
    mu = xf.mean(-1, keepdims=True)
    var = jnp.square(xf - mu).mean(-1, keepdims=True)
    y = (xf - mu) * lax.rsqrt(var + LN_EPS) * g.astype(jnp.float32) + b.astype(jnp.float32)
    return y.astype(x.dtype)

def spatial_gating(z, ln_g, ln_b, w_s, b_s):
    u, v = jnp.split(z, 2, axis=-1)
    v = layer_norm(v, ln_g, ln_b)
    bsz, seq, _ = v.shape
    v = v.reshape(bsz, seq // SGU_CHUNK, SGU_CHUNK, SGU_HEADS, SGU_HEAD_DIM)
    frame_chunk = jnp.arange(SGU_CHUNK) // CHUNK
    mask = frame_chunk[:, None] >= frame_chunk[None, :]
    w = jnp.where(mask[None], w_s, jnp.zeros_like(w_s))
    mixed = jnp.einsum('hij,bcjhd->bcihd', w, v) + b_s.T[None, None, :, :, None]
    return u * mixed.reshape(bsz, seq, MIX_WIDTH)

def short_conv_mixer(z, conv_w):
    bg, cg, xt = jnp.split(z, 3, axis=-1)
    h = cg * xt
    h = lax.conv_general_dilated(
        h, conv_w[:, None, :].astype(h.dtype), window_strides=(1,),
        padding=[(CONV_WIDTH - 1, 0)], dimension_numbers=('NWC', 'WIO', 'NWC'),
        feature_group_count=MIX_WIDTH)
    return bg * h

def memory_cross_attention(q, mem, w_kv):
    bsz, seq, _ = q.shape
    n_mem = mem.shape[1]
    k, v = jnp.split(mem @ w_kv, 2, axis=-1)
    q = q.reshape(bsz, seq, XA_HEADS, XA_HEAD_DIM)
    k = k.reshape(bsz, n_mem, XA_HEADS, XA_HEAD_DIM)
    v = v.reshape(bsz, n_mem, XA_HEADS, XA_HEAD_DIM)
    s = jnp.einsum('bshd,bmhd->bhsm', q, k).astype(jnp.float32) * (XA_HEAD_DIM ** -0.5)
    p = jax.nn.softmax(s, axis=-1).astype(v.dtype)
    o = jnp.einsum('bhsm,bmhd->bshd', p, v)
    return o.reshape(bsz, seq, MIX_WIDTH)

def grouped_moe(x, router_w, router_b, w_gate, w_up, w_down):
    bsz, seq, d = x.shape
    xt = x.reshape(-1, d)
    scores = jax.nn.sigmoid(jnp.dot(xt.astype(jnp.float32), router_w.astype(jnp.float32)))
    sel = scores + router_b.astype(jnp.float32)
    group_score = lax.top_k(sel.reshape(-1, N_GROUPS, GROUP_SIZE), TOP_K)[0].sum(-1)
    top_group = jnp.argmax(group_score, axis=-1)
    expert_group = jnp.arange(N_EXPERTS) // GROUP_SIZE
    in_group = expert_group[None, :] == top_group[:, None]
    _, idx = lax.top_k(jnp.where(in_group, sel, -jnp.inf), TOP_K)
    gate = jnp.take_along_axis(scores, idx, axis=-1)
    gate = gate / gate.sum(-1, keepdims=True)
    combine = jnp.einsum('tk,tke->te', gate,
                         jax.nn.one_hot(idx, N_EXPERTS, dtype=jnp.float32)).astype(x.dtype)
    out = jnp.zeros_like(xt)
    for e in range(N_EXPERTS):
        h = jax.nn.silu(xt @ w_gate[e]) * (xt @ w_up[e])
        out = out + combine[:, e:e + 1] * (h @ w_down[e])
    return out.reshape(bsz, seq, d)

def first_inputs(seed: int = 0) -> dict:
    key = jax.random.key(seed)
    ks = jax.random.split(key, 20)
    d = D_MODEL

    def nrm(k, shape, scale):
        return jax.random.normal(k, shape, jnp.float32) * scale

    x = nrm(ks[0], (BATCH, SEQ, d), 1.0)
    mem = nrm(ks[1], (BATCH, N_MEM, d), 1.0)
    w_in_a = nrm(ks[2], (N_A, d, 3 * MIX_WIDTH), d ** -0.5)
    sgu_ln_g = 1.0 + nrm(ks[3], (N_A, MIX_WIDTH), 0.02)
    sgu_ln_b = nrm(ks[4], (N_A, MIX_WIDTH), 0.02)
    sgu_w = nrm(ks[5], (N_A, SGU_HEADS, SGU_CHUNK, SGU_CHUNK), SGU_CHUNK ** -0.5)
    sgu_b = 1.0 + nrm(ks[6], (N_A, SGU_HEADS, SGU_CHUNK), 0.02)
    w_in_b = nrm(ks[7], (N_B, d, 4 * MIX_WIDTH), d ** -0.5)
    conv_w = nrm(ks[8], (N_B, CONV_WIDTH, MIX_WIDTH), CONV_WIDTH ** -0.5)
    kv_scale = jnp.concatenate([jnp.ones((MIX_WIDTH,), jnp.float32),
                                jnp.full((MIX_WIDTH,), BETA, jnp.float32)]) * (d ** -0.5)
    w_kv = nrm(ks[9], (DEPTH, d, 2 * MIX_WIDTH), 1.0) * kv_scale
    w_out = nrm(ks[10], (DEPTH, 2 * MIX_WIDTH, d), BETA * (2 * MIX_WIDTH) ** -0.5)
    ln1_g = 1.0 + nrm(ks[11], (DEPTH, d), 0.02)
    ln1_b = nrm(ks[12], (DEPTH, d), 0.02)
    router_w = nrm(ks[13], (d, N_EXPERTS), d ** -0.5)
    router_b = nrm(ks[14], (N_EXPERTS,), 0.01)
    w_gate = nrm(ks[15], (DEPTH, N_EXPERTS, d, D_EXPERT), d ** -0.5)
    w_up = nrm(ks[16], (DEPTH, N_EXPERTS, d, D_EXPERT), d ** -0.5)
    w_down = nrm(ks[17], (DEPTH, N_EXPERTS, D_EXPERT, d), BETA * D_EXPERT ** -0.5)
    ln2_g = 1.0 + nrm(ks[18], (DEPTH, d), 0.02)
    ln2_b = nrm(ks[19], (DEPTH, d), 0.02)
    return {"x": x, "mem": mem, "w_in_a": w_in_a, "sgu_ln_g": sgu_ln_g, "sgu_ln_b": sgu_ln_b,
            "sgu_w": sgu_w, "sgu_b": sgu_b, "w_in_b": w_in_b, "conv_w": conv_w,
            "w_kv": w_kv, "w_out": w_out, "ln1_g": ln1_g, "ln1_b": ln1_b,
            "router_w": router_w, "router_b": router_b, "w_gate": w_gate, "w_up": w_up,
            "w_down": w_down, "ln2_g": ln2_g, "ln2_b": ln2_b}

def first_block(x, mem, w_in_a, sgu_ln_g, sgu_ln_b, sgu_w, sgu_b, w_in_b, conv_w,
              w_kv, w_out, ln1_g, ln1_b, router_w, router_b, w_gate, w_up, w_down,
              ln2_g, ln2_b):
    for i in range(DEPTH):
        j = i // N_MIXERS
        if i % N_MIXERS == 0:
            z = x @ w_in_a[j]
            uv = jax.nn.gelu(z[..., :2 * MIX_WIDTH], approximate=False)
            tok = spatial_gating(uv, sgu_ln_g[j], sgu_ln_b[j], sgu_w[j], sgu_b[j])
            q = z[..., 2 * MIX_WIDTH:]
        else:
            z = x @ w_in_b[j]
            tok = short_conv_mixer(z[..., :3 * MIX_WIDTH], conv_w[j])
            q = z[..., 3 * MIX_WIDTH:]
        xa = memory_cross_attention(q, mem, w_kv[i])
        o = jnp.concatenate([tok, xa], axis=-1) @ w_out[i]
        x = layer_norm(ALPHA * x + o, ln1_g[i], ln1_b[i])
        f = grouped_moe(x, router_w, router_b, w_gate[i], w_up[i], w_down[i])
        x = layer_norm(ALPHA * x + f, ln2_g[i], ln2_b[i])
    return x


H_A = 8
NOPE = 64
ROPE_D = 32
V_A = 64
Q_LORA = 256
KV_LORA = 128
W_A = H_A * V_A
H_B = 8
HD_B = 64
W_B = H_B * HD_B
H_C = 8
HD_C = 64
W_C = H_C * HD_C
DECAY_LORA = 64
AAA_LORA = 64
MV_LORA = 32
SHIFT_COLS = 3 * W_C + DECAY_LORA + AAA_LORA
ROPE_THETA = 10000.0
Q_BLOCK = 128
RWKV_DECAY_SCALE = 0.606531
GN_EPS = 64e-5
EPS = 1e-6
NEG_INF = -1e30

IN_SIZES = (Q_LORA, KV_LORA, ROPE_D, W_A,
            W_B, W_B, W_B, H_B, W_B,
            SHIFT_COLS, W_C,
            3 * D_MODEL)
IN_COLS = sum(IN_SIZES)
RWKV_SIZES = (W_C, W_C, W_C, DECAY_LORA, AAA_LORA)


def rmsnorm(x, g, eps=EPS):
    xf = x.astype(jnp.float32)
    y = xf * lax.rsqrt(jnp.mean(xf * xf, axis=-1, keepdims=True) + eps)
    return (y * g.astype(jnp.float32)).astype(x.dtype)

def split_cols(p, sizes):
    idx = np.cumsum(np.array(sizes))[:-1].tolist()
    return jnp.split(p, idx, axis=-1)

def rope_tables(seq):
    inv = ROPE_THETA ** (-jnp.arange(0, ROPE_D, 2, dtype=jnp.float32) / ROPE_D)
    ang = jnp.arange(seq, dtype=jnp.float32)[:, None] * inv[None, :]
    return jnp.cos(ang)[:, None, :], jnp.sin(ang)[:, None, :]

def apply_rope(x, cos, sin):
    half = ROPE_D // 2
    x1 = x[..., :half].astype(jnp.float32)
    x2 = x[..., half:].astype(jnp.float32)
    out = jnp.concatenate([x1 * cos - x2 * sin, x2 * cos + x1 * sin], axis=-1)
    return out.astype(x.dtype)

def causal_block_attention(q, k, v, cum=None):
    B, H, S, Dk = q.shape
    Dv = v.shape[-1]
    nb = S // Q_BLOCK
    scale = Dk ** -0.5
    kpos = jnp.arange(S)
    q_blocks = q.reshape(B, H, nb, Q_BLOCK, Dk).transpose(2, 0, 1, 3, 4)
    use_decay = cum is not None
    xs = (jnp.arange(nb), q_blocks)
    if use_decay:
        xs = xs + (cum.reshape(B, H, nb, Q_BLOCK).transpose(2, 0, 1, 3),)

    def block(args):
        i, qb = args[0], args[1]
        s = jnp.einsum('bhqd,bhkd->bhqk', qb, k).astype(jnp.float32) * scale
        if use_decay:
            s = s + args[2][..., :, None] - cum[:, :, None, :]
        qpos = i * Q_BLOCK + jnp.arange(Q_BLOCK)
        s = jnp.where(kpos[None, :] <= qpos[:, None], s, NEG_INF)
        p = jax.nn.softmax(s, axis=-1)
        return jnp.einsum('bhqk,bhkd->bhqd', p.astype(v.dtype), v)

    o = lax.map(block, xs)
    return o.transpose(1, 0, 3, 2, 4).reshape(B, S, H * Dv)

def mla_branch(c_q, c_kv, k_r, gate, qa_g, w_uq, kva_g, w_ukv, q_g, knope_g, krope_g, cos, sin):
    B, S, _ = c_q.shape
    q = (rmsnorm(c_q, qa_g) @ w_uq).reshape(B, S, H_A, NOPE + ROPE_D)
    q = rmsnorm(q, q_g)
    q = jnp.concatenate([q[..., :NOPE], apply_rope(q[..., NOPE:], cos, sin)], axis=-1)
    kv = (rmsnorm(c_kv, kva_g) @ w_ukv).reshape(B, S, H_A, NOPE + V_A)
    k_nope = rmsnorm(kv[..., :NOPE], knope_g)
    v = kv[..., NOPE:]
    k_rope = apply_rope(rmsnorm(k_r, krope_g)[:, :, None, :], cos, sin)
    k = jnp.concatenate([k_nope, jnp.broadcast_to(k_rope, (B, S, H_A, ROPE_D))], axis=-1)
    o = causal_block_attention(q.transpose(0, 2, 1, 3), k.transpose(0, 2, 1, 3), v.transpose(0, 2, 1, 3))
    return o * jax.nn.silu(gate)

def fox_branch(fq, fk, fv, ff, gate, b_f, q_g, k_g):
    B, S, _ = fq.shape
    q = rmsnorm(fq.reshape(B, S, H_B, HD_B), q_g)
    k = rmsnorm(fk.reshape(B, S, H_B, HD_B), k_g)
    v = fv.reshape(B, S, H_B, HD_B)
    log_f = jax.nn.log_sigmoid((ff + b_f).astype(jnp.float32))
    cum = jnp.cumsum(log_f, axis=1).transpose(0, 2, 1)
    o = causal_block_attention(q.transpose(0, 2, 1, 3), k.transpose(0, 2, 1, 3), v.transpose(0, 2, 1, 3), cum)
    return o * jax.nn.silu(gate)

def rwkv7_scan(r, w, k, v, kk, a):
    B, S, H, N = r.shape

    def step(state, inp):
        r_t, w_t, k_t, v_t, kk_t, a_t = inp
        sa = jnp.einsum('bhvk,bhk->bhv', state, -kk_t)
        state = (state * w_t[:, :, None, :] + sa[..., None] * (kk_t * a_t)[:, :, None, :]
                 + v_t[..., None] * k_t[:, :, None, :])
        return state, jnp.einsum('bhvk,bhk->bhv', state, r_t)

    xs = tuple(t.transpose(1, 0, 2, 3) for t in (r, w, k, v, kk, a))
    _, y = lax.scan(step, jnp.zeros((B, H, N, N), jnp.float32), xs)
    return y.transpose(1, 0, 2, 3)

def rwkv_branch(r, k, v, wl, al, gate, w0, w_up, a0, a_up, k_k, k_a, r_k, lnx_g, lnx_b):
    B, S, _ = r.shape
    f32 = jnp.float32
    heads = lambda t: t.astype(f32).reshape(B, S, H_C, HD_C)
    w = jnp.exp(-RWKV_DECAY_SCALE * jax.nn.sigmoid((w0 + jnp.tanh(wl) @ w_up).astype(f32)))
    a = jax.nn.sigmoid((a0 + al @ a_up).astype(f32))
    kk = heads(k * k_k)
    kk = kk / jnp.maximum(jnp.sqrt(jnp.sum(kk * kk, axis=-1, keepdims=True)), 1e-12)
    k_mod = k.astype(f32) * (1.0 + (a - 1.0) * k_a.astype(f32))
    r_h, w_h, k_h, v_h, a_h = heads(r), heads(w), heads(k_mod), heads(v), heads(a)
    y = rwkv7_scan(r_h, w_h, k_h, v_h, kk, a_h)
    mu = jnp.mean(y, axis=-1, keepdims=True)
    var = jnp.mean(jnp.square(y - mu), axis=-1, keepdims=True)
    y = ((y - mu) * lax.rsqrt(var + GN_EPS)).reshape(B, S, W_C) * lnx_g.astype(f32) + lnx_b.astype(f32)
    bonus = jnp.sum(r_h * k_h * r_k.astype(f32), axis=-1, keepdims=True) * v_h
    out = (y + bonus.reshape(B, S, W_C)) * jax.nn.silu(gate.astype(f32))
    return out.astype(gate.dtype)

def second_inputs(seed: int = 0) -> dict:
    key = jax.random.key(seed)
    ks = iter(jax.random.split(key, 48))
    f32 = jnp.float32
    L, Lv = DEPTH, DEPTH - 1

    def nrm(shape, scale):
        return scale * jax.random.normal(next(ks), shape, f32)

    def gain(shape):
        return 1.0 + nrm(shape, 0.02)

    x = jax.random.normal(next(ks), (BATCH, SEQ, D_MODEL), f32)
    return {
        "x": x,
        "norm_g": gain((L, D_MODEL)),
        "w_in": nrm((L, D_MODEL, IN_COLS), D_MODEL ** -0.5),
        "mla_qa_g": gain((L, Q_LORA)),
        "mla_w_uq": nrm((L, Q_LORA, H_A * (NOPE + ROPE_D)), Q_LORA ** -0.5),
        "mla_kva_g": gain((L, KV_LORA)),
        "mla_w_ukv": nrm((L, KV_LORA, H_A * (NOPE + V_A)), KV_LORA ** -0.5),
        "mla_q_g": gain((L, NOPE + ROPE_D)),
        "mla_knope_g": gain((L, NOPE)),
        "mla_krope_g": gain((L, ROPE_D)),
        "fox_b_f": jnp.broadcast_to(jnp.linspace(1.0, 6.0, H_B, dtype=f32), (L, H_B)) + nrm((L, H_B), 0.1),
        "fox_q_g": gain((L, HD_B)),
        "fox_k_g": gain((L, HD_B)),
        "rwkv_mu": jax.random.uniform(next(ks), (L, SHIFT_COLS), f32),
        "rwkv_w0": nrm((L, W_C), 1.0),
        "rwkv_w_up": nrm((L, DECAY_LORA, W_C), 0.5 * DECAY_LORA ** -0.5),
        "rwkv_a0": nrm((L, W_C), 0.5),
        "rwkv_a_up": nrm((L, AAA_LORA, W_C), 0.5 * AAA_LORA ** -0.5),
        "rwkv_k_k": 0.85 + nrm((L, W_C), 0.1),
        "rwkv_k_a": 1.0 + nrm((L, W_C), 0.1),
        "rwkv_r_k": nrm((L, H_C, HD_C), 0.1),
        "rwkv_lnx_g": gain((L, W_C)),
        "rwkv_lnx_b": nrm((L, W_C), 0.02),
        "rwkv_v0": nrm((Lv, W_C), 0.5),
        "rwkv_v_down": nrm((Lv, W_C, MV_LORA), W_C ** -0.5),
        "rwkv_v_up": nrm((Lv, MV_LORA, W_C), 0.5 * MV_LORA ** -0.5),
        "w_pa": nrm((L, W_A, D_MODEL), W_A ** -0.5),
        "w_pb": nrm((L, W_B, D_MODEL), W_B ** -0.5),
        "w_pc": nrm((L, W_C, D_MODEL), W_C ** -0.5),
        "w_out": nrm((L, D_MODEL, D_MODEL), D_MODEL ** -0.5),
    }

def second_block(x, norm_g, w_in, mla_qa_g, mla_w_uq, mla_kva_g, mla_w_ukv, mla_q_g, mla_knope_g,
              mla_krope_g, fox_b_f, fox_q_g, fox_k_g, rwkv_mu, rwkv_w0, rwkv_w_up, rwkv_a0, rwkv_a_up,
              rwkv_k_k, rwkv_k_a, rwkv_r_k, rwkv_lnx_g, rwkv_lnx_b, rwkv_v0, rwkv_v_down, rwkv_v_up,
              w_pa, w_pb, w_pc, w_out):
    S = x.shape[1]
    cos, sin = rope_tables(S)
    v_first = None
    for l in range(DEPTH):
        h = rmsnorm(x, norm_g[l])
        p = h @ w_in[l]
        (c_q, c_kv, k_r, gate_a, fq, fk, fv, ff, gate_b,
         shift_cols, gate_c, merge_cols) = split_cols(p, IN_SIZES)

        o_a = mla_branch(c_q, c_kv, k_r, gate_a, mla_qa_g[l], mla_w_uq[l], mla_kva_g[l], mla_w_ukv[l],
                         mla_q_g[l], mla_knope_g[l], mla_krope_g[l], cos, sin)
        o_b = fox_branch(fq, fk, fv, ff, gate_b, fox_b_f[l], fox_q_g[l], fox_k_g[l])
        prev = jnp.pad(shift_cols, ((0, 0), (1, 0), (0, 0)))[:, :-1]
        shifted = shift_cols + rwkv_mu[l] * (prev - shift_cols)
        r, k, v, wl, al = split_cols(shifted, RWKV_SIZES)
        if l == 0:
            v_first = v
        else:
            nu = jax.nn.sigmoid(rwkv_v0[l - 1] + (v @ rwkv_v_down[l - 1]) @ rwkv_v_up[l - 1])
            v = v + (v_first - v) * nu
        o_c = rwkv_branch(r, k, v, wl, al, gate_c, rwkv_w0[l], rwkv_w_up[l], rwkv_a0[l], rwkv_a_up[l],
                          rwkv_k_k[l], rwkv_k_a[l], rwkv_r_k[l], rwkv_lnx_g[l], rwkv_lnx_b[l])

        g_a, g_b, g_c = jnp.split(merge_cols, 3, axis=-1)
        merged = (jax.nn.sigmoid(g_a) * (o_a @ w_pa[l])
                  + jax.nn.sigmoid(g_b) * (o_b @ w_pb[l])
                  + jax.nn.sigmoid(g_c) * (o_c @ w_pc[l]))
        x = x + (merged @ w_out[l]).astype(x.dtype)
    return x


def setup_inputs(seed=0):
    out = dict(first_inputs(seed))
    for name, value in second_inputs(seed + 1).items():
        if name != "x":
            out[name + "_2"] = value
    return out


def reference(
    x, mem, w_in_a, sgu_ln_g, sgu_ln_b, sgu_w, sgu_b, w_in_b, conv_w, w_kv, w_out, ln1_g, ln1_b,
    router_w, router_b, w_gate, w_up, w_down, ln2_g, ln2_b, norm_g_2, w_in_2, mla_qa_g_2,
    mla_w_uq_2, mla_kva_g_2, mla_w_ukv_2, mla_q_g_2, mla_knope_g_2, mla_krope_g_2, fox_b_f_2,
    fox_q_g_2, fox_k_g_2, rwkv_mu_2, rwkv_w0_2, rwkv_w_up_2, rwkv_a0_2, rwkv_a_up_2, rwkv_k_k_2,
    rwkv_k_a_2, rwkv_r_k_2, rwkv_lnx_g_2, rwkv_lnx_b_2, rwkv_v0_2, rwkv_v_down_2, rwkv_v_up_2,
    w_pa_2, w_pb_2, w_pc_2, w_out_2,
):
    x = first_block(
        x, mem, w_in_a, sgu_ln_g, sgu_ln_b, sgu_w, sgu_b, w_in_b, conv_w, w_kv, w_out, ln1_g,
        ln1_b, router_w, router_b, w_gate, w_up, w_down, ln2_g, ln2_b,
    )
    return second_block(
        x, norm_g_2, w_in_2, mla_qa_g_2, mla_w_uq_2, mla_kva_g_2, mla_w_ukv_2, mla_q_g_2,
        mla_knope_g_2, mla_krope_g_2, fox_b_f_2, fox_q_g_2, fox_k_g_2, rwkv_mu_2, rwkv_w0_2,
        rwkv_w_up_2, rwkv_a0_2, rwkv_a_up_2, rwkv_k_k_2, rwkv_k_a_2, rwkv_r_k_2, rwkv_lnx_g_2,
        rwkv_lnx_b_2, rwkv_v0_2, rwkv_v_down_2, rwkv_v_up_2, w_pa_2, w_pb_2, w_pc_2, w_out_2,
    )


_drawn_inputs = setup_inputs


def setup_inputs(seed=0):
    import zlib

    import numpy as np

    out = dict(_drawn_inputs(seed))
    spreads = {}
    factors = {'sgu_ln_g': 3.352,
     'sgu_b': 2.82,
     'mla_qa_g_2': 8.0,
     'mla_kva_g_2': 8.0,
     'mla_q_g_2': 8.0,
     'mla_knope_g_2': 8.0,
     'mla_krope_g_2': 8.0,
     'fox_q_g_2': 8.0,
     'fox_k_g_2': 8.0,
     'rwkv_k_k_2': 4.502,
     'rwkv_lnx_g_2': 6.327,
     'rwkv_lnx_b_2': 6.379}
    for name, (base, spread) in spreads.items():
        noise = np.random.default_rng([zlib.crc32(name.encode()), seed]).standard_normal(out[name].shape)
        drawn = base * np.exp(spread * noise) if base else spread * noise
        out[name] = __import__('jax').numpy.asarray(drawn.astype(out[name].dtype))
    for name, factor in factors.items():
        out[name] = (out[name] * factor).astype(out[name].dtype)
    return out
```

```python
import concourse.bass as bass
from concourse import mybir
from contextlib import ExitStack

P = 128
T = 256
TT = T // P
D = 1024
KD = D // P
MIX = 512
KM = MIX // P
NHX = 4
XSCALE = P ** -0.5
NE, NG, GS = 16, 4, 4
F = 512
DEPTH = 2
ALPHA = (2 * DEPTH) ** 0.25
LN_EPS, RMS_EPS, GN_EPS = 1e-5, 1e-6, 64e-5
NH = 8
HC = 64
NOPE, ROPE, QK = 64, 32, 96
HALF = ROPE // 2
FOXK = 66
LAT = 416
CH = 64
DECAY = -0.606531
SLOT = 4096
RING = 4
PER_EXPERT = 3
PAIRS = NE * TT + 1
EPB = 4
NDB = 5

LOADS_FIRST = [[SLOT] * 7, [SLOT] * 8]
LOADS_SECOND = ([KD * LAT, SLOT, 1536, 1024, SLOT, SLOT, SLOT, SLOT, SLOT, SLOT, SLOT, KD * P] + [SLOT] * 12)

C_ID, C_STRICT, C_INCL, C_BLOCK, C_TRI, C_ONES, C_ALPHA, C_LEV = [P * n for n in range(8)]
LEVELS = 6
C_CAUSAL = C_LEV + LEVELS * P
C_SCAN = C_CAUSAL + 3 * P
C_SGU = C_SCAN + 4 * P
C_COS = C_SGU + P
C_SIN = C_COS + TT * HALF
C_SEL = C_SIN + TT * HALF
C_TIE = C_SEL + 4 * NH
NCONST = C_TIE + GS * GS

CP_CONV = 0
CP_LAYER = 13 + 6 * 4
NCOLP = 12 + DEPTH * CP_LAYER
W0, A0, KK, KA, RK, V0 = range(6)

R_SGUG, R_SGUB, R_SGUBIAS, R_RB = 0, MIX, 2 * MIX, 3 * MIX
NROWA = R_RB + NE
ROWS = {}
NROWS = 0
for _name, _n in (("norm", D), ("qa", 256), ("kva", 128), ("q", QK), ("kn", NOPE), ("kr", ROPE), ("fq", HC),
                  ("fk", HC), ("bf", NH), ("lg", MIX), ("lb", MIX)):
    ROWS[_name] = (NROWS, _n)
    NROWS += _n


def two_blocks(nc, x0, x0T, memT0, sguT, wfirst0, wfirst1, wmoe, wsecond, wff, lora, rw, consts, colp, rowa, lnrows, rows2, out):
    f32 = mybir.dt.float32
    ALU = mybir.AluOpType
    ACT = mybir.ActivationFunctionType
    AX = mybir.AxisListType.X
    MUL, ADD, SUB, MAX, MIN = ALU.mult, ALU.add, ALU.subtract, ALU.max, ALU.min

    ctx = ExitStack()
    with ctx:
        def sb(name, n):
            return ctx.enter_context(nc.sbuf_tensor(name, [P, n], f32))[:, :]

        semaphores = {}

        def sem(name):
            if name not in semaphores:
                semaphores[name] = ctx.enter_context(nc.semaphore(name))
            return semaphores[name]

        def v3(ap, a):
            return ap.rearrange("p (a b) -> p a b", a=a)

        def v4(ap, a, b):
            return ap.rearrange("p (a b c) -> p a b c", a=a, b=b)

        ring = sb("ring", RING * SLOT)
        cst = sb("cst", NCONST)
        col = sb("col", NCOLP)
        x_nat = v3(sb("x_nat", TT * D), TT)
        y_nat = v3(sb("y_nat", TT * D), TT)
        xT = v3(sb("xT", KD * T), KD)
        rows = sb("rows", NROWS)
        rwt = v3(sb("rwt", KD * NE), KD)
        small = sb("small", 640)
        ARENA = 24200
        arena = sb("arena", ARENA)
        banks = [ctx.enter_context(nc.psum_tensor(f"bank{b}", [P, 512], f32)) for b in range(8)]

        class Carve:
            def __init__(self, at=0):
                self.at = at

            def __call__(self, *shape):
                n = 1
                for s in shape:
                    n *= s
                ap = arena[:, self.at:self.at + n]
                self.at += n
                assert self.at <= ARENA, self.at
                if len(shape) == 2:
                    return v3(ap, shape[0])
                if len(shape) == 3:
                    return v4(ap, shape[0], shape[1])
                return ap

        def bc(ap, *shape):
            return ap.to_broadcast(list(shape))

        def mat(c):
            return cst[:, c:c + P]

        def mat4(c):
            return bc(mat(c).unsqueeze(1), P, 4, P)

        ident = mat(C_ID)

        def per_channel(ap, n):
            return bc(ap.unsqueeze(2), P, ap.shape[1], n)

        def per_column(ap, n):
            return bc(ap.unsqueeze(1), P, n, ap.shape[1])

        S_BN, S_MV, S_VAR, S_RSTD = small[:, 0:24], small[:, 24:28], small[:, 28:60], small[:, 60:92]
        S_MX, S_NM, S_SUM, S_RS = small[:, 92:108], small[:, 108:124], small[:, 124:140], small[:, 140:156]
        S_SC, S_SEL, S_COMB = small[:, 160:192], small[:, 192:224], small[:, 224:256]
        S_GSC, S_GRANK, S_RANK = small[:, 256:264], small[:, 264:272], small[:, 272:304]
        S_BIG, S_BIG2 = small[:, 304:432], small[:, 432:560]
        S_MARK = small[:, 600:604]

        c1 = Carve()
        memT = c1(KD, T)
        qT, kT = c1(4, T), c1(4, T)
        vmem = c1(TT, MIX)
        catT = c1(KD, T)
        uT = c1(4, T)
        vv = c1(TT, MIX)
        cgT, tmpT = c1(4, T), c1(4, T)
        hpad = c1(4, T + 2)
        sgw = c1(4, P)
        rowa_sb = c1(NROWA)
        xsc, xPT = c1(NHX, TT, T), c1(NHX, TT, T)
        sg, hh = c1(TT, F), c1(TT, F)
        hT = c1(TT, KM, P)
        bgT = uT

        c2 = Carve()
        gates = c2(2, 4, T)
        sh = c2(13, T)
        rlT, klT, vlT = sh[:, 0:4, :], sh[:, 4:8, :], sh[:, 8:12, :]
        lora_sb = c2(1152)
        wup, vdown, vup = lora_sb[:, 0:512], v3(lora_sb[:, 512:640], 4), lora_sb[:, 640:1152]
        wff_sb = c2(KD, NH)
        oT = c2(4, T)
        vfirst = c2(4, T)
        merged = y_nat
        base2 = c2.at
        ca = Carve(base2)
        pcol = ca(2, T + 1)
        cnat = ca(TT, LAT)
        dcol = v3(arena[:, ca.at - TT * LAT:ca.at - TT * LAT + 2 * T], 2)
        cT = ca(3, T)
        PT = v3(arena[:, ca.at - 3 * T:ca.at], 2)
        qn, kn = ca(TT, NH, QK), ca(TT, NH, QK)
        vn2 = [ca(TT, NH, HC), ca(TT, NH, HC)]
        qTt, kTt = ca(NH, T), ca(NH, T)
        Pm = ca(NH, 3 * P)
        ffn = ca(3 * TT * NH)
        sq = Pm.rearrange("p a b -> p (a b)")
        sgm = v3(qTt.rearrange("p a b -> p (a b)"), TT)
        cr = Carve(base2)
        t_at = cr.at
        lw, cum, pp, pinv, pex, aa, kk, km, t1 = (cr(4, P) for _ in range(9))
        ci = Carve(t_at)
        Tm, TTm, Xm, Nl = (ci(2, 4, P) for _ in range(4))
        rk = cr(4, P)
        tw = cr(P)
        NTm, MTm, AkT, AbT = (cr(2, 4, P) for _ in range(4))
        Vn, Kn, Rn, Bn, Kp = (cr(MIX) for _ in range(5))
        Hs = cr(2, MIX)
        states = [cr(MIX) for _ in range(3)]
        pcs, pc0 = cr(8), cr(16)

        def flat2(ap):
            return ap.rearrange("p a b -> p (a b)")

        v_mid = flat2(t1)[0:32, 0:T]
        nuT = v3(arena[:, t_at + 5 * 512:t_at + 7 * 512], 4)
        vdiff = v3(arena[:, t_at:t_at + 2 * 512], 4)
        Wn, mv = flat2(Xm[:, 0, :, :]), flat2(Xm[:, 1, :, :])
        uv, yv = flat2(Nl[:, 0, :, :]), flat2(Nl[:, 1, :, :])
        QT = NTm
        GT = v4(MTm.rearrange("p a b c -> p (a b c)"), 2, NH)
        ysq = flat2(Tm[:, 0, :, :])

        def rowv(name):
            a, n = ROWS[name]
            return rows[:, a:a + n]

        def colv(l, which):
            a = 12 + l * CP_LAYER + 13 + 4 * which
            return col[:, a:a + 4]

        def hc(ap, h):
            return ap[:, h * HC:(h + 1) * HC]

        bank_full = [sem(f"bank_full{b}") for b in range(8)]
        bank_free = [sem(f"bank_free{b}") for b in range(8)]
        dve_step, act_step = sem("dve_step"), sem("act_step")

        class Counts:
            def __init__(self):
                self.seen, self.sent = {}, {}
                self.last, self.value = None, 0

            def next(self, name):
                self.seen[name] = self.seen.get(name, 0) + 1
                return self.seen[name]

            def sends(self, s):
                first = 1 if s in bank_free else 0
                self.sent[s.name] = self.sent.get(s.name, first) + 1
                self.last, self.value = s, self.sent[s.name]
                return 1

        class TensorCounts(Counts):
            def __init__(self):
                super().__init__()
                self.uses = [0] * 8
                self.slots = 0
                self.open = False
                self.pending = 0

            def reuse(self, b):
                self.uses[b] += 1
                return self.uses[b]

            def used(self, b):
                return self.uses[b] + 1

            def close(self):
                if self.open:
                    self.pending += 1
                    self.open = False

        block = ctx.enter_context(nc.Block())
        per_body = EPB * PER_EXPERT

        @block.sync
        def _(sp):
            n = 0

            def load(src, width):
                nonlocal n
                if n >= RING:
                    sp.wait_ge(sem("ring_free"), n - RING + 1)
                s = n % RING
                sp.dma_start(ring[:, s * SLOT:s * SLOT + width], src).then_inc(sem(f"ring_full{s}"), 16)
                n += 1

            sp.dma_start(x_nat, x0).then_inc(sem("x_loaded"), 16)
            for i in range(DEPTH):
                at = 0
                for width in LOADS_FIRST[i]:
                    load((wfirst0, wfirst1)[i][:, at:at + width], width)
                    at += width
                with sp.Fori(0, NE // EPB) as j:
                    for s in range(per_body):
                        sp.wait_ge(sem("ring_free"), j * per_body + (n + s - RING + 1))
                        r = (n + s) % RING
                        sp.dma_start(ring[:, r * SLOT:(r + 1) * SLOT],
                                     wmoe[i, j, s, :, :]).then_inc(sem(f"ring_full{r}"), 16)
                n += NE * PER_EXPERT
            for l in range(DEPTH):
                at = 0
                for width in LOADS_SECOND:
                    load(wsecond[l, :, at:at + width], width)
                    at += width
            sp.wait_ge(sem("x_ready"), 2 * DEPTH + DEPTH)
            sp.dma_start(out, x_nat).then_inc(sem("out_stored"), 16)
            sp.wait_ge(sem("out_stored"), 16)

        @block.gpsimd
        def _(pool):
            pool.dma_start(cst, consts).then_inc(sem("cst_loaded"), 16)
            pool.dma_start(xT, x0T).then_inc(sem("xT_loaded"), 16)
            pool.dma_start(memT, memT0).then_inc(sem("memT_loaded"), 16)
            pool.dma_start(col, colp).then_inc(sem("par_loaded"), 16)
            pool.dma_start(sgw, sguT).then_inc(sem("par_loaded"), 16)
            pool.dma_start(rowa_sb, rowa[0, :].partition_broadcast(P)).then_inc(sem("par_loaded"), 16)
            pool.dma_start(rwt, rw).then_inc(sem("par_loaded"), 16)
            for n in range(2 * DEPTH):
                if n:
                    pool.wait_ge(sem("x_ready"), n)
                pool.dma_start(rows[:, 0:2 * D], lnrows[n, :].partition_broadcast(P)).then_inc(sem("rows_loaded"), 16)
            for l in range(DEPTH):
                pool.wait_ge(sem("x_ready"), 2 * DEPTH + l)
                pool.dma_start(rows, rows2[l, :].partition_broadcast(P)).then_inc(sem("rows_loaded"), 16)
                pool.dma_start(lora_sb, lora[l, :, :]).then_inc(sem("lora_loaded"), 16)
                pool.dma_start(wff_sb, wff[l, :, :, :]).then_inc(sem("lora_loaded"), 16)

        @block.tensor
        def _(pe_eng):
            pe = TensorCounts()

            def mark(ins, full):
                if full is not None:
                    ins.then_inc(bank_full[full], 1)
                elif pe.pending:
                    pe.pending -= 1
                    ins.then_inc(sem("ring_free"), 1)

            def mm(o, lhsT, rhs, start=True, stop=True, full=None, loose=False):
                mark(nc.tensor.matmul(o, lhsT, rhs, start=start, stop=stop, skip_group_check=loose), full)

            def tr(o, i, full=None):
                mark(nc.tensor.transpose(o, i, ident), full)

            def slot(width=SLOT):
                pe.close()
                n = pe.slots
                pe.slots, pe.open = n + 1, True
                pe_eng.wait_ge(sem(f"ring_full{n % RING}"), 16 * (n // RING + 1))
                return ring[:, (n % RING) * SLOT:(n % RING) * SLOT + width]

            def transpose_tokens(src):
                for g, b in enumerate((0, 5, 1, 6)):
                    tt, half = g // 2, g % 2
                    pe_eng.wait_ge(bank_free[b], pe.reuse(b))
                    bank = banks[b]
                    for k in range(4):
                        tr(bank[:, k * P:(k + 1) * P], src[:, tt, (4 * half + k) * P:(4 * half + k + 1) * P],
                           full=b if k == 3 else None)
                pe_eng.wait_ge(bank_free[0], pe.used(0))
                pe_eng.wait_ge(bank_free[5], pe.used(5))
                pe_eng.wait_ge(bank_free[1], pe.used(1))
                pe_eng.wait_ge(bank_free[6], pe.used(6))

            def proj_T(w, rhsT, bs, tiles=4):
                for m in range(tiles):
                    b = bs[m // 2]
                    if m % 2 == 0:
                        pe_eng.wait_ge(bank_free[b], pe.reuse(b))
                        bank = banks[b]
                    for k in range(KD):
                        end = k == KD - 1 and (m % 2 == 1 or m == tiles - 1)
                        mm(bank[:, (m % 2) * T:(m % 2 + 1) * T], w[:, k, m * P:(m + 1) * P], rhsT[:, k, :],
                           start=k == 0, stop=k == KD - 1, full=b if end else None)

            def proj(w, lT, bs, n=512, kt=KD, at=0):
                for tt in range(TT):
                    pe_eng.wait_ge(bank_free[bs[tt]], pe.reuse(bs[tt]))
                    bank = banks[bs[tt]]
                    for k in range(kt):
                        mm(bank[:, 0:n], lT[:, k, tt * P:(tt + 1) * P], w[:, k, at:at + n], start=k == 0, stop=k == kt - 1,
                           full=bs[tt] if k == kt - 1 else None)

            def wslot():
                return v3(slot(), KD)

            pe_eng.wait_ge(sem("cst_loaded"), 16)
            pe_eng.wait_ge(sem("memT_loaded"), 16)
            pe_eng.wait_ge(sem("xT_loaded"), 16)
            for i in range(DEPTH):
                if i:
                    pe_eng.wait_ge(sem("x_ready"), pe.next("x_ready"))
                    transpose_tokens(x_nat)
                proj_T(wslot(), memT, (0, 5))
                proj(wslot(), memT, (1, 6))
                if i == 0:
                    proj_T(wslot(), xT, (5, 6))
                    proj(wslot(), xT, (7, 5))
                    proj_T(wslot(), xT, (2, 3))
                    pe_eng.wait_ge(sem("sgu_v_ready"), pe.next("sgu_v_ready"))
                    pe_eng.wait_ge(sem("sgu_w_ready"), pe.next("sgu_w_ready"))
                    for c in range(TT):
                        pe_eng.wait_ge(bank_free[c], pe.reuse(c))
                        bank = banks[c]
                        for h in range(4):
                            mm(bank[:, h * P:(h + 1) * P], vv[:, c, h * P:(h + 1) * P], sgw[:, h, :],
                               full=c if h == 3 else None)
                else:
                    proj_T(wslot(), xT, (5, 6))
                    proj_T(wslot(), xT, (7, 5))
                    proj_T(wslot(), xT, (0, 1))
                    proj_T(wslot(), xT, (2, 3))
                pe.close()
                pe_eng.wait_ge(bank_free[0], pe.used(0))
                pe_eng.wait_ge(bank_free[1], pe.used(1))
                pe_eng.wait_ge(bank_free[2], pe.used(2))
                pe_eng.wait_ge(bank_free[3], pe.used(3))
                pe_eng.wait_ge(bank_free[5], pe.used(5))
                pe_eng.wait_ge(bank_free[6], pe.used(6))
                for h in range(NHX):
                    pe_eng.wait_ge(bank_free[h], pe.reuse(h))
                    bank = banks[h]
                    for tt in range(TT):
                        mm(bank[:, tt * T:(tt + 1) * T], qT[:, h, tt * P:(tt + 1) * P], kT[:, h, :],
                           full=h if tt else None)
                for h in range(NHX):
                    pe_eng.wait_ge(sem("p_ready"), pe.next("p_ready"))
                    b = 5 + h % 3
                    pe_eng.wait_ge(bank_free[b], pe.reuse(b))
                    bank = banks[b]
                    for m in range(TT):
                        for tt in range(TT):
                            tr(bank[:, m * T + tt * P:m * T + (tt + 1) * P], xsc[:, h, tt, m * P:(m + 1) * P],
                               full=b if m and tt else None)
                    pe_eng.wait_ge(bank_free[b], pe.used(b))
                    pe_eng.wait_ge(bank_free[4], pe.reuse(4))
                    bank = banks[4]
                    for m in range(TT):
                        mm(bank[:, 0:T], vmem[:, m, h * P:(h + 1) * P], xPT[:, h, m, :], start=m == 0, stop=m == 1,
                           full=4 if m else None)
                pe_eng.wait_ge(bank_free[0], pe.used(0))
                pe_eng.wait_ge(bank_free[1], pe.used(1))
                pe_eng.wait_ge(bank_free[2], pe.used(2))
                pe_eng.wait_ge(bank_free[3], pe.used(3))
                pe_eng.wait_ge(bank_free[4], pe.used(4))
                pe_eng.wait_ge(sem("tok_ready"), pe.next("tok_ready"))
                for n in range(2):
                    proj(wslot(), catT, (n, 2 + n))
                pe.close()
                pe_eng.wait_ge(sem("x_ready"), pe.next("x_ready"))
                transpose_tokens(x_nat)
                if i == 0:
                    pe_eng.wait_ge(sem("par_loaded"), 64)
                pe_eng.wait_ge(bank_free[5], pe.reuse(5))
                bank = banks[5]
                for tt in range(TT):
                    for k in range(KD):
                        mm(bank[:, tt * NE:(tt + 1) * NE], xT[:, k, tt * P:(tt + 1) * P], rwt[:, k, :],
                           start=k == 0, stop=k == KD - 1, full=5 if tt and k == KD - 1 else None)
                for b in range(8):
                    pe_eng.wait_ge(bank_free[b], pe.used(b))
                for b in range(4):
                    pe_eng.wait_ge(bank_free[b], pe.reuse(b))
                    mm(banks[b][:, :], mat(C_ALPHA), x_nat[:, b // 2, (b % 2) * 512:(b % 2 + 1) * 512], stop=False, loose=True)
                base = pe.slots

                with pe_eng.Fori(0, NE // EPB) as j:
                    def expert_slot(s, kt):
                        n = base + s
                        pe_eng.wait_ge(sem(f"ring_full{n % RING}"), j * (16 * per_body // RING) + 16 * (n // RING + 1))
                        return v3(ring[:, (n % RING) * SLOT:(n % RING + 1) * SLOT], kt)

                    for e in range(EPB):
                        pair = j * (EPB * TT) + (PAIRS * i + 1 + TT * e)

                        def gate(tt):
                            pe_eng.wait_ge(sem("silu_done"), pair + tt)
                            for k in range(KD):
                                ins = nc.tensor.matmul(banks[5][:, :], xT[:, k, tt * P:(tt + 1) * P], wg[:, k, :],
                                                       start=k == 0, stop=k == KD - 1)
                            ins.then_inc(sem("gate_full"), 1)

                        def up(tt):
                            pe_eng.wait_ge(sem("h_ready"), pair + tt)
                            for k in range(KD):
                                ins = nc.tensor.matmul(banks[4][:, :], xT[:, k, tt * P:(tt + 1) * P], wu[:, k, :],
                                                       start=k == 0, stop=k == KD - 1)
                            ins.then_inc(sem("up_full"), 1)

                        def turn(tt):
                            pe_eng.wait_ge(sem("h_ready"), pair + (tt + 1))
                            for k in range(KM):
                                ins = nc.tensor.transpose(banks[6 + tt][:, k * P:(k + 1) * P], hh[:, tt, k * P:(k + 1) * P], ident)
                                if k == 0 and tt == 0:
                                    ins.then_inc(sem("ring_free"), 1)
                            ins.then_inc(sem("hT_full"), 1)

                        def down(tt, n):
                            if n == 0:
                                pe_eng.wait_ge(sem("hT_ready"), pair + (tt - i))
                            for k in range(KM):
                                ins = nc.tensor.matmul(banks[2 * tt + n][:, :], hT[:, tt, k, :], wd[:, k, n * 512:(n + 1) * 512],
                                                       start=False, stop=True, skip_group_check=True)
                                if tt == 0 and n == 0 and k == 0:
                                    ins.then_inc(sem("ring_free"), 1)
                            if tt == 1 and n == 1:
                                ins.then_inc(sem("ring_free"), 1)

                        wg = expert_slot(3 * e, KD)
                        gate(0)
                        wu = expert_slot(3 * e + 1, KD)
                        up(0)
                        gate(1)
                        turn(0)
                        up(1)
                        wd = expert_slot(3 * e + 2, KM)
                        down(0, 0)
                        turn(1)
                        down(0, 1)
                        down(1, 0)
                        down(1, 1)
                pe.slots += NE * PER_EXPERT

            def turn_qk(kdim):
                pe_eng.wait_ge(sem("qk_ready"), pe.next("qk_ready"))
                for src, bs in ((qn, (0, 1, 5, 6)), (kn, (2, 3, 7, 5))):
                    for g in range(4):
                        tt, hg = g // 2, g % 2
                        pe_eng.wait_ge(bank_free[bs[g]], pe.reuse(bs[g]))
                        bank = banks[bs[g]]
                        for h in range(4):
                            tr(bank[0:kdim, h * P:(h + 1) * P], src[:, tt, hg * 4 + h, 0:kdim], full=bs[g] if h == 3 else None)
                pe_eng.wait_ge(bank_free[0], pe.used(0))
                pe_eng.wait_ge(bank_free[1], pe.used(1))
                pe_eng.wait_ge(bank_free[2], pe.used(2))
                pe_eng.wait_ge(bank_free[3], pe.used(3))
                pe_eng.wait_ge(bank_free[5], pe.used(5))
                pe_eng.wait_ge(bank_free[6], pe.used(6))
                pe_eng.wait_ge(bank_free[7], pe.used(7))

            def scores(kdim):
                for h in range(NH):
                    b = h % NDB
                    pe_eng.wait_ge(bank_free[b], pe.reuse(b))
                    bank = banks[b]
                    mm(bank[:, 0:P], qTt[0:kdim, h, 0:P], kTt[0:kdim, h, 0:P])
                    mm(bank[:, P:3 * P], qTt[0:kdim, h, P:T], kTt[0:kdim, h, :], full=b)

            def apply(vn):
                for h in range(NH):
                    if h % 4 == 0:
                        pe_eng.wait_ge(sem("p_ready"), pe.next("p_ready"))
                    b = 5 + h % 2
                    pe_eng.wait_ge(bank_free[b], pe.reuse(b))
                    bank = banks[b]
                    for t in range(3):
                        tr(bank[:, t * P:(t + 1) * P], Pm[:, h, t * P:(t + 1) * P], full=b if t == 2 else None)
                    pe_eng.wait_ge(bank_free[b], pe.used(b))
                    ob = h // 2
                    if h % 2 == 0:
                        pe_eng.wait_ge(bank_free[ob], pe.reuse(ob))
                    o = banks[ob][HC * (h % 2):HC * (h % 2) + HC, :]
                    mm(o[:, 0:T], vn[:, 0, h, :], PT[:, h % 2, 0:T], stop=False, loose=True)
                    mm(o[:, P:T], vn[:, 1, h, :], PT[:, h % 2, T:T + P], start=False, full=ob if h % 2 else None, loose=True)

            def merge_values():
                w = v3(slot(), KM)
                pe_eng.wait_ge(bank_free[0], pe.used(0))
                pe_eng.wait_ge(bank_free[1], pe.used(1))
                pe_eng.wait_ge(bank_free[2], pe.used(2))
                pe_eng.wait_ge(bank_free[3], pe.used(3))
                for n in range(2):
                    proj(w, oT, (n, 2 + n), kt=KM, at=n * 512)

            def merge_gates():
                for n in range(2):
                    proj(wslot(), xT, (5, 6))

            for l in range(DEPTH):
                pe_eng.wait_ge(sem("h_ready2"), pe.next("h_ready2"))
                transpose_tokens(y_nat)
                pe_eng.wait_ge(sem("lora_loaded"), 32 * (l + 1))
                proj(v3(slot(KD * LAT), KD), xT, (0, 1), n=LAT)
                pe_eng.wait_ge(bank_free[4], pe.reuse(4))
                bank = banks[4]
                for tt in range(TT):
                    for k in range(KD):
                        mm(bank[:, tt * NH:(tt + 1) * NH], xT[:, k, tt * P:(tt + 1) * P], wff_sb[:, k, :],
                           start=k == 0, stop=k == KD - 1, full=4 if tt and k == KD - 1 else None)
                proj_T(wslot(), xT, (5, 6))
                pe_eng.wait_ge(sem("lat_ready"), pe.next("lat_ready"))
                for b, at, n in ((2, 0, 2), (3, 2, 1)):
                    pe_eng.wait_ge(bank_free[b], pe.reuse(b))
                    bank = banks[b]
                    for k in range(n):
                        for tt in range(TT):
                            tr(bank[:, k * T + tt * P:k * T + (tt + 1) * P], cnat[:, tt, (at + k) * P:(at + k + 1) * P],
                               full=b if tt and k == n - 1 else None)
                pe_eng.wait_ge(bank_free[2], pe.used(2))
                pe_eng.wait_ge(bank_free[3], pe.used(3))
                w = v3(slot(1536), 2)
                for n in range(2):
                    for tt in range(TT):
                        b = 2 * n + tt
                        pe_eng.wait_ge(bank_free[b], pe.reuse(b))
                        bank = banks[b]
                        for k in range(2):
                            mm(bank[:, 0:4 * QK], cT[:, k, tt * P:(tt + 1) * P], w[:, k, n * 4 * QK:(n + 1) * 4 * QK],
                               start=k == 0, stop=k == 1, full=b if k else None)
                w = slot(1024)
                for n in range(2):
                    for tt in range(TT):
                        b = 5 + (2 * n + tt) % 3
                        pe_eng.wait_ge(bank_free[b], pe.reuse(b))
                        bank = banks[b]
                        mm(bank[:, 0:256], cT[:, 2, tt * P:(tt + 1) * P], w[:, n * 512:n * 512 + 256])
                        mm(bank[:, 256:512], cT[:, 2, tt * P:(tt + 1) * P], w[:, n * 512 + 256:(n + 1) * 512], full=b)
                proj_T(wslot(), xT, (5, 6))
                proj_T(wslot(), xT, (5, 6))
                turn_qk(QK)
                scores(QK)
                pe_eng.wait_ge(sem("logf_ready"), pe.next("logf_ready"))
                lf = ffn[:, 0:TT * NH]
                pe_eng.wait_ge(bank_free[4], pe.reuse(4))
                bank = banks[4]
                mm(bank[:, 0:NH], mat(C_TRI), lf[:, 0:NH])
                mm(bank[:, NH:2 * NH], mat(C_ONES), lf[:, 0:NH], stop=False)
                mm(bank[:, NH:2 * NH], mat(C_TRI), lf[:, NH:2 * NH], start=False, full=4)
                proj(wslot(), xT, (0, 1))
                proj(wslot(), xT, (2, 3))
                proj(wslot(), xT, (5, 6))
                proj_T(wslot(), xT, (5, 6))
                apply(vn2[0])
                proj_T(wslot(), xT, (5, 6))
                proj_T(v3(slot(KD * P), KD), xT, (7,), tiles=1)
                turn_qk(FOXK)
                scores(FOXK)
                merge_values()
                merge_gates()
                apply(vn2[1])
                proj_T(wslot(), xT, (5, 6))
                merge_values()
                merge_gates()

                pe_eng.wait_ge(sem("shift_ready"), pe.next("shift_ready"))
                if l:
                    pe_eng.wait_ge(bank_free[4], pe.reuse(4))
                    bank = banks[4]
                    for k in range(4):
                        mm(bank[0:32, 0:T], vdown[:, k, :], vlT[:, k, :], start=k == 0, stop=k == 3, full=4 if k == 3 else None)
                    pe_eng.wait_ge(bank_free[4], pe.used(4))
                    for g in range(2):
                        pe_eng.wait_ge(bank_free[g], pe.reuse(g))
                        bank = banks[g]
                        for j in range(2):
                            mm(bank[:, j * T:(j + 1) * T], vup[0:32, (2 * g + j) * P:(2 * g + j + 1) * P], v_mid,
                               full=g if j else None)
                for tt in range(TT):
                    tok = slice(tt * P, (tt + 1) * P)
                    pe_eng.wait_ge(sem("tw_ready"), pe.next("tw_ready"))
                    pe_eng.wait_ge(bank_free[0], pe.reuse(0))
                    bank = banks[0]
                    for j in range(4):
                        mm(bank[:, j * P:(j + 1) * P], wup[0:64, j * P:(j + 1) * P], tw[0:64, :], full=0 if j == 3 else None)
                    pe_eng.wait_ge(bank_free[1], pe.reuse(1))
                    bank = banks[1]
                    for j in range(4):
                        mm(bank[:, j * P:(j + 1) * P], wup[64:128, j * P:(j + 1) * P], sh[64:128, 12, tok], full=1 if j == 3 else None)
                    pe_eng.wait_ge(sem("ksq_ready"), pe.next("ksq_ready"))
                    pe_eng.wait_ge(bank_free[2], pe.reuse(2))
                    bank = banks[2]
                    mm(bank[:, :], mat(C_BLOCK), flat2(t1), full=2)
                    pe_eng.wait_ge(sem("rows_ready"), pe.next("rows_ready"))
                    for par in range(2):
                        hs = slice(64 * par, 64 * par + 64)
                        for b, left, right in ((0, aa, pex), (1, pinv, pex), (2, pinv, pp), (3, aa, pp)):
                            pe_eng.wait_ge(bank_free[b], pe.reuse(b))
                            bank = banks[b]
                            for j in range(4):
                                mm(bank[:, j * P:(j + 1) * P], left[hs, j, :], right[hs, j, :], full=b if j == 3 else None)
                    pe_eng.wait_ge(bank_free[4], pe.reuse(4))
                    bank = banks[4]
                    for j in range(4):
                        mm(bank[:, 0:NH], rk[:, j, :], cst[:, C_SEL + j * NH:C_SEL + (j + 1) * NH], start=j == 0, stop=j == 3)
                    for par in range(2):
                        mm(bank[0:64, 64 + 8 * par:72 + 8 * par], mat(C_ID)[:, 64 * par:64 * par + 64], pcs, full=4 if par else None)
                    for b, src in ((5, vlT[:, :, tok]), (6, pex), (7, pp), (5, cum), (3, lw)):
                        pe_eng.wait_ge(bank_free[b], pe.reuse(b))
                        bank = banks[b]
                        for j in range(4):
                            tr(bank[:, j * P:(j + 1) * P], src[:, j, :], full=b if j == 3 else None)
                    for par in range(2):
                        pe_eng.wait_ge(sem("level_ready"), pe.next("level_ready"))
                        pe_eng.wait_ge(bank_free[par], pe.reuse(par))
                        bank = banks[par]
                        for j in range(4):
                            tr(bank[:, j * P:(j + 1) * P], TTm[:, par, j, :], full=par if j == 3 else None)
                    for lev in range(1, LEVELS):
                        for par in range(2):
                            pe_eng.wait_ge(sem("level_ready"), pe.next("level_ready"))
                            b = 5 + par
                            pe_eng.wait_ge(bank_free[b], pe.reuse(b))
                            bank = banks[b]
                            for j in range(4):
                                mm(bank[:, j * P:(j + 1) * P], Nl[:, par, j, :], Tm[:, par, j, :], full=b if j == 3 else None)
                        for par in range(2):
                            pe_eng.wait_ge(bank_free[5 + par], pe.used(5 + par))
                            if lev < LEVELS - 1:
                                pe_eng.wait_ge(bank_free[2 * par], pe.reuse(2 * par))
                                bank = banks[2 * par]
                                for j in range(4):
                                    mm(bank[:, j * P:(j + 1) * P], TTm[:, par, j, :], Xm[:, par, j, :], full=2 * par if j == 3 else None)
                            pe_eng.wait_ge(bank_free[2 * par + 1], pe.reuse(2 * par + 1))
                            bank = banks[2 * par + 1]
                            for j in range(4):
                                mm(bank[:, j * P:(j + 1) * P], Xm[:, par, j, :], TTm[:, par, j, :], full=2 * par + 1 if j == 3 else None)
                    pe_eng.wait_ge(bank_free[1], pe.used(1))
                    pe_eng.wait_ge(bank_free[3], pe.used(3))
                    pe_eng.wait_ge(bank_free[5], pe.used(5))
                    pe_eng.wait_ge(bank_free[6], pe.used(6))
                    pe_eng.wait_ge(bank_free[7], pe.used(7))
                    pe_eng.wait_ge(bank_free[2], pe.reuse(2))
                    bank = banks[2]
                    for h in range(NH):
                        mm(hc(bank, h), TTm[:, h % 2, h // 2, :], hc(Kn, h), full=2 if h == NH - 1 else None)
                    pe_eng.wait_ge(bank_free[3], pe.reuse(3))
                    bank = banks[3]
                    for h in range(NH):
                        mm(hc(bank, h), MTm[:, h % 2, h // 2, :], hc(Vn, h), full=3 if h == NH - 1 else None)
                    pe_eng.wait_ge(bank_free[3], pe.used(3))
                    pe_eng.wait_ge(bank_free[4], pe.reuse(4))
                    bank = banks[4]
                    for h in range(NH):
                        mm(hc(bank, h), TTm[:, h % 2, h // 2, :], hc(mv, h), full=4 if h == NH - 1 else None)
                    pe_eng.wait_ge(bank_free[2], pe.used(2))
                    pe_eng.wait_ge(bank_free[4], pe.used(4))
                    chunks = (0, 1) if tt == 0 else (0,)
                    for c in chunks:
                        rowsc = slice(64 * c, 64 * c + 64)
                        if 2 * tt + c:
                            pe_eng.wait_ge(bank_free[c], pe.reuse(c))
                            bank = banks[c]
                            for h in range(NH):
                                mm(hc(bank[0:64, :], h), hc(Wn[rowsc, :], h), hc(Bn[rowsc, :], h), full=c if h == NH - 1 else None)
                        pe_eng.wait_ge(bank_free[2 + c], pe.reuse(2 + c))
                        bank = banks[2 + c]
                        for h in range(NH):
                            mm(hc(bank[0:64, :], h), hc(Kp[rowsc, :], h), hc(Vn[rowsc, :], h), stop=False)
                            mm(hc(bank[0:64, :], h), hc(Bn[rowsc, :], h), hc(uv[rowsc, :], h), start=False, full=2 + c if h == NH - 1 else None)
                    for par in range(2):
                        b = 5 + par
                        pe_eng.wait_ge(bank_free[b], pe.reuse(b))
                        bank = banks[b]
                        for j in range(4):
                            h = 2 * j + par
                            mm(bank[0:64, j * P:(j + 1) * P], hc(Rn, h), ident, stop=False)
                            mm(bank[0:64, j * P:(j + 1) * P], hc(Wn, h), AbT[:, par, j, :], start=False, full=b if j == 3 else None)
                    for c in chunks:
                        g = 2 * tt + c
                        if g == 0:
                            continue
                        pe_eng.wait_ge(bank_free[c], pe.used(c))
                        pe_eng.wait_ge(bank_free[2], pe.used(2))
                        pe_eng.wait_ge(bank_free[3], pe.used(3))
                        pe_eng.wait_ge(bank_free[4], pe.used(4))
                        pe_eng.wait_ge(bank_free[4], pe.reuse(4))
                        bank = banks[4]
                        for h in range(NH):
                            mm(hc(bank[0:64, :], h), GT[0:64, c, h, :], hc(states[g - 1][0:64, :], h), full=4 if h == NH - 1 else None)
                    pe_eng.wait_ge(bank_free[5], pe.used(5))
                    pe_eng.wait_ge(bank_free[6], pe.used(6))
                    pe_eng.wait_ge(bank_free[4], pe.reuse(4))
                    bank = banks[4]
                    for h in range(NH):
                        par, j = h % 2, h // 2
                        o = hc(bank, h)
                        mm(o, AkT[:, par, j, :], hc(Vn, h), stop=False, loose=True)
                        mm(o, AbT[:, par, j, :], hc(uv, h), start=False, stop=False, loose=True)
                        for c in range(2):
                            g = 2 * tt + c
                            if g:
                                mm(o[64 * c:64 * c + 64, :], QT[0:64, par, j, c * CH:(c + 1) * CH], hc(states[g - 1][0:64, :], h),
                                   start=False, full=4 if h == NH - 1 and c else None, loose=True)
                    pe_eng.wait_ge(sem("y_ready"), pe.next("y_ready"))
                    pe_eng.wait_ge(bank_free[0], pe.reuse(0))
                    bank = banks[0]
                    for j in range(4):
                        tr(bank[:, j * P:(j + 1) * P], yv[:, j * P:(j + 1) * P], full=0 if j == 3 else None)
                merge_values()
                merge_gates()
                pe_eng.wait_ge(sem("merged_ready"), pe.next("merged_ready"))
                transpose_tokens(merged)
                for n in range(2):
                    proj(wslot(), xT, (n, 2 + n))
                pe.close()

        @block.scalar
        def _(act_eng):
            act = Counts()
            act.shifts = 0

            def copy_out(o, b, bank_ap, func=ACT.Copy):
                act_eng.wait_ge(bank_full[b], act.next(("full", b)))
                nc.scalar.activation(o, bank_ap, func).then_inc(bank_free[b], act.sends(bank_free[b]))

            def roots(n):
                act_eng.wait_ge(sem("var_ready"), act.next("var_ready"))
                nc.scalar.activation(S_VAR[:, 0:n], S_VAR[:, 0:n], ACT.Sqrt).then_inc(sem("std_ready"), act.sends(sem("std_ready")))

            def turned_x():
                for g, b in ((1, 5), (3, 6)):
                    copy_out(xT[:, 4:8, (g // 2) * P:(g // 2 + 1) * P], b, v3(banks[b][:, :], 4))

            def two_tiles(dst, b, m, func=ACT.Copy):
                copy_out(dst[:, 2 * m:2 * m + 2, :], b, v3(banks[b][:, :], 2), func)

            for i in range(DEPTH):
                if i:
                    turned_x()
                two_tiles(kT, 5, 1)
                copy_out(vmem[:, 1, :], 6, banks[6][:, :])
                if i == 0:
                    two_tiles(uT, 5, 0, ACT.Gelu)
                    two_tiles(uT, 6, 1, ACT.Gelu)
                    copy_out(vv[:, 0, :], 7, banks[7][:, :], ACT.Gelu)
                    act_eng.wait_ge(bank_full[5], act.next(("full", 5)))
                    nc.scalar.activation(vv[:, 1, :], banks[5][:, :], ACT.Gelu).then_inc(bank_free[5], act.sends(bank_free[5]))
                    act_eng.wait_ge(act.last, act.value)
                    nc.scalar.activation(S_MARK[:, 0:1], vv[:, 1, 0:1], ACT.Copy).then_inc(sem("gelu_done"), act.sends(sem("gelu_done")))
                    roots(2)
                else:
                    two_tiles(bgT, 5, 0)
                    two_tiles(bgT, 6, 1)
                    two_tiles(cgT, 7, 0)
                    two_tiles(cgT, 5, 1)
                    act_eng.wait_ge(act.last, act.value)
                    nc.scalar.activation(S_MARK[:, 0:1], cgT[:, 3, 0:1], ACT.Copy).then_inc(sem("gelu_done"), act.sends(sem("gelu_done")))
                for h in range(NHX):
                    act_eng.wait_ge(sem("max_ready"), act.next("max_ready"))
                    for tt in range(TT):
                        ins = nc.scalar.activation(xsc[:, h, tt, :], xsc[:, h, tt, :], ACT.Exp, bias=S_NM[:, h * TT + tt:h * TT + tt + 1],
                                                   scale=XSCALE, accum_out=S_SUM[:, h * TT + tt:h * TT + tt + 1])
                    ins.then_inc(sem("exp_done"), act.sends(sem("exp_done")))
                for h in range(NHX):
                    b = 5 + h % 3
                    copy_out(xPT[:, h, :, :], b, v3(banks[b][:, :], 2))
                roots(2)
                turned_x()
                act_eng.wait_ge(bank_full[5], act.next(("full", 5)))
                nc.scalar.activation(S_SC, banks[5][:, 0:TT * NE], ACT.Sigmoid).then_inc(bank_free[5], act.sends(bank_free[5]))
                act_eng.wait_ge(act.last, act.value)
                nc.scalar.activation(S_MARK[:, 1:2], S_SC[:, 0:1], ACT.Copy).then_inc(sem("scores_ready"), act.sends(sem("scores_ready")))
                nc.scalar.activation(S_MARK[:, 2:3], S_SC[:, 0:1], ACT.Silu).then_inc(sem("silu_done"), 1)
                with act_eng.Fori(0, NE // EPB) as j:
                    for e in range(EPB):
                        pair = j * (EPB * TT) + (NE * TT * i + TT * e)
                        for tt in range(TT):
                            act_eng.wait_ge(sem("gate_full"), pair + (tt + 1))
                            nc.scalar.activation(sg[:, tt, :], banks[5][:, :], ACT.Silu).then_inc(sem("silu_done"), 1)
                        for tt in range(TT):
                            act_eng.wait_ge(sem("hT_full"), pair + (tt + 1))
                            nc.scalar.activation(hT[:, tt, :, :], v3(banks[6 + tt][:, :], KM), ACT.Copy).then_inc(sem("hT_ready"), 1)
                roots(2)

            def shifted_in(n):
                for m in range(2):
                    act_shift(5 + m, 2)

            def act_shift(b, tiles):
                if act.shifts:
                    act_eng.wait_ge(sem("shift_done"), act.next("shift_done"))
                act.shifts += 1
                act_eng.wait_ge(bank_full[b], act.next(("full", b)))
                nc.scalar.activation(pcol[:, 0:tiles, 1:T + 1], v3(banks[b][:, 0:tiles * T], tiles), ACT.Copy).then_inc(bank_free[b], act.sends(bank_free[b]))
                act_eng.wait_ge(act.last, act.value)
                nc.scalar.activation(S_MARK[:, 0:1], pcol[:, tiles - 1, T:T + 1], ACT.Copy).then_inc(sem("shift_in"), act.sends(sem("shift_in")))

            def silu_gate(g):
                for m in range(2):
                    two_tiles(gates[:, g, :, :], 5 + m, m, ACT.Silu)

            def turned_qk(kdim):
                for dst, g, b in ((qTt, 2, 5), (qTt, 3, 6), (kTt, 2, 7), (kTt, 3, 5)):
                    hg = g % 2
                    copy_out(dst[0:kdim, 4 * hg:4 * hg + 4, P:T], b, v3(banks[b][0:kdim, :], 4))

            def softmax():
                for half in range(2):
                    act_eng.wait_ge(sem("max_ready"), act.next("max_ready"))
                    for h in range(4):
                        for tt in range(TT):
                            at = half * 8 + tt * 4 + h
                            span = Pm[:, half * 4 + h, 0:P] if tt == 0 else Pm[:, half * 4 + h, P:3 * P]
                            ins = nc.scalar.activation(span, span, ACT.Exp, bias=S_NM[:, at:at + 1], accum_out=S_SUM[:, at:at + 1])
                    ins.then_inc(sem("exp_done"), act.sends(sem("exp_done")))

            def turned_p():
                for h in range(NH):
                    b = 5 + h % 2
                    copy_out(PT[:, h % 2, :], b, banks[b][:, 0:3 * P])

            def merge_sigmoid():
                for n in range(2):
                    for tt in range(TT):
                        copy_out(sgm[:, tt, n * 512:(n + 1) * 512], 5 + tt, banks[5 + tt][:, :], ACT.Sigmoid)
                act_eng.wait_ge(act.last, act.value)
                nc.scalar.activation(S_MARK[:, 0:1], sgm[:, 1, D - 1:D], ACT.Copy).then_inc(sem("sgm_ready"), act.sends(sem("sgm_ready")))

            for l in range(DEPTH):
                roots(2)
                turned_x()
                silu_gate(0)
                roots(6)
                act_eng.wait_ge(sem("gates_neg"), act.next("gates_neg"))
                lfe = ffn[:, TT * NH:2 * TT * NH]
                nc.scalar.activation(lfe, lfe, ACT.Exp).then_inc(act_step, act.sends(act_step))
                act_eng.wait_ge(act.last, act.value)
                nc.scalar.activation(lfe, lfe, ACT.Ln, bias=1.0).then_inc(sem("gates_ln"), act.sends(sem("gates_ln")))
                for n in range(2):
                    for tt in range(TT):
                        b = 5 + (2 * n + tt) % 3
                        act_eng.wait_ge(bank_full[b], act.next(("full", b)))
                        kv = v3(banks[b][:, :], 4)
                        nc.scalar.activation(kn[:, tt, 4 * n:4 * n + 4, 0:NOPE], kv[:, :, 0:NOPE], ACT.Copy).then_inc(act_step, act.sends(act_step))
                        nc.scalar.activation(vn2[0][:, tt, 4 * n:4 * n + 4, :], kv[:, :, NOPE:P], ACT.Copy).then_inc(bank_free[b], act.sends(bank_free[b]))
                act_eng.wait_ge(act.last, act.value)
                nc.scalar.activation(S_MARK[:, 0:1], vn2[0][:, 1, 7, 0:1], ACT.Copy).then_inc(sem("kv_ready"), act.sends(sem("kv_ready")))
                roots(32)
                shifted_in(0)
                shifted_in(1)
                turned_qk(QK)
                softmax()
                for tt in range(TT):
                    copy_out(vn2[1][:, tt, :, :], 5 + tt, v3(banks[5 + tt][:, :], NH))
                silu_gate(1)
                roots(32)
                turned_p()
                shifted_in(2)
                act_shift(7, 1)
                turned_qk(FOXK)
                softmax()
                merge_sigmoid()
                turned_p()
                silu_gate(0)
                merge_sigmoid()
                if l:
                    act_eng.wait_ge(sem("nu_in"), act.next("nu_in"))
                    nc.scalar.activation(nuT, nuT, ACT.Sigmoid).then_inc(sem("nu_ready"), act.sends(sem("nu_ready")))
                for tt in range(TT):
                    tok = slice(tt * P, (tt + 1) * P)
                    act_eng.wait_ge(sem("shift_all"), act.next("shift_all"))
                    nc.scalar.activation(tw[0:64, :], sh[0:64, 12, tok], ACT.Tanh).then_inc(sem("tw_ready"), act.sends(sem("tw_ready")))
                    act_eng.wait_ge(sem("wa_in"), act.next("wa_in"))
                    nc.scalar.activation(flat2(lw), flat2(lw), ACT.Sigmoid).then_inc(act_step, act.sends(act_step))
                    nc.scalar.activation(flat2(aa), flat2(aa), ACT.Sigmoid).then_inc(sem("wa_ready"), act.sends(sem("wa_ready")))
                    act_eng.wait_ge(sem("ksum_ready"), act.next("ksum_ready"))
                    nc.scalar.activation(flat2(t1), flat2(t1), ACT.Sqrt).then_inc(sem("knorm_ready"), act.sends(sem("knorm_ready")))
                    act_eng.wait_ge(sem("cum_ready"), act.next("cum_ready"))
                    nc.scalar.activation(flat2(pp), flat2(cum), ACT.Exp).then_inc(act_step, act.sends(act_step))
                    nc.scalar.activation(flat2(pinv), flat2(cum), ACT.Exp, scale=-1.0).then_inc(act_step, act.sends(act_step))
                    nc.scalar.activation(flat2(pex), flat2(pex), ACT.Exp).then_inc(sem("decay_ready"), act.sends(sem("decay_ready")))
                    for b, dst in ((5, Vn), (6, Kn), (7, Rn), (5, Bn)):
                        copy_out(dst, b, banks[b][:, :])
                    for lev in range(1, LEVELS):
                        for par in range(2):
                            copy_out(Xm[:, par, :, :], 5 + par, v3(banks[5 + par][:, :], 4))
                    for par in range(2):
                        copy_out(QT[0:64, par, :, :], 5 + par, v3(banks[5 + par][0:64, :], 4))
                    roots(8)
                merge_sigmoid()
                turned_x()

        @block.vector
        def _(dve_eng):
            dve = Counts()
            v = nc.vector
            for b in range(8):
                v.memset(banks[b][:, 0:1], 0.0).then_inc(bank_free[b], 1)

            def copy_out(o, b, bank_ap):
                dve_eng.wait_ge(bank_full[b], dve.next(("full", b)))
                v.tensor_copy(o, bank_ap).then_inc(bank_free[b], dve.sends(bank_free[b]))

            def turned_x():
                for g, b in ((0, 0), (2, 1)):
                    copy_out(xT[:, 0:4, (g // 2) * P:(g // 2 + 1) * P], b, v3(banks[b][:, :], 4))

            def roots(n):
                dve_eng.wait_ge(sem("std_ready"), dve.next("std_ready"))
                v.reciprocal(S_RSTD[:, 0:n], S_VAR[:, 0:n]).then_inc(dve_step, dve.sends(dve_step))
                dve_eng.wait_ge(dve.last, dve.value)

            def mean_var(src):
                n = src.shape[2] // 512
                for tt in range(TT):
                    for s in range(n):
                        v.bn_stats(S_BN[:, (tt * n + s) * 6:(tt * n + s + 1) * 6], src[:, tt, s * 512:(s + 1) * 512]).then_inc(dve_step, dve.sends(dve_step))
                dve_eng.wait_ge(dve.last, dve.value)
                for tt in range(TT):
                    v.bn_aggr(S_MV[:, 2 * tt:2 * tt + 2], S_BN[:, tt * n * 6:(tt + 1) * n * 6]).then_inc(dve_step, dve.sends(dve_step))
                dve_eng.wait_ge(dve.last, dve.value)
                v.tensor_scalar(S_VAR[:, 0:TT], S_MV[:, 1:4:2], LN_EPS, None, ADD).then_inc(sem("var_ready"), dve.sends(sem("var_ready")))
                roots(TT)

            def layer_norm(src, dst, g, b, end):
                mean_var(src)
                for tt in range(TT):
                    v.tensor_scalar(dst[:, tt, :], src[:, tt, :], S_MV[:, 2 * tt:2 * tt + 1], S_RSTD[:, tt:tt + 1], SUB, MUL).then_inc(dve_step, dve.sends(dve_step))
                n = dst.shape[2]
                dve_eng.wait_ge(dve.last, dve.value)
                v.tensor_tensor(dst, dst, per_column(g, TT), MUL).then_inc(dve_step, dve.sends(dve_step))
                dve_eng.wait_ge(dve.last, dve.value)
                v.tensor_tensor(dst, dst, per_column(b, TT), ADD).then_inc(sem(end), dve.sends(sem(end)))

            def two_tiles(dst, b, m):
                copy_out(dst[:, 2 * m:2 * m + 2, :], b, v3(banks[b][:, :], 2))

            dve_eng.wait_ge(sem("cst_loaded"), 16)
            dve_eng.wait_ge(sem("par_loaded"), 64)
            v.tensor_tensor(sgw, sgw, mat4(C_SGU), MUL).then_inc(dve_step, dve.sends(dve_step))
            dve_eng.wait_ge(dve.last, dve.value)
            v.tensor_copy(S_BIG[:, 0:1], sgw[:, 0, 0:1]).then_inc(sem("sgu_w_ready"), dve.sends(sem("sgu_w_ready")))
            for i in range(DEPTH):
                if i:
                    turned_x()
                two_tiles(kT, 0, 0)
                copy_out(vmem[:, 0, :], 1, banks[1][:, :])
                if i == 0:
                    for m in range(2):
                        two_tiles(qT, 2 + m, m)
                    dve_eng.wait_ge(sem("gelu_done"), dve.next("gelu_done"))
                    layer_norm(vv, vv, rowa_sb[:, R_SGUG:R_SGUG + MIX], rowa_sb[:, R_SGUB:R_SGUB + MIX], "sgu_v_ready")
                    for c in range(TT):
                        dve_eng.wait_ge(bank_full[c], dve.next(("full", c)))
                        t = tmpT[:, :, c * P:(c + 1) * P]
                        v.tensor_tensor(t, v3(banks[c][:, :], 4), v3(rowa_sb[:, R_SGUBIAS:R_SGUBIAS + 512], 4), ADD).then_inc(bank_free[c], dve.sends(bank_free[c]))
                    dve_eng.wait_ge(dve.last, dve.value)
                    v.tensor_tensor(catT[:, 0:4, :], uT, tmpT, MUL).then_inc(sem("tok_ready"), dve.sends(sem("tok_ready")))
                else:
                    v.memset(hpad[:, :, 0:2], 0.0).then_inc(dve_step, dve.sends(dve_step))
                    dve_eng.wait_ge(dve.last, dve.value)
                    dve_eng.wait_ge(sem("gelu_done"), dve.next("gelu_done"))
                    for m in range(2):
                        dve_eng.wait_ge(bank_full[m], dve.next(("full", m)))
                        v.tensor_tensor(hpad[:, 2 * m:2 * m + 2, 2:], cgT[:, 2 * m:2 * m + 2, :], v3(banks[m][:, :], 2), MUL).then_inc(bank_free[m], dve.sends(bank_free[m]))
                    for m in range(2):
                        two_tiles(qT, 2 + m, m)
                    dve_eng.wait_ge(dve.last, dve.value)
                    for k in range(4):
                        cw = col[:, 3 * k:3 * k + 3]
                        v.tensor_scalar(tmpT[:, k, :], hpad[:, k, 0:T], cw[:, 0:1], None, MUL).then_inc(dve_step, dve.sends(dve_step))
                    for tap in range(1, 3):
                        dve_eng.wait_ge(dve.last, dve.value)
                        for k in range(4):
                            v.scalar_tensor_tensor(tmpT[:, k, :], hpad[:, k, tap:tap + T], col[:, 3 * k + tap:3 * k + tap + 1],
                                                      tmpT[:, k, :], MUL, ADD).then_inc(dve_step, dve.sends(dve_step))
                    dve_eng.wait_ge(dve.last, dve.value)
                    v.tensor_tensor(catT[:, 0:4, :], bgT, tmpT, MUL).then_inc(sem("tok_ready"), dve.sends(sem("tok_ready")))
                for h in range(NHX):
                    copy_out(xsc[:, h, :, :], h, v3(banks[h][:, :], 2))
                    dve_eng.wait_ge(dve.last, dve.value)
                    v.tensor_reduce(S_MX[:, 2 * h:2 * h + 2], xsc[:, h, :, :], AX, MAX).then_inc(dve_step, dve.sends(dve_step))
                    dve_eng.wait_ge(dve.last, dve.value)
                    v.tensor_scalar(S_NM[:, 2 * h:2 * h + 2], S_MX[:, 2 * h:2 * h + 2], -XSCALE, None, MUL).then_inc(sem("max_ready"), dve.sends(sem("max_ready")))
                for h in range(NHX):
                    dve_eng.wait_ge(sem("exp_done"), dve.next("exp_done"))
                    v.reciprocal(S_RS[:, 2 * h:2 * h + 2], S_SUM[:, 2 * h:2 * h + 2]).then_inc(dve_step, dve.sends(dve_step))
                    dve_eng.wait_ge(dve.last, dve.value)
                    v.tensor_tensor(xsc[:, h, :, :], xsc[:, h, :, :], per_channel(S_RS[:, 2 * h:2 * h + 2], T), MUL).then_inc(sem("p_ready"), dve.sends(sem("p_ready")))
                for h in range(NHX):
                    copy_out(catT[:, 4 + h, :], 4, banks[4][:, 0:T])
                if i == 0:
                    dve_eng.wait_ge(sem("x_loaded"), 16)
                for n in range(2):
                    for tt in range(TT):
                        b = n + 2 * tt
                        dve_eng.wait_ge(bank_full[b], dve.next(("full", b)))
                        v.scalar_tensor_tensor(y_nat[:, tt, n * 512:(n + 1) * 512], x_nat[:, tt, n * 512:(n + 1) * 512], ALPHA,
                                                        banks[b][:, :], MUL, ADD).then_inc(bank_free[b], dve.sends(bank_free[b]))
                dve_eng.wait_ge(dve.last, dve.value)
                dve_eng.wait_ge(sem("rows_loaded"), 16 * (2 * i + 1))
                layer_norm(y_nat, x_nat, rows[:, 0:D], rows[:, D:2 * D], "x_ready")
                turned_x()
                dve_eng.wait_ge(sem("scores_ready"), dve.next("scores_ready"))
                sel4 = v3(S_SEL, TT * NG)
                v.tensor_tensor(v3(S_SEL, TT), v3(S_SC, TT), per_column(rowa_sb[:, R_RB:R_RB + NE], TT), ADD).then_inc(dve_step, dve.sends(dve_step))
                dve_eng.wait_ge(dve.last, dve.value)
                pairs = v3(S_BIG[:, 0:48], TT * NG)
                v.tensor_tensor(pairs[:, :, 0:3], sel4[:, :, 1:4], bc(sel4[:, :, 0:1], P, TT * NG, 3), ADD).then_inc(dve_step, dve.sends(dve_step))
                v.tensor_tensor(pairs[:, :, 3:5], sel4[:, :, 2:4], bc(sel4[:, :, 1:2], P, TT * NG, 2), ADD).then_inc(dve_step, dve.sends(dve_step))
                v.tensor_tensor(pairs[:, :, 5:6], sel4[:, :, 3:4], sel4[:, :, 2:3], ADD).then_inc(dve_step, dve.sends(dve_step))
                dve_eng.wait_ge(dve.last, dve.value)
                v.tensor_reduce(S_GSC, pairs, AX, MAX).then_inc(dve_step, dve.sends(dve_step))
                dve_eng.wait_ge(dve.last, dve.value)

                def ranks(vals, a, dst):
                    other = bc(vals.unsqueeze(2), P, a, GS, GS)
                    own = bc(vals.unsqueeze(3), P, a, GS, GS)
                    n = a * GS * GS
                    gt, eq = S_BIG[:, 0:n], S_BIG2[:, 0:n]
                    v.tensor_tensor(v4(gt, a, GS), other, own, ALU.is_gt).then_inc(dve_step, dve.sends(dve_step))
                    v.tensor_tensor(v4(eq, a, GS), other, own, ALU.is_equal).then_inc(dve_step, dve.sends(dve_step))
                    dve_eng.wait_ge(dve.last, dve.value)
                    v.tensor_tensor(v3(eq, a), v3(eq, a), per_column(cst[:, C_TIE:C_TIE + GS * GS], a), MUL).then_inc(dve_step, dve.sends(dve_step))
                    dve_eng.wait_ge(dve.last, dve.value)
                    v.tensor_tensor(gt, gt, eq, ADD).then_inc(dve_step, dve.sends(dve_step))
                    dve_eng.wait_ge(dve.last, dve.value)
                    v.tensor_reduce(dst, v3(gt, a * GS), AX, ADD).then_inc(dve_step, dve.sends(dve_step))
                    dve_eng.wait_ge(dve.last, dve.value)

                ranks(v3(S_GSC, TT), TT, S_GRANK)
                ranks(sel4, TT * NG, S_RANK)
                v.tensor_scalar(S_GRANK, S_GRANK, 0.5, None, ALU.is_lt).then_inc(dve_step, dve.sends(dve_step))
                v.tensor_scalar(S_RANK, S_RANK, 1.5, None, ALU.is_lt).then_inc(dve_step, dve.sends(dve_step))
                dve_eng.wait_ge(dve.last, dve.value)
                v.tensor_tensor(v3(S_RANK, TT * NG), v3(S_RANK, TT * NG), per_channel(S_GRANK, GS), MUL).then_inc(dve_step, dve.sends(dve_step))
                dve_eng.wait_ge(dve.last, dve.value)
                v.tensor_tensor(S_COMB, S_SC, S_RANK, MUL).then_inc(dve_step, dve.sends(dve_step))
                dve_eng.wait_ge(dve.last, dve.value)
                v.tensor_reduce(S_RS[:, 0:TT], v3(S_COMB, TT), AX, ADD).then_inc(dve_step, dve.sends(dve_step))
                dve_eng.wait_ge(dve.last, dve.value)
                v.reciprocal(S_RS[:, 0:TT], S_RS[:, 0:TT]).then_inc(dve_step, dve.sends(dve_step))
                dve_eng.wait_ge(dve.last, dve.value)
                v.tensor_tensor(v3(S_COMB, TT), v3(S_COMB, TT), per_channel(S_RS[:, 0:TT], NE), MUL).then_inc(sem("h_ready"), 1)
                dve_eng.wait_ge(sem("h_ready"), PAIRS * i + 1)
                with dve_eng.Fori(0, NE // EPB) as j:
                    for e in range(EPB):
                        for tt in range(TT):
                            pair = j * (EPB * TT) + (NE * TT * i + TT * e + tt + 1)
                            dve_eng.wait_ge(sem("up_full"), pair)
                            dve_eng.wait_ge(sem("silu_done"), pair + (i + 1))
                            v.scalar_tensor_tensor(hh[:, tt, :], banks[4][:, :], S_COMB[:, bass.ds(j * EPB + (tt * NE + e), 1)], sg[:, tt, :],
                                                   MUL, MUL).then_inc(sem("h_ready"), 1)
                dve_eng.wait_ge(sem("ring_free"), sum(len(LOADS_FIRST[k]) for k in range(i + 1)) + NE * PER_EXPERT * (i + 1))
                for b in range(4):
                    v.tensor_copy(y_nat[:, b // 2, (b % 2) * 512:(b % 2 + 1) * 512], banks[b][:, :]).then_inc(bank_free[b], dve.sends(bank_free[b]))
                dve_eng.wait_ge(dve.last, dve.value)
                dve_eng.wait_ge(sem("rows_loaded"), 16 * (2 * i + 2))
                layer_norm(y_nat, x_nat, rows[:, 0:D], rows[:, D:2 * D], "x_ready")

            dve_eng.wait_ge(dve.last, dve.value)

            def squares(src, a, n, dst):
                s = v3(sq[:, 0:a * n], a)
                v.tensor_tensor(s, src, src, MUL).then_inc(dve_step, dve.sends(dve_step))
                dve_eng.wait_ge(dve.last, dve.value)
                v.tensor_reduce(dst, s, AX, ADD).then_inc(dve_step, dve.sends(dve_step))

            def mean_eps(at, n, width, eps, last):
                ins = v.tensor_scalar(S_VAR[:, at:at + n], S_VAR[:, at:at + n], 1.0 / width, eps, MUL, ADD)
                if last:
                    ins.then_inc(sem("var_ready"), dve.sends(sem("var_ready")))
                else:
                    ins.then_inc(dve_step, dve.sends(dve_step))

            def scaled(view, r, gain, a, n):
                v.tensor_tensor(view, view, per_channel(r, n), MUL).then_inc(dve_step, dve.sends(dve_step))
                dve_eng.wait_ge(dve.last, dve.value)
                v.tensor_tensor(view, view, per_column(gain, a), MUL).then_inc(dve_step, dve.sends(dve_step))
                dve_eng.wait_ge(dve.last, dve.value)

            def rope(src, dst, nh):
                cos = bc(v3(cst[:, C_COS:C_COS + TT * HALF], TT).unsqueeze(2), P, TT, nh, HALF)
                sin = bc(v3(cst[:, C_SIN:C_SIN + TT * HALF], TT).unsqueeze(2), P, TT, nh, HALF)
                n = TT * nh * HALF
                t = [v4(sq[:, k * n:(k + 1) * n], TT, nh) for k in range(4)]
                lo, hi = src[:, :, :, 0:HALF], src[:, :, :, HALF:ROPE]
                v.tensor_tensor(t[0], lo, cos, MUL).then_inc(dve_step, dve.sends(dve_step))
                v.tensor_tensor(t[1], hi, sin, MUL).then_inc(dve_step, dve.sends(dve_step))
                v.tensor_tensor(t[2], hi, cos, MUL).then_inc(dve_step, dve.sends(dve_step))
                v.tensor_tensor(t[3], lo, sin, MUL).then_inc(dve_step, dve.sends(dve_step))
                dve_eng.wait_ge(dve.last, dve.value)
                if nh != NH:
                    t = [bc(s, P, TT, NH, HALF) for s in t]
                v.tensor_tensor(dst[:, :, :, 0:HALF], t[0], t[1], SUB).then_inc(dve_step, dve.sends(dve_step))
                return v.tensor_tensor(dst[:, :, :, HALF:ROPE], t[2], t[3], ADD)

            def flat3(ap):
                return ap.rearrange("p a b c -> p (a b) c")

            def shift(l, first, tiles):
                dve_eng.wait_ge(sem("shift_in"), dve.next("shift_in"))
                v.tensor_tensor(dcol[:, 0:tiles, :], pcol[:, 0:tiles, 0:T], pcol[:, 0:tiles, 1:T + 1], SUB).then_inc(dve_step, dve.sends(dve_step))
                dve_eng.wait_ge(dve.last, dve.value)
                for m in range(tiles):
                    mu = 12 + l * CP_LAYER + first + m
                    ins = v.scalar_tensor_tensor(sh[:, first + m, :], dcol[:, m, :], col[:, mu:mu + 1], pcol[:, m, 1:T + 1], MUL, ADD)
                    if m == tiles - 1:
                        ins.then_inc(sem("shift_done"), dve.sends(sem("shift_done")))
                    else:
                        ins.then_inc(dve_step, dve.sends(dve_step))

            def turned_qk(kdim):
                for dst, g, b in ((qTt, 0, 0), (qTt, 1, 1), (kTt, 0, 2), (kTt, 1, 3)):
                    copy_out(dst[0:kdim, 4 * g:4 * g + 4, 0:P], b, v3(banks[b][0:kdim, :], 4))

            def softmax(scale):
                for half in range(2):
                    for h in range(4 * half, 4 * half + 4):
                        b = h % NDB
                        dve_eng.wait_ge(bank_full[b], dve.next(("full", b)))
                        v.scalar_tensor_tensor(Pm[:, h, :], banks[b][:, 0:3 * P], scale, cst[:, C_CAUSAL:C_CAUSAL + 3 * P], MUL, ADD).then_inc(bank_free[b], dve.sends(bank_free[b]))
                    dve_eng.wait_ge(dve.last, dve.value)
                    hs, at = slice(4 * half, 4 * half + 4), 8 * half
                    v.tensor_reduce(S_MX[:, at:at + 4], Pm[:, hs, 0:P], AX, MAX).then_inc(dve_step, dve.sends(dve_step))
                    v.tensor_reduce(S_MX[:, at + 4:at + 8], Pm[:, hs, P:3 * P], AX, MAX).then_inc(dve_step, dve.sends(dve_step))
                    dve_eng.wait_ge(dve.last, dve.value)
                    v.tensor_scalar(S_NM[:, at:at + 8], S_MX[:, at:at + 8], -1.0, None, MUL).then_inc(sem("max_ready"), dve.sends(sem("max_ready")))

            def normalise():
                for half in range(2):
                    hs, at = slice(4 * half, 4 * half + 4), 8 * half
                    dve_eng.wait_ge(sem("exp_done"), dve.next("exp_done"))
                    v.reciprocal(S_RS[:, at:at + 8], S_SUM[:, at:at + 8]).then_inc(dve_step, dve.sends(dve_step))
                    dve_eng.wait_ge(dve.last, dve.value)
                    v.tensor_tensor(Pm[:, hs, 0:P], Pm[:, hs, 0:P], per_channel(S_RS[:, at:at + 4], P), MUL).then_inc(dve_step, dve.sends(dve_step))
                    v.tensor_tensor(Pm[:, hs, P:3 * P], Pm[:, hs, P:3 * P], per_channel(S_RS[:, at + 4:at + 8], T), MUL).then_inc(sem("p_ready"), dve.sends(sem("p_ready")))

            def gated_out(g):
                for j in range(4):
                    dve_eng.wait_ge(bank_full[j], dve.next(("full", j)))
                    v.tensor_tensor(oT[:, j, :], banks[j][:, 0:T], gates[:, g, j, :], MUL).then_inc(bank_free[j], dve.sends(bank_free[j]))

            def merge(first):
                dve_eng.wait_ge(sem("sgm_ready"), dve.next("sgm_ready"))
                for n in range(2):
                    for tt in range(TT):
                        b = n + 2 * tt
                        dve_eng.wait_ge(bank_full[b], dve.next(("full", b)))
                        half = slice(n * 512, (n + 1) * 512)
                        o = merged[:, tt, half] if first else sgm[:, tt, half]
                        v.tensor_tensor(o, banks[b][:, :], sgm[:, tt, half], MUL).then_inc(bank_free[b], dve.sends(bank_free[b]))
                dve_eng.wait_ge(dve.last, dve.value)
                if not first:
                    v.tensor_tensor(merged, merged, sgm, ADD).then_inc(dve_step, dve.sends(dve_step))

            for l in range(DEPTH):
                for tt in range(TT):
                    v.tensor_tensor_reduce(out=y_nat[:, tt, :], in0=x_nat[:, tt, :], in1=x_nat[:, tt, :], scale=1.0, scalar=0.0,
                                              op0=MUL, op1=ADD, accum_out=S_VAR[:, tt:tt + 1]).then_inc(dve_step, dve.sends(dve_step))
                dve_eng.wait_ge(dve.last, dve.value)
                mean_eps(0, TT, D, RMS_EPS, True)
                roots(TT)
                dve_eng.wait_ge(sem("rows_loaded"), 16 * (2 * DEPTH + l + 1))
                for tt in range(TT):
                    ins = v.scalar_tensor_tensor(y_nat[:, tt, :], x_nat[:, tt, :], S_RSTD[:, tt:tt + 1], rowv("norm"), MUL, MUL)
                    if tt:
                        ins.then_inc(sem("h_ready2"), dve.sends(sem("h_ready2")))
                    else:
                        ins.then_inc(dve_step, dve.sends(dve_step))
                turned_x()
                for tt in range(TT):
                    copy_out(cnat[:, tt, :], tt, banks[tt][:, 0:LAT])
                dve_eng.wait_ge(dve.last, dve.value)
                for at, a, n in ((0, 0, 256), (2, 256, 128), (4, 384, ROPE)):
                    squares(cnat[:, :, a:a + n], TT, n, S_VAR[:, at:at + 2])
                    dve_eng.wait_ge(dve.last, dve.value)
                mean_eps(0, 2, 256, RMS_EPS, False)
                mean_eps(2, 2, 128, RMS_EPS, False)
                mean_eps(4, 2, ROPE, RMS_EPS, True)
                roots(6)
                scaled(cnat[:, :, 384:LAT], S_RSTD[:, 4:6], rowv("kr"), TT, ROPE)
                scaled(cnat[:, :, 0:256], S_RSTD[:, 0:2], rowv("qa"), TT, 256)
                v.tensor_tensor(cnat[:, :, 256:384], cnat[:, :, 256:384], per_channel(S_RSTD[:, 2:4], 128), MUL).then_inc(dve_step, dve.sends(dve_step))
                dve_eng.wait_ge(dve.last, dve.value)
                v.tensor_tensor(cnat[:, :, 256:384], cnat[:, :, 256:384], per_column(rowv("kva"), TT), MUL).then_inc(sem("lat_ready"), dve.sends(sem("lat_ready")))
                n = TT * NH
                lf, lfe, neg = ffn[:, 0:n], ffn[:, n:2 * n], ffn[:, 2 * n:3 * n]
                dve_eng.wait_ge(bank_full[4], dve.next(("full", 4)))
                v.tensor_tensor(v3(lf, TT), v3(banks[4][:, 0:n], TT), per_column(rowv("bf"), TT), ADD).then_inc(bank_free[4], dve.sends(bank_free[4]))
                dve_eng.wait_ge(dve.last, dve.value)
                v.tensor_scalar(neg, lf, -1.0, None, MUL).then_inc(dve_step, dve.sends(dve_step))
                dve_eng.wait_ge(dve.last, dve.value)
                v.tensor_tensor(lfe, lf, neg, MIN).then_inc(sem("gates_neg"), dve.sends(sem("gates_neg")))
                v.tensor_scalar(lf, lf, 0.0, None, MIN).then_inc(dve_step, dve.sends(dve_step))
                dve_eng.wait_ge(dve.last, dve.value)
                copy_out(cT[:, 0:2, :], 2, v3(banks[2][:, :], 2))
                copy_out(cT[:, 2, :], 3, banks[3][:, 0:T])
                dve_eng.wait_ge(dve.last, dve.value)
                dve_eng.wait_ge(sem("gates_ln"), dve.next("gates_ln"))
                v.tensor_tensor(lf, lf, lfe, SUB).then_inc(sem("logf_ready"), dve.sends(sem("logf_ready")))
                for n4 in range(2):
                    for tt in range(TT):
                        b = 2 * n4 + tt
                        copy_out(qn[:, tt, 4 * n4:4 * n4 + 4, :], b, v3(banks[b][:, 0:4 * QK], 4))
                dve_eng.wait_ge(dve.last, dve.value)
                dve_eng.wait_ge(sem("kv_ready"), dve.next("kv_ready"))
                qf, kf = flat3(qn), flat3(kn)
                squares(qf, TT * NH, QK, S_VAR[:, 0:16])
                dve_eng.wait_ge(dve.last, dve.value)
                squares(kf[:, :, 0:NOPE], TT * NH, NOPE, S_VAR[:, 16:32])
                dve_eng.wait_ge(dve.last, dve.value)
                mean_eps(0, 16, QK, RMS_EPS, False)
                mean_eps(16, 16, NOPE, RMS_EPS, True)
                roots(32)
                scaled(qf, S_RSTD[:, 0:16], rowv("q"), TT * NH, QK)
                scaled(kf[:, :, 0:NOPE], S_RSTD[:, 16:32], rowv("kn"), TT * NH, NOPE)
                rope(qn[:, :, :, NOPE:QK], qn[:, :, :, NOPE:QK], NH).then_inc(dve_step, dve.sends(dve_step))
                dve_eng.wait_ge(dve.last, dve.value)
                krope = rope(cnat[:, :, 384:LAT].unsqueeze(2), kn[:, :, :, NOPE:QK], 1)
                krope.then_inc(sem("qk_ready"), dve.sends(sem("qk_ready")))
                v.memset(pcol[:, :, 0:1], 0.0).then_inc(dve_step, dve.sends(dve_step))
                dve_eng.wait_ge(dve.last, dve.value)
                for t in range(0, 8, 2):
                    shift(l, t, 2)
                turned_qk(QK)
                softmax(QK ** -0.5)
                cum_sb = neg
                copy_out(cum_sb, 4, banks[4][:, 0:TT * NH])
                for tt in range(TT):
                    copy_out(qn[:, tt, :, 0:HC], tt, v3(banks[tt][:, :], NH))
                for tt in range(TT):
                    copy_out(kn[:, tt, :, 0:HC], 2 + tt, v3(banks[2 + tt][:, :], NH))
                normalise()
                dve_eng.wait_ge(dve.last, dve.value)
                sqf = flat2(sgm)
                for src, at in ((qf, 0), (kf, 16)):
                    s = v3(sqf[:, 0:TT * NH * HC], TT * NH)
                    v.tensor_tensor(s, src[:, :, 0:HC], src[:, :, 0:HC], MUL).then_inc(dve_step, dve.sends(dve_step))
                    dve_eng.wait_ge(dve.last, dve.value)
                    v.tensor_reduce(S_VAR[:, at:at + 16], s, AX, ADD).then_inc(dve_step, dve.sends(dve_step))
                    dve_eng.wait_ge(dve.last, dve.value)
                mean_eps(0, 32, HC, RMS_EPS, True)
                roots(32)
                scaled(qf[:, :, 0:HC], S_RSTD[:, 0:16], rowv("fq"), TT * NH, HC)
                scaled(kf[:, :, 0:HC], S_RSTD[:, 16:32], rowv("fk"), TT * NH, HC)
                v.tensor_scalar(qf[:, :, 0:HC], qf[:, :, 0:HC], HC ** -0.5, None, MUL).then_inc(dve_step, dve.sends(dve_step))
                cum3 = cum_sb.unsqueeze(2)
                v.tensor_copy(qf[:, :, HC:HC + 1], cum3).then_inc(dve_step, dve.sends(dve_step))
                v.memset(qf[:, :, HC + 1:HC + 2], 1.0).then_inc(dve_step, dve.sends(dve_step))
                v.memset(kf[:, :, HC:HC + 1], 1.0).then_inc(dve_step, dve.sends(dve_step))
                v.tensor_scalar(kf[:, :, HC + 1:HC + 2], cum3, -1.0, None, MUL).then_inc(sem("qk_ready"), dve.sends(sem("qk_ready")))
                gated_out(0)
                for t in range(8, 12, 2):
                    shift(l, t, 2)
                shift(l, 12, 1)
                dve_eng.wait_ge(dve.last, dve.value)
                turned_qk(FOXK)
                softmax(1.0)
                merge(True)
                normalise()
                gated_out(1)
                merge(False)
                dve_eng.wait_ge(dve.last, dve.value)
                v.tensor_copy(S_BIG[:, 0:1], sh[:, 12, 0:1]).then_inc(sem("shift_ready"), dve.sends(sem("shift_ready")))
                if l == 0:
                    v.tensor_copy(vfirst, vlT).then_inc(dve_step, dve.sends(dve_step))
                    dve_eng.wait_ge(dve.last, dve.value)
                else:
                    copy_out(v_mid, 4, banks[4][0:32, 0:T])
                    for g in range(2):
                        dve_eng.wait_ge(bank_full[g], dve.next(("full", g)))
                        v.tensor_tensor(nuT[:, 2 * g:2 * g + 2, :], v3(banks[g][:, :], 2), per_channel(colv(l, V0)[:, 2 * g:2 * g + 2], T), ADD).then_inc(bank_free[g], dve.sends(bank_free[g]))
                    dve_eng.wait_ge(dve.last, dve.value)
                    v.tensor_tensor(vdiff, vfirst, vlT, SUB).then_inc(sem("nu_in"), dve.sends(sem("nu_in")))
                    dve_eng.wait_ge(sem("nu_ready"), dve.next("nu_ready"))
                    dve_eng.wait_ge(dve.last, dve.value)
                    v.tensor_tensor(vdiff, vdiff, nuT, MUL).then_inc(dve_step, dve.sends(dve_step))
                    dve_eng.wait_ge(dve.last, dve.value)
                    v.tensor_tensor(vlT, vlT, vdiff, ADD).then_inc(dve_step, dve.sends(dve_step))
                    dve_eng.wait_ge(dve.last, dve.value)
                for tt in range(TT):
                    tok = slice(tt * P, (tt + 1) * P)
                    r_, k_, v_ = rlT[:, :, tok], klT[:, :, tok], vlT[:, :, tok]
                    v.tensor_copy(S_BIG[:, 0:1], sh[:, 12, 0:1]).then_inc(sem("shift_all"), dve.sends(sem("shift_all")))
                    v.tensor_tensor(kk, k_, per_channel(colv(l, KK), P), MUL).then_inc(dve_step, dve.sends(dve_step))
                    dve_eng.wait_ge(dve.last, dve.value)
                    v.tensor_tensor(t1, kk, kk, MUL).then_inc(sem("ksq_ready"), dve.sends(sem("ksq_ready")))
                    dve_eng.wait_ge(bank_full[0], dve.next(("full", 0)))
                    v.tensor_tensor(lw, v3(banks[0][:, :], 4), per_channel(colv(l, W0), P), ADD).then_inc(bank_free[0], dve.sends(bank_free[0]))
                    dve_eng.wait_ge(bank_full[1], dve.next(("full", 1)))
                    v.tensor_tensor(aa, v3(banks[1][:, :], 4), per_channel(colv(l, A0), P), ADD).then_inc(bank_free[1], dve.sends(bank_free[1]))
                    dve_eng.wait_ge(dve.last, dve.value)
                    v.tensor_copy(S_BIG[:, 0:1], sh[:, 12, 0:1]).then_inc(sem("wa_in"), dve.sends(sem("wa_in")))
                    dve_eng.wait_ge(bank_full[2], dve.next(("full", 2)))
                    v.tensor_scalar(flat2(t1), banks[2][:, :], 1e-24, None, MAX).then_inc(bank_free[2], dve.sends(bank_free[2]))
                    dve_eng.wait_ge(dve.last, dve.value)
                    v.tensor_copy(S_BIG[:, 0:1], sh[:, 12, 0:1]).then_inc(sem("ksum_ready"), dve.sends(sem("ksum_ready")))
                    dve_eng.wait_ge(sem("wa_ready"), dve.next("wa_ready"))
                    v.tensor_scalar(flat2(lw), flat2(lw), DECAY, None, MUL).then_inc(dve_step, dve.sends(dve_step))
                    dve_eng.wait_ge(dve.last, dve.value)
                    v.tensor_tensor_scan(flat2(cum), cst[:, C_SCAN:C_SCAN + 4 * P], flat2(lw), 0.0, MUL, ADD).then_inc(dve_step, dve.sends(dve_step))
                    dve_eng.wait_ge(dve.last, dve.value)
                    v.tensor_tensor(pex, cum, lw, SUB).then_inc(sem("cum_ready"), dve.sends(sem("cum_ready")))
                    dve_eng.wait_ge(sem("knorm_ready"), dve.next("knorm_ready"))
                    v.reciprocal(flat2(t1), flat2(t1)).then_inc(dve_step, dve.sends(dve_step))
                    dve_eng.wait_ge(dve.last, dve.value)
                    v.tensor_tensor(kk, kk, t1, MUL).then_inc(dve_step, dve.sends(dve_step))
                    dve_eng.wait_ge(dve.last, dve.value)
                    v.tensor_scalar(flat2(t1), flat2(aa), -1.0, None, ADD).then_inc(dve_step, dve.sends(dve_step))
                    dve_eng.wait_ge(dve.last, dve.value)
                    v.tensor_tensor(t1, t1, per_channel(colv(l, KA), P), MUL).then_inc(dve_step, dve.sends(dve_step))
                    dve_eng.wait_ge(dve.last, dve.value)
                    v.tensor_scalar(flat2(t1), flat2(t1), 1.0, None, ADD).then_inc(dve_step, dve.sends(dve_step))
                    dve_eng.wait_ge(dve.last, dve.value)
                    v.tensor_tensor(km, t1, k_, MUL).then_inc(dve_step, dve.sends(dve_step))
                    dve_eng.wait_ge(dve.last, dve.value)
                    v.tensor_tensor(rk, km, r_, MUL).then_inc(dve_step, dve.sends(dve_step))
                    dve_eng.wait_ge(dve.last, dve.value)
                    v.tensor_tensor(rk, rk, per_channel(colv(l, RK), P), MUL).then_inc(dve_step, dve.sends(dve_step))
                    dve_eng.wait_ge(dve.last, dve.value)
                    v.tensor_scalar(flat2(aa), flat2(aa), -1.0, None, MUL).then_inc(dve_step, dve.sends(dve_step))
                    dve_eng.wait_ge(sem("decay_ready"), dve.next("decay_ready"))
                    v.tensor_copy(pcs.unsqueeze(2), pp.rearrange("p a (c t) -> p (a c) t", c=2)[:, :, CH - 1:CH]).then_inc(dve_step, dve.sends(dve_step))
                    dve_eng.wait_ge(dve.last, dve.value)
                    v.tensor_tensor(aa, aa, kk, MUL).then_inc(dve_step, dve.sends(dve_step))
                    dve_eng.wait_ge(dve.last, dve.value)
                    v.tensor_tensor(pex, pex, kk, MUL).then_inc(dve_step, dve.sends(dve_step))
                    v.tensor_tensor(aa, aa, pinv, MUL).then_inc(dve_step, dve.sends(dve_step))
                    dve_eng.wait_ge(dve.last, dve.value)
                    v.tensor_tensor(pinv, pinv, km, MUL).then_inc(dve_step, dve.sends(dve_step))
                    dve_eng.wait_ge(dve.last, dve.value)

                    def to_end(dst, src):
                        return v.tensor_tensor(dst.rearrange("p a (c t) -> p (a c) t", c=2), src.rearrange("p a (c t) -> p (a c) t", c=2),
                                               per_channel(pcs, CH), MUL)

                    to_end(cum, aa).then_inc(dve_step, dve.sends(dve_step))
                    to_end(lw, pinv).then_inc(dve_step, dve.sends(dve_step))
                    v.tensor_tensor(pp, pp, r_, MUL).then_inc(sem("rows_ready"), dve.sends(sem("rows_ready")))
                    for par in range(2):
                        copy_out(NTm[:, par, :, :], 0, v3(banks[0][:, :], 4))
                        for b, dst, mask in ((1, MTm, C_STRICT), (2, AkT, C_INCL), (3, AbT, C_INCL)):
                            dve_eng.wait_ge(bank_full[b], dve.next(("full", b)))
                            v.tensor_tensor(dst[:, par, :, :], v3(banks[b][:, :], 4), mat4(mask), MUL).then_inc(bank_free[b], dve.sends(bank_free[b]))
                    dve_eng.wait_ge(bank_full[4], dve.next(("full", 4)))
                    v.tensor_copy(S_RS[:, 0:NH], banks[4][:, 0:NH]).then_inc(dve_step, dve.sends(dve_step))
                    v.tensor_copy(pc0[0:64, :], banks[4][0:64, 64:80]).then_inc(bank_free[4], dve.sends(bank_free[4]))
                    copy_out(Kp, 3, banks[3][:, :])
                    dve_eng.wait_ge(dve.last, dve.value)
                    for par in range(2):
                        v.tensor_tensor(Nl[:, par, :, :], NTm[:, par, :, :], mat4(C_LEV), MUL).then_inc(dve_step, dve.sends(dve_step))
                        dve_eng.wait_ge(dve.last, dve.value)
                        v.tensor_tensor(TTm[:, par, :, :], Nl[:, par, :, :], mat4(C_ID), ADD).then_inc(sem("level_ready"), dve.sends(sem("level_ready")))
                    for par in range(2):
                        copy_out(Tm[:, par, :, :], par, v3(banks[par][:, :], 4))
                        dve_eng.wait_ge(dve.last, dve.value)
                        v.tensor_tensor(Nl[:, par, :, :], NTm[:, par, :, :], mat4(C_LEV + P), MUL).then_inc(sem("level_ready"), dve.sends(sem("level_ready")))
                    for lev in range(1, LEVELS):
                        for par in range(2):
                            if lev < LEVELS - 1:
                                dve_eng.wait_ge(bank_full[2 * par], dve.next(("full", 2 * par)))
                                v.tensor_tensor(Tm[:, par, :, :], Tm[:, par, :, :], v3(banks[2 * par][:, :], 4), ADD).then_inc(bank_free[2 * par], dve.sends(bank_free[2 * par]))
                            dve_eng.wait_ge(bank_full[2 * par + 1], dve.next(("full", 2 * par + 1)))
                            v.tensor_tensor(TTm[:, par, :, :], TTm[:, par, :, :], v3(banks[2 * par + 1][:, :], 4), ADD).then_inc(bank_free[2 * par + 1], dve.sends(bank_free[2 * par + 1]))
                            if lev < LEVELS - 1:
                                v.tensor_tensor(Nl[:, par, :, :], NTm[:, par, :, :], mat4(C_LEV + (lev + 1) * P), MUL).then_inc(sem("level_ready"), dve.sends(sem("level_ready")))
                    copy_out(Wn, 2, banks[2][:, :])
                    copy_out(mv, 3, banks[3][:, :])
                    copy_out(uv, 4, banks[4][:, :])
                    chunks = (0, 1) if tt == 0 else (0,)
                    for c in chunks:
                        g = 2 * tt + c
                        if g:
                            shape = [64, 4, 2, HC]
                            diag = ysq[0:64, :]
                            dec = pc0[0:64, :].rearrange("p (b a c) -> p a b c", b=2, c=2)[:, :, :, c:c + 1]
                            v.tensor_tensor(v4(diag, 4, 2), bc(mat(C_ID)[0:64, 0:64].unsqueeze(1).unsqueeze(1), *shape), bc(dec, *shape), MUL).then_inc(dve_step, dve.sends(dve_step))
                            dve_eng.wait_ge(dve.last, dve.value)
                            dve_eng.wait_ge(bank_full[c], dve.next(("full", c)))
                            v.tensor_tensor(GT[0:64, c, :, :], v3(banks[c][0:64, :], NH), v3(diag, NH), ADD).then_inc(bank_free[c], dve.sends(bank_free[c]))
                            copy_out(Hs[0:64, c, :], 2 + c, banks[2 + c][0:64, :])
                        else:
                            copy_out(states[0][0:64, :], 2, banks[2][0:64, :])
                    dve_eng.wait_ge(dve.last, dve.value)
                    for c in chunks:
                        g = 2 * tt + c
                        if g:
                            dve_eng.wait_ge(bank_full[4], dve.next(("full", 4)))
                            v.tensor_tensor(states[g][0:64, :], banks[4][0:64, :], Hs[0:64, c, :], ADD).then_inc(bank_free[4], dve.sends(bank_free[4]))
                    copy_out(yv, 4, banks[4][:, :])
                    dve_eng.wait_ge(dve.last, dve.value)
                    y3, q3 = v3(yv, NH), v3(ysq, NH)
                    v.tensor_reduce(S_MX[:, 0:NH], y3, AX, ADD).then_inc(dve_step, dve.sends(dve_step))
                    dve_eng.wait_ge(dve.last, dve.value)
                    v.tensor_scalar(S_MX[:, 0:NH], S_MX[:, 0:NH], 1.0 / HC, None, MUL).then_inc(dve_step, dve.sends(dve_step))
                    dve_eng.wait_ge(dve.last, dve.value)
                    v.tensor_tensor(y3, y3, per_channel(S_MX[:, 0:NH], HC), SUB).then_inc(dve_step, dve.sends(dve_step))
                    dve_eng.wait_ge(dve.last, dve.value)
                    v.tensor_tensor(ysq, yv, yv, MUL).then_inc(dve_step, dve.sends(dve_step))
                    dve_eng.wait_ge(dve.last, dve.value)
                    v.tensor_reduce(S_VAR[:, 0:NH], q3, AX, ADD).then_inc(dve_step, dve.sends(dve_step))
                    dve_eng.wait_ge(dve.last, dve.value)
                    mean_eps(0, NH, HC, GN_EPS, True)
                    roots(NH)
                    v.tensor_tensor(y3, y3, per_channel(S_RSTD[:, 0:NH], HC), MUL).then_inc(dve_step, dve.sends(dve_step))
                    dve_eng.wait_ge(dve.last, dve.value)
                    v.tensor_tensor(yv, yv, rowv("lg"), MUL).then_inc(dve_step, dve.sends(dve_step))
                    dve_eng.wait_ge(dve.last, dve.value)
                    v.tensor_tensor(q3, v3(Vn, NH), per_channel(S_RS[:, 0:NH], HC), MUL).then_inc(dve_step, dve.sends(dve_step))
                    v.tensor_tensor(yv, yv, rowv("lb"), ADD).then_inc(dve_step, dve.sends(dve_step))
                    dve_eng.wait_ge(dve.last, dve.value)
                    v.tensor_tensor(yv, yv, ysq, ADD).then_inc(sem("y_ready"), dve.sends(sem("y_ready")))
                    dve_eng.wait_ge(bank_full[0], dve.next(("full", 0)))
                    v.tensor_tensor(oT[:, :, tok], v3(banks[0][:, :], 4), gates[:, 0, :, tok], MUL).then_inc(bank_free[0], dve.sends(bank_free[0]))
                merge(False)
                dve_eng.wait_ge(dve.last, dve.value)
                v.tensor_copy(S_BIG[:, 0:1], merged[:, 1, D - 1:D]).then_inc(sem("merged_ready"), dve.sends(sem("merged_ready")))
                turned_x()
                for n in range(2):
                    for tt in range(TT):
                        b = n + 2 * tt
                        dve_eng.wait_ge(bank_full[b], dve.next(("full", b)))
                        half = slice(n * 512, (n + 1) * 512)
                        v.tensor_tensor(x_nat[:, tt, half], x_nat[:, tt, half], banks[b][:, :], ADD).then_inc(bank_free[b], dve.sends(bank_free[b]))
                dve_eng.wait_ge(dve.last, dve.value)
                v.tensor_copy(S_BIG[:, 0:1], x_nat[:, 1, D - 1:D]).then_inc(sem("x_ready"), dve.sends(sem("x_ready")))


def constants():
    import numpy as np
    c = np.zeros((P, NCONST), np.float32)
    i, t = np.arange(P)[:, None], np.arange(P)[None, :]
    same = i // CH == t // CH
    c[:, C_ID:C_ID + P] = i == t
    c[:, C_STRICT:C_STRICT + P] = (i < t) & same
    c[:, C_INCL:C_INCL + P] = (i <= t) & same
    c[:, C_BLOCK:C_BLOCK + P] = same
    c[:, C_TRI:C_TRI + P] = i <= t
    c[:, C_ONES:C_ONES + P] = 1
    c[:, C_ALPHA:C_ALPHA + P] = (i == t) * ALPHA
    for n in range(LEVELS):
        b = 1 << n
        c[:, C_LEV + n * P:C_LEV + (n + 1) * P] = (i // (2 * b) == t // (2 * b)) & (i % (2 * b) < b) & (t % (2 * b) >= b)
    causal = np.where(t <= i, 0.0, -1e30)
    c[:, C_CAUSAL:C_CAUSAL + P] = causal
    c[:, C_CAUSAL + 2 * P:C_CAUSAL + 3 * P] = causal
    c[:, C_SCAN:C_SCAN + 4 * P] = np.arange(4 * P)[None, :] % CH != 0
    c[:, C_SGU:C_SGU + P] = t // CH >= i // CH
    inv = np.float32(10000.0) ** (-np.arange(0, ROPE, 2, dtype=np.float32) / ROPE)
    ang = np.arange(T, dtype=np.float32)[:, None] * inv[None, :].astype(np.float32)
    for at, f in ((C_COS, np.cos), (C_SIN, np.sin)):
        c[:, at:at + TT * HALF] = f(ang).reshape(TT, P, HALF).transpose(1, 0, 2).reshape(P, -1)
    for j in range(4):
        for m in range(2):
            c[64 * m:64 * m + 64, C_SEL + j * NH + 2 * j + m] = 1
    own, other = np.arange(GS)[:, None], np.arange(GS)[None, :]
    c[:, C_TIE:C_TIE + GS * GS] = (other < own).reshape(1, -1)
    return c


def kernel(**inputs):
    import numpy as np
    import concourse.bacc as bacc
    from concourse import mybir
    from concourse.bass_utils import run_bass_kernel_spmd

    a = {k: np.asarray(v) for k, v in inputs.items()}

    def tiles(w):
        k, n = w.shape
        return w.reshape(k // P, P, n).transpose(1, 0, 2).reshape(P, -1)

    def cut(w, edges):
        return [tiles(w[:, lo:hi]) for lo, hi in zip(edges[:-1], edges[1:])]

    def chan(w):
        return w.reshape(-1, P).T

    def cat(parts):
        return np.ascontiguousarray(np.concatenate(parts, axis=1))

    halves, half3, half4 = (0, 512, 1024), (0, 512, 1024, 1536), (0, 512, 1024, 1536, 2048)
    first = [cat(cut(a["w_kv"][i], halves) + cut(w, e) + cut(a["w_out"][i], halves))
             for i, (w, e) in enumerate(((a["w_in_a"][0], half3), (a["w_in_b"][0], half4)))]
    moe = np.empty((DEPTH, NE, PER_EXPERT, P, SLOT), np.float32)
    for s, name, k in ((0, "w_gate", KD), (1, "w_up", KD), (2, "w_down", KM)):
        w = a[name]
        moe[:, :, s] = w.reshape(DEPTH, NE, k, P, w.shape[-1]).transpose(0, 1, 3, 2, 4).reshape(DEPTH, NE, P, SLOT)
    moe = moe.reshape(DEPTH, NE // EPB, EPB * PER_EXPERT, P, SLOT)

    at = np.cumsum([0, LAT, MIX, MIX, MIX, MIX, NH, MIX, MIX, MIX, MIX, 128, MIX])
    c_lat, c_ga, c_fq, c_fk, c_fv, c_ff, c_gb, c_r, c_k, c_v, c_wa, c_gc, c_mg = at
    second, ff, lora, cols, rows2 = [], [], [], [], []
    colp = [a["conv_w"][0].reshape(3, 4, P).transpose(2, 1, 0).reshape(P, 12)]
    for l in range(DEPTH):
        w = a["w_in_2"][l]

        def c(lo, n=MIX):
            return tiles(w[:, lo:lo + n])

        parts = [c(c_lat, LAT), c(c_ga), tiles(a["mla_w_uq_2"][l]), tiles(a["mla_w_ukv_2"][l]), c(c_r), c(c_k), c(c_fq), c(c_fk),
                 c(c_fv), c(c_gb), c(c_v), c(c_wa, P)]
        parts += [tiles(a["w_pa_2"][l]), c(c_mg), c(c_mg + 512), c(c_gc), tiles(a["w_pb_2"][l]), c(c_mg + 1024), c(c_mg + 1536),
                  tiles(a["w_pc_2"][l]), c(c_mg + 2048), c(c_mg + 2560)] + cut(a["w_out_2"][l], halves)
        assert [p.shape[1] for p in parts] == LOADS_SECOND
        second.append(cat(parts))
        ff.append(c(c_ff, NH).reshape(P, KD, NH))
        lo = np.zeros((P, 1152), np.float32)
        lo[0:64, 0:512], lo[64:128, 0:512] = a["rwkv_w_up_2"][l], a["rwkv_a_up_2"][l]
        lo[:, 512:640] = tiles(a["rwkv_v_down_2"][0])
        lo[0:32, 640:1152] = a["rwkv_v_up_2"][0]
        lora.append(lo)
        colp += [chan(a[n + "_2"][l].reshape(-1)) for n in ("rwkv_mu", "rwkv_w0", "rwkv_a0", "rwkv_k_k", "rwkv_k_a", "rwkv_r_k")]
        colp.append(chan(a["rwkv_v0_2"][0]))
        rows2.append(np.concatenate([a[n + "_2"][l] for n in ("norm_g", "mla_qa_g", "mla_kva_g", "mla_q_g", "mla_knope_g", "mla_krope_g",
                                                             "fox_q_g", "fox_k_g", "fox_b_f", "rwkv_lnx_g", "rwkv_lnx_b")]))
    tokens = a["x"][0]
    arrays = {
        "x0": tokens.reshape(TT, P, D).transpose(1, 0, 2), "x0T": tokens.T.reshape(KD, P, T).transpose(1, 0, 2),
        "memT0": a["mem"][0].T.reshape(KD, P, T).transpose(1, 0, 2), "sguT": a["sgu_w"][0].transpose(2, 0, 1),
        "wfirst0": first[0], "wfirst1": first[1], "wmoe": moe, "wsecond": np.stack(second), "wff": np.stack(ff),
        "lora": np.stack(lora), "rw": tiles(a["router_w"]).reshape(P, KD, NE), "consts": constants(), "colp": np.concatenate(colp, axis=1),
        "rowa": np.concatenate([a["sgu_ln_g"][0], a["sgu_ln_b"][0], a["sgu_b"][0].reshape(-1), a["router_b"]])[None],
        "lnrows": np.stack([np.concatenate([a[g][i], a[b][i]]) for i in range(DEPTH) for g, b in (("ln1_g", "ln1_b"), ("ln2_g", "ln2_b"))]),
        "rows2": np.stack(rows2),
    }
    arrays = {k: np.ascontiguousarray(v) for k, v in arrays.items()}
    nc = bacc.Bacc("TRN2", target_bir_lowering=False, num_devices=1)
    aps = [nc.dram_tensor(k, v.shape, mybir.dt.float32, kind="ExternalInput").ap() for k, v in arrays.items()]
    out = nc.dram_tensor("out", (P, TT, D), mybir.dt.float32, kind="ExternalOutput").ap()
    two_blocks(nc, *aps, out)
    r = run_bass_kernel_spmd(nc, [arrays], core_ids=[0])
    got = r.results[0]["out"]
    return got.transpose(1, 0, 2).reshape(1, T, D)
```

```python
import concourse.bass as bass
from concourse import mybir
from contextlib import ExitStack

P = 128
T = 256
TT = T // P
D = 1024
KD = D // P
MIX = 512
KM = MIX // P
NHX = 4
XSCALE = P ** -0.5
NE, NG, GS = 16, 4, 4
F = 512
DEPTH = 2
ALPHA = (2 * DEPTH) ** 0.25
LN_EPS, RMS_EPS, GN_EPS = 1e-5, 1e-6, 64e-5
NH = 8
HC = 64
NOPE, ROPE, QK = 64, 32, 96
HALF = ROPE // 2
FOXK = 66
LAT = 416
CH = 64
DECAY = -0.606531
SLOT = 4096
RING = 4
PER_EXPERT = 3
HSIGS = NE + 1
GSIGS = NG + 1
GROUP_SLOTS = (("gate", 0), ("up", 0), ("gate", 1), ("up", 1), ("down", 0), ("gate", 2), ("up", 2), ("down", 1),
               ("gate", 3), ("up", 3), ("down", 2), ("down", 3))
NDB = 5

LOADS_FIRST = [[SLOT] * 7, [SLOT] * 8]
LOADS_SECOND = ([KD * LAT, SLOT, 1536, 1024, SLOT, SLOT, SLOT, SLOT, SLOT, SLOT, SLOT, KD * P] + [SLOT] * 12)

C_ID, C_STRICT, C_INCL, C_BLOCK, C_TRI, C_ONES, C_ALPHA, C_LEV = [P * n for n in range(8)]
LEVELS = 6
C_CAUSAL = C_LEV + LEVELS * P
C_SCAN = C_CAUSAL + 3 * P
C_SGU = C_SCAN + 4 * P
C_COS = C_SGU + P
C_SIN = C_COS + TT * HALF
C_SEL = C_SIN + TT * HALF
C_TIE = C_SEL + 4 * NH
C_IOTA = C_TIE + GS * GS
NCONST = C_IOTA + T

CP_CONV = 0
CP_LAYER = 13 + 6 * 4
NCOLP = 12 + DEPTH * CP_LAYER
W0, A0, KK, KA, RK, V0 = range(6)

R_SGUG, R_SGUB, R_SGUBIAS, R_RB = 0, MIX, 2 * MIX, 3 * MIX
NROWA = R_RB + NE
ROWS = {}
NROWS = 0
for _name, _n in (("norm", D), ("qa", 256), ("kva", 128), ("q", QK), ("kn", NOPE), ("kr", ROPE), ("fq", HC),
                  ("fk", HC), ("bf", NH), ("lg", MIX), ("lb", MIX)):
    ROWS[_name] = (NROWS, _n)
    NROWS += _n


def two_blocks(nc, x0, x0T, memT0, sguT, wfirst0, wfirst1, wmoe, wsecond, wff, lora, rw, consts, colp, rowa, lnrows, rows2, out):
    f32 = mybir.dt.float32
    ALU = mybir.AluOpType
    ACT = mybir.ActivationFunctionType
    AX = mybir.AxisListType.X
    MUL, ADD, SUB, MAX, MIN = ALU.mult, ALU.add, ALU.subtract, ALU.max, ALU.min

    ctx = ExitStack()
    with ctx:
        def sb(name, n):
            return ctx.enter_context(nc.sbuf_tensor(name, [P, n], f32))[:, :]

        semaphores = {}

        def sem(name):
            if name not in semaphores:
                semaphores[name] = ctx.enter_context(nc.semaphore(name))
            return semaphores[name]

        def v3(ap, a):
            return ap.rearrange("p (a b) -> p a b", a=a)

        def v4(ap, a, b):
            return ap.rearrange("p (a b c) -> p a b c", a=a, b=b)

        ring = sb("ring", RING * SLOT)
        cst = sb("cst", NCONST)
        col = sb("col", NCOLP)
        x_nat = v3(sb("x_nat", TT * D), TT)
        wide = sb("wide", SLOT)
        y_nat = v3(wide[:, 0:TT * D], TT)
        xT = v3(wide[:, TT * D:SLOT], KD)
        spill_w = wide
        rows = sb("rows", NROWS)
        rwt = v3(sb("rwt", KD * NE), KD)
        small = sb("small", 640)
        ARENA = 23950
        arena = sb("arena", ARENA)
        banks = [ctx.enter_context(nc.psum_tensor(f"bank{b}", [P, 512], f32)) for b in range(8)]

        class Carve:
            def __init__(self, at=0):
                self.at = at

            def __call__(self, *shape):
                n = 1
                for s in shape:
                    n *= s
                ap = arena[:, self.at:self.at + n]
                self.at += n
                assert self.at <= ARENA, self.at
                if len(shape) == 2:
                    return v3(ap, shape[0])
                if len(shape) == 3:
                    return v4(ap, shape[0], shape[1])
                return ap

        def bc(ap, *shape):
            return ap.to_broadcast(list(shape))

        def mat(c):
            return cst[:, c:c + P]

        def mat4(c):
            return bc(mat(c).unsqueeze(1), P, 4, P)

        ident = mat(C_ID)

        def per_channel(ap, n):
            return bc(ap.unsqueeze(2), P, ap.shape[1], n)

        def per_column(ap, n):
            return bc(ap.unsqueeze(1), P, n, ap.shape[1])

        S_BN, S_MV, S_VAR, S_RSTD = small[:, 0:24], small[:, 24:28], small[:, 28:60], small[:, 60:92]
        S_MX, S_NM, S_SUM, S_RS = small[:, 92:108], small[:, 108:124], small[:, 124:140], small[:, 140:156]
        S_SC, S_SEL, S_COMB = small[:, 160:192], small[:, 192:224], small[:, 224:256]
        S_GSC, S_GRANK, S_RANK = small[:, 256:264], small[:, 264:272], small[:, 272:304]
        S_BIG, S_BIG2 = small[:, 304:432], small[:, 432:560]
        S_KEY, S_C4, S_CG, S_CNT = small[:, 560:568], small[:, 568:576], small[:, 576:592], small[:, 592:596]
        S_CGS, S_KMAX = small[:, 596:600], small[:, 604:606]
        spill_info = ctx.enter_context(nc.sbuf_tensor("spill_info", [P, 2], mybir.dt.int32))[:, :]
        S_MARK = small[:, 600:604]

        c1 = Carve()
        memT = c1(KD, T)
        rowa_sb = c1(NROWA)
        kT, vmem = c1(4, T), c1(TT, MIX)
        base1 = c1.at
        qT = c1(4, T)
        catT = c1(KD, T)
        uT = c1(4, T)
        vv = c1(TT, MIX)
        cgT, tmpT = c1(4, T), c1(4, T)
        hpad = c1(4, T + 2)
        sgw = c1(4, P)
        xsc, xPT = c1(NHX, TT, T), c1(NHX, TT, T)
        bgT = uT
        ce = Carve(base1)
        xg = ce(NG, KD, P)
        og = ce(NG, D)
        og_spill = ce(D)
        pick = ce(TT, NG, P)
        put = ce(TT, NG, P)
        put_spill = ce(TT, P)
        sg, hh = ce(F), ce(F)
        hT = ce(2, KM, P)
        xg_now = ce(KD, P)

        c2 = Carve()
        gates = c2(2, 4, T)
        sh = c2(13, T)
        rlT, klT, vlT = sh[:, 0:4, :], sh[:, 4:8, :], sh[:, 8:12, :]
        lora_sb = c2(1152)
        wup, vdown, vup = lora_sb[:, 0:512], v3(lora_sb[:, 512:640], 4), lora_sb[:, 640:1152]
        wff_sb = c2(KD, NH)
        oT = c2(4, T)
        vfirst = c2(4, T)
        merged = y_nat
        base2 = c2.at
        ca = Carve(base2)
        pcol = ca(2, T + 1)
        cnat = ca(TT, LAT)
        dcol = v3(arena[:, ca.at - TT * LAT:ca.at - TT * LAT + 2 * T], 2)
        cT = ca(3, T)
        PT = v3(arena[:, ca.at - 3 * T:ca.at], 2)
        qn, kn = ca(TT, NH, QK), ca(TT, NH, QK)
        vn2 = [ca(TT, NH, HC), ca(TT, NH, HC)]
        qTt, kTt = ca(NH, T), ca(NH, T)
        Pm = ca(NH, 3 * P)
        ffn = ca(3 * TT * NH)
        sq = Pm.rearrange("p a b -> p (a b)")
        sgm = v3(qTt.rearrange("p a b -> p (a b)"), TT)
        cr = Carve(base2)
        t_at = cr.at
        lw, cum, pp, pinv, pex, aa, kk, km, t1 = (cr(4, P) for _ in range(9))
        ci = Carve(t_at)
        Tm, TTm, Xm, Nl = (ci(2, 4, P) for _ in range(4))
        rk = cr(4, P)
        tw = cr(P)
        NTm, MTm, AkT, AbT = (cr(2, 4, P) for _ in range(4))
        Vn, Kn, Rn, Bn, Kp = (cr(MIX) for _ in range(5))
        Hs = cr(2, MIX)
        states = [cr(MIX) for _ in range(3)]
        pcs, pc0 = cr(8), cr(16)

        def flat2(ap):
            return ap.rearrange("p a b -> p (a b)")

        v_mid = flat2(t1)[0:32, 0:T]
        nuT = v3(arena[:, t_at + 5 * 512:t_at + 7 * 512], 4)
        vdiff = v3(arena[:, t_at:t_at + 2 * 512], 4)
        Wn, mv = flat2(Xm[:, 0, :, :]), flat2(Xm[:, 1, :, :])
        uv, yv = flat2(Nl[:, 0, :, :]), flat2(Nl[:, 1, :, :])
        QT = NTm
        GT = v4(MTm.rearrange("p a b c -> p (a b c)"), 2, NH)
        ysq = flat2(Tm[:, 0, :, :])

        def rowv(name):
            a, n = ROWS[name]
            return rows[:, a:a + n]

        def colv(l, which):
            a = 12 + l * CP_LAYER + 13 + 4 * which
            return col[:, a:a + 4]

        def hc(ap, h):
            return ap[:, h * HC:(h + 1) * HC]

        bank_full = [sem(f"bank_full{b}") for b in range(8)]
        bank_free = [sem(f"bank_free{b}") for b in range(8)]
        dve_step, act_step = sem("dve_step"), sem("act_step")

        class Counts:
            def __init__(self):
                self.seen, self.sent = {}, {}
                self.last, self.value = None, 0

            def next(self, name):
                self.seen[name] = self.seen.get(name, 0) + 1
                return self.seen[name]

            def sends(self, s):
                first = 1 if s in bank_free else 0
                self.sent[s.name] = self.sent.get(s.name, first) + 1
                self.last, self.value = s, self.sent[s.name]
                return 1

        class TensorCounts(Counts):
            def __init__(self):
                super().__init__()
                self.uses = [0] * 8
                self.slots = 0
                self.open = False
                self.pending = 0

            def reuse(self, b):
                self.uses[b] += 1
                return self.uses[b]

            def used(self, b):
                return self.uses[b] + 1

            def close(self):
                if self.open:
                    self.pending += 1
                    self.open = False

        block = ctx.enter_context(nc.Block())
        per_body = GS * PER_EXPERT

        @block.sync
        def _(sp):
            n = 0

            def load(src, width):
                nonlocal n
                if n >= RING:
                    sp.wait_ge(sem("ring_free"), n - RING + 1)
                s = n % RING
                sp.dma_start(ring[:, s * SLOT:s * SLOT + width], src).then_inc(sem(f"ring_full{s}"), 16)
                n += 1

            sp.dma_start(x_nat, x0).then_inc(sem("x_loaded"), 16)
            for i in range(DEPTH):
                at = 0
                for width in LOADS_FIRST[i]:
                    load((wfirst0, wfirst1)[i][:, at:at + width], width)
                    at += width
                with sp.Fori(0, NG) as j:
                    for s in range(per_body):
                        sp.wait_ge(sem("ring_free"), j * per_body + (n + s - RING + 1))
                        r = (n + s) % RING
                        sp.dma_start(ring[:, r * SLOT:(r + 1) * SLOT],
                                     wmoe[i, j, s, :, :]).then_inc(sem(f"ring_full{r}"), 16)
                n += NE * PER_EXPERT
                sp.wait_ge(sem("spill_known"), i + 1)
                spilt = sp.value_load(spill_info[0:1, 0:1], min_val=0, max_val=NG)
                group = sp.value_load(spill_info[0:1, 1:2], min_val=0, max_val=NG - 1)
                with sp.If(spilt > 0):
                    for s in range(per_body):
                        if s:
                            sp.wait_ge(sem(f"spill{i}_ring_free"), s)
                        sp.dma_start(spill_w, wmoe[i, bass.ds(group, 1), s, :, :]).then_inc(sem(f"spill{i}_ring_full"), 16)
            for l in range(DEPTH):
                at = 0
                for width in LOADS_SECOND:
                    load(wsecond[l, :, at:at + width], width)
                    at += width
            sp.wait_ge(sem("x_ready"), 2 * DEPTH + DEPTH)
            sp.dma_start(out, x_nat).then_inc(sem("out_stored"), 16)
            sp.wait_ge(sem("out_stored"), 16)

        @block.gpsimd
        def _(pool):
            pool.dma_start(cst, consts).then_inc(sem("cst_loaded"), 16)
            pool.dma_start(xT, x0T).then_inc(sem("xT_loaded"), 16)
            pool.dma_start(memT, memT0).then_inc(sem("memT_loaded"), 16)
            pool.dma_start(col, colp).then_inc(sem("par_loaded"), 16)
            pool.dma_start(sgw, sguT).then_inc(sem("par_loaded"), 16)
            pool.dma_start(rowa_sb, rowa[0, :].partition_broadcast(P)).then_inc(sem("par_loaded"), 16)
            pool.dma_start(rwt, rw).then_inc(sem("par_loaded"), 16)
            xg_flat, now_flat = xg.rearrange("p g k t -> p (g k t)"), xg_now.rearrange("p k t -> p (k t)")
            for n in range(2 * DEPTH):
                if n:
                    pool.wait_ge(sem("x_ready"), n)
                pool.dma_start(rows[:, 0:2 * D], lnrows[n, :].partition_broadcast(P)).then_inc(sem("rows_loaded"), 16)
                if n % 2 == 0:
                    with pool.Fori(0, NG) as j:
                        pool.wait_ge(sem("h_ready"), j * GS + (HSIGS * (n // 2) + 1))
                        pool.wait_ge(sem("silu_done"), j * GS + (HSIGS * (n // 2) + 1))
                        nc.gpsimd.tensor_copy(now_flat, xg_flat[:, bass.ds(j * (KD * P), KD * P)]).then_inc(sem("tokens_ready"), 1)
            for l in range(DEPTH):
                pool.wait_ge(sem("x_ready"), 2 * DEPTH + l)
                pool.dma_start(rows, rows2[l, :].partition_broadcast(P)).then_inc(sem("rows_loaded"), 16)
                pool.dma_start(lora_sb, lora[l, :, :]).then_inc(sem("lora_loaded"), 16)
                pool.dma_start(wff_sb, wff[l, :, :, :]).then_inc(sem("lora_loaded"), 16)

        @block.tensor
        def _(pe_eng):
            pe = TensorCounts()

            def mark(ins, full):
                if full is not None:
                    ins.then_inc(bank_full[full], 1)
                elif pe.pending:
                    pe.pending -= 1
                    ins.then_inc(sem("ring_free"), 1)

            def mm(o, lhsT, rhs, start=True, stop=True, full=None, loose=False):
                mark(nc.tensor.matmul(o, lhsT, rhs, start=start, stop=stop, skip_group_check=loose), full)

            def tr(o, i, full=None):
                mark(nc.tensor.transpose(o, i, ident), full)

            def slot(width=SLOT):
                pe.close()
                n = pe.slots
                pe.slots, pe.open = n + 1, True
                pe_eng.wait_ge(sem(f"ring_full{n % RING}"), 16 * (n // RING + 1))
                return ring[:, (n % RING) * SLOT:(n % RING) * SLOT + width]

            def transpose_tokens(src):
                for g, b in enumerate((0, 5, 1, 6)):
                    tt, half = g // 2, g % 2
                    pe_eng.wait_ge(bank_free[b], pe.reuse(b))
                    bank = banks[b]
                    for k in range(4):
                        tr(bank[:, k * P:(k + 1) * P], src[:, tt, (4 * half + k) * P:(4 * half + k + 1) * P],
                           full=b if k == 3 else None)
                pe_eng.wait_ge(bank_free[0], pe.used(0))
                pe_eng.wait_ge(bank_free[5], pe.used(5))
                pe_eng.wait_ge(bank_free[1], pe.used(1))
                pe_eng.wait_ge(bank_free[6], pe.used(6))

            def proj_T(w, rhsT, bs, tiles=4):
                for m in range(tiles):
                    b = bs[m // 2]
                    if m % 2 == 0:
                        pe_eng.wait_ge(bank_free[b], pe.reuse(b))
                        bank = banks[b]
                    for k in range(KD):
                        end = k == KD - 1 and (m % 2 == 1 or m == tiles - 1)
                        mm(bank[:, (m % 2) * T:(m % 2 + 1) * T], w[:, k, m * P:(m + 1) * P], rhsT[:, k, :],
                           start=k == 0, stop=k == KD - 1, full=b if end else None)

            def proj(w, lT, bs, n=512, kt=KD, at=0):
                for tt in range(TT):
                    pe_eng.wait_ge(bank_free[bs[tt]], pe.reuse(bs[tt]))
                    bank = banks[bs[tt]]
                    for k in range(kt):
                        mm(bank[:, 0:n], lT[:, k, tt * P:(tt + 1) * P], w[:, k, at:at + n], start=k == 0, stop=k == kt - 1,
                           full=bs[tt] if k == kt - 1 else None)

            def wslot():
                return v3(slot(), KD)

            pe_eng.wait_ge(sem("cst_loaded"), 16)
            pe_eng.wait_ge(sem("memT_loaded"), 16)
            pe_eng.wait_ge(sem("xT_loaded"), 16)
            for i in range(DEPTH):
                if i:
                    pe_eng.wait_ge(sem("x_ready"), pe.next("x_ready"))
                    transpose_tokens(x_nat)
                proj_T(wslot(), memT, (0, 5))
                proj(wslot(), memT, (1, 6))
                if i == 0:
                    proj_T(wslot(), xT, (5, 6))
                    proj(wslot(), xT, (7, 5))
                    proj_T(wslot(), xT, (2, 3))
                    pe_eng.wait_ge(sem("sgu_v_ready"), pe.next("sgu_v_ready"))
                    pe_eng.wait_ge(sem("sgu_w_ready"), pe.next("sgu_w_ready"))
                    for c in range(TT):
                        pe_eng.wait_ge(bank_free[c], pe.reuse(c))
                        bank = banks[c]
                        for h in range(4):
                            mm(bank[:, h * P:(h + 1) * P], vv[:, c, h * P:(h + 1) * P], sgw[:, h, :],
                               full=c if h == 3 else None)
                else:
                    proj_T(wslot(), xT, (5, 6))
                    proj_T(wslot(), xT, (7, 5))
                    proj_T(wslot(), xT, (0, 1))
                    proj_T(wslot(), xT, (2, 3))
                pe.close()
                pe_eng.wait_ge(bank_free[0], pe.used(0))
                pe_eng.wait_ge(bank_free[1], pe.used(1))
                pe_eng.wait_ge(bank_free[2], pe.used(2))
                pe_eng.wait_ge(bank_free[3], pe.used(3))
                pe_eng.wait_ge(bank_free[5], pe.used(5))
                pe_eng.wait_ge(bank_free[6], pe.used(6))
                for h in range(NHX):
                    pe_eng.wait_ge(bank_free[h], pe.reuse(h))
                    bank = banks[h]
                    for tt in range(TT):
                        mm(bank[:, tt * T:(tt + 1) * T], qT[:, h, tt * P:(tt + 1) * P], kT[:, h, :],
                           full=h if tt else None)
                for h in range(NHX):
                    pe_eng.wait_ge(sem("p_ready"), pe.next("p_ready"))
                    b = 5 + h % 3
                    pe_eng.wait_ge(bank_free[b], pe.reuse(b))
                    bank = banks[b]
                    for m in range(TT):
                        for tt in range(TT):
                            tr(bank[:, m * T + tt * P:m * T + (tt + 1) * P], xsc[:, h, tt, m * P:(m + 1) * P],
                               full=b if m and tt else None)
                    pe_eng.wait_ge(bank_free[b], pe.used(b))
                    pe_eng.wait_ge(bank_free[4], pe.reuse(4))
                    bank = banks[4]
                    for m in range(TT):
                        mm(bank[:, 0:T], vmem[:, m, h * P:(h + 1) * P], xPT[:, h, m, :], start=m == 0, stop=m == 1,
                           full=4 if m else None)
                pe_eng.wait_ge(bank_free[0], pe.used(0))
                pe_eng.wait_ge(bank_free[1], pe.used(1))
                pe_eng.wait_ge(bank_free[2], pe.used(2))
                pe_eng.wait_ge(bank_free[3], pe.used(3))
                pe_eng.wait_ge(bank_free[4], pe.used(4))
                pe_eng.wait_ge(sem("tok_ready"), pe.next("tok_ready"))
                for n in range(2):
                    proj(wslot(), catT, (n, 2 + n))
                pe.close()
                pe_eng.wait_ge(sem("x_ready"), pe.next("x_ready"))
                transpose_tokens(x_nat)
                if i == 0:
                    pe_eng.wait_ge(sem("par_loaded"), 64)
                pe_eng.wait_ge(bank_free[5], pe.reuse(5))
                bank = banks[5]
                for tt in range(TT):
                    for k in range(KD):
                        mm(bank[:, tt * NE:(tt + 1) * NE], xT[:, k, tt * P:(tt + 1) * P], rwt[:, k, :],
                           start=k == 0, stop=k == KD - 1, full=5 if tt and k == KD - 1 else None)
                pe_eng.wait_ge(sem("group_ready"), pe.next("group_ready"))
                pe_eng.wait_ge(bank_free[0], pe.reuse(0))
                bank = banks[0]
                chosen = [S_GRANK[:, tt * NG:(tt + 1) * NG] for tt in range(TT)]
                mm(bank[:, 0:NG], mat(C_TRI), chosen[0])
                for at, second in ((NG, C_TRI), (2 * NG, C_ONES)):
                    mm(bank[:, at:at + NG], mat(C_ONES), chosen[0], stop=False)
                    mm(bank[:, at:at + NG], mat(second), chosen[1], start=False, full=0 if at > NG else None)
                pe_eng.wait_ge(sem("slots_ready"), pe.next("slots_ready"))
                for k, b in enumerate((0, 5, 1, 6, 2, 7, 3, 5)):
                    pe_eng.wait_ge(bank_free[b], pe.reuse(b))
                    for tt in range(TT):
                        mm(banks[b][:, :], x_nat[:, tt, k * P:(k + 1) * P], pick[:, tt, :, :], start=tt == 0, stop=tt == 1,
                           full=b if tt else None)
                for tt in range(TT):
                    b = 6 + tt
                    pe_eng.wait_ge(bank_free[b], pe.reuse(b))
                    for g in range(NG):
                        tr(banks[b][:, g * P:(g + 1) * P], pick[:, tt, g, :], full=b if g == NG - 1 else None)
                pe_eng.wait_ge(sem("comb_ready"), pe.next("comb_ready"))
                pe_eng.wait_ge(bank_free[4], pe.reuse(4))
                for g in range(NG):
                    for tt in range(TT):
                        mm(banks[4][:, g * GS:(g + 1) * GS], pick[:, tt, g, :], S_C4[:, tt * GS:(tt + 1) * GS],
                           start=tt == 0, stop=tt == 1, full=4 if tt and g == NG - 1 else None)
                pe_eng.wait_ge(sem("spill_known"), i + 1)
                spilt = pe_eng.value_load(spill_info[0:1, 0:1], min_val=0, max_val=NG)
                for b in range(8):
                    pe_eng.wait_ge(bank_free[b], pe.used(b))
                base = pe.slots

                def group_products(kind, j, layer, slot_ready):
                    one = j * GS + (HSIGS * layer + 1)
                    turned = j * GS + NE * layer

                    def gate(e):
                        w = slot_ready(GROUP_SLOTS.index(("gate", e)), KD)
                        if e == 0:
                            pe_eng.wait_ge(sem(kind + "tokens_ready"), j + (NG * layer + 1))
                        pe_eng.wait_ge(sem(kind + "silu_done"), one + e)
                        for k in range(KD):
                            ins = nc.tensor.matmul(banks[5][:, :], xg_now[:, k, :], w[:, k, :], start=k == 0, stop=k == KD - 1)
                            if e == 1 and k == 0:
                                ins.then_inc(sem(kind + "ring_free"), 1)
                        ins.then_inc(sem(kind + "gate_full"), 1)

                    def up(e):
                        w = slot_ready(GROUP_SLOTS.index(("up", e)), KD)
                        pe_eng.wait_ge(sem(kind + "h_ready"), one + e)
                        for k in range(KD):
                            ins = nc.tensor.matmul(banks[4][:, :], xg_now[:, k, :], w[:, k, :], start=k == 0, stop=k == KD - 1)
                            if e == 0 and k == 0:
                                ins.then_inc(sem(kind + "ring_free"), 1)
                        ins.then_inc(sem(kind + "up_full"), 1)

                    def turn(e):
                        pe_eng.wait_ge(sem(kind + "h_ready"), one + (e + 1))
                        for k in range(KM):
                            ins = nc.tensor.transpose(banks[6][:, k * P:(k + 1) * P], hh[:, k * P:(k + 1) * P], ident)
                            if e < GS - 1 and k == 0:
                                ins.then_inc(sem(kind + "ring_free"), 1)
                        ins.then_inc(sem(kind + "hT_full"), 1)

                    def down(e, n):
                        if n == 0:
                            down.w = slot_ready(GROUP_SLOTS.index(("down", e)), KM)
                            pe_eng.wait_ge(sem(kind + "hT_ready"), turned + (e + 1))
                        if e == 0:
                            if n == 0:
                                pe_eng.wait_ge(sem(kind + "og0_ready"), j + (GSIGS * layer + 1))
                            else:
                                pe_eng.wait_ge(sem(kind + "og1_ready"), j + (GSIGS * layer + 1))
                        for k in range(KM):
                            ins = nc.tensor.matmul(banks[(7, 3)[n]][:, :], hT[:, e % 2, k, :], down.w[:, k, n * 512:(n + 1) * 512],
                                                   start=e == 0 and k == 0, stop=e == GS - 1 and k == KM - 1)
                            if n == 0 and k == 0 and e < GS - 1:
                                ins.then_inc(sem(kind + "ring_free"), 1)
                        if n == 1:
                            ins.then_inc(sem(kind + "ring_free"), 1)
                        elif e == GS - 1:
                            ins.then_inc(sem(kind + "down_full"), 1)

                    gate(0)
                    up(0)
                    for e in range(1, GS):
                        gate(e)
                        turn(e - 1)
                        up(e)
                        down(e - 1, 0)
                        if e == GS - 1:
                            turn(e)
                        down(e - 1, 1)
                    down(GS - 1, 0)
                    down(GS - 1, 1)

                with pe_eng.Fori(0, NG) as j:
                    def ring_slot(s, kt):
                        n = base + s
                        pe_eng.wait_ge(sem(f"ring_full{n % RING}"), j * (16 * per_body // RING) + 16 * (n // RING + 1))
                        return v3(ring[:, (n % RING) * SLOT:(n % RING + 1) * SLOT], kt)

                    group_products("", j, i, ring_slot)
                pe.slots += NE * PER_EXPERT

                with pe_eng.If(spilt > 0):
                    kind = f"spill{i}_"
                    pe_eng.wait_ge(sem(kind + "slots_ready"), 1)
                    for k in range(KD):
                        for tt in range(TT):
                            nc.tensor.matmul(banks[4 + k // 4][:, (k % 4) * P:(k % 4 + 1) * P], x_nat[:, tt, k * P:(k + 1) * P],
                                             pick[:, tt, 0, :], start=tt == 0, stop=tt == 1)
                    for tt in range(TT):
                        nc.tensor.matmul(banks[6][:, 0:GS], pick[:, tt, 0, :], S_C4[:, tt * GS:(tt + 1) * GS], start=tt == 0, stop=tt == 1)
                    for tt in range(TT):
                        ins = nc.tensor.transpose(banks[7][:, tt * P:(tt + 1) * P], pick[:, tt, 0, :], ident)
                    ins.then_inc(sem(kind + "gathered"), 1)
                    def spill_slot(s, kt):
                        pe_eng.wait_ge(sem(f"spill{i}_ring_full"), 16 * (s + 1))
                        return v3(spill_w, kt)

                    group_products(kind, 0, 0, spill_slot)
                    pe_eng.wait_ge(sem(kind + "og0_ready"), 2)
                    pe_eng.wait_ge(sem(kind + "og1_ready"), 2)

                pe_eng.wait_ge(sem("og0_ready"), GSIGS * (i + 1))
                pe_eng.wait_ge(sem("og1_ready"), GSIGS * (i + 1))
                for b in range(4):
                    pe_eng.wait_ge(bank_free[b], pe.reuse(b))
                    for g in range(NG - 1):
                        mm(banks[b][:, :], put[:, b // 2, g, :], og[:, g, (b % 2) * 512:(b % 2 + 1) * 512], start=g == 0, stop=False, loose=True)
                with pe_eng.If(spilt > 0):
                    for b in range(4):
                        nc.tensor.matmul(banks[b][:, :], put_spill[:, b // 2, :], og_spill[:, (b % 2) * 512:(b % 2 + 1) * 512],
                                         start=False, stop=False, skip_group_check=True)
                for b in range(4):
                    mm(banks[b][:, :], put[:, b // 2, NG - 1, :], og[:, NG - 1, (b % 2) * 512:(b % 2 + 1) * 512], start=False, full=b, loose=True)

            def turn_qk(kdim):
                pe_eng.wait_ge(sem("qk_ready"), pe.next("qk_ready"))
                for src, bs in ((qn, (0, 1, 5, 6)), (kn, (2, 3, 7, 5))):
                    for g in range(4):
                        tt, hg = g // 2, g % 2
                        pe_eng.wait_ge(bank_free[bs[g]], pe.reuse(bs[g]))
                        bank = banks[bs[g]]
                        for h in range(4):
                            tr(bank[0:kdim, h * P:(h + 1) * P], src[:, tt, hg * 4 + h, 0:kdim], full=bs[g] if h == 3 else None)
                pe_eng.wait_ge(bank_free[0], pe.used(0))
                pe_eng.wait_ge(bank_free[1], pe.used(1))
                pe_eng.wait_ge(bank_free[2], pe.used(2))
                pe_eng.wait_ge(bank_free[3], pe.used(3))
                pe_eng.wait_ge(bank_free[5], pe.used(5))
                pe_eng.wait_ge(bank_free[6], pe.used(6))
                pe_eng.wait_ge(bank_free[7], pe.used(7))

            def scores(kdim):
                for h in range(NH):
                    b = h % NDB
                    pe_eng.wait_ge(bank_free[b], pe.reuse(b))
                    bank = banks[b]
                    mm(bank[:, 0:P], qTt[0:kdim, h, 0:P], kTt[0:kdim, h, 0:P])
                    mm(bank[:, P:3 * P], qTt[0:kdim, h, P:T], kTt[0:kdim, h, :], full=b)

            def apply(vn):
                for h in range(NH):
                    if h % 4 == 0:
                        pe_eng.wait_ge(sem("p_ready"), pe.next("p_ready"))
                    b = 5 + h % 2
                    pe_eng.wait_ge(bank_free[b], pe.reuse(b))
                    bank = banks[b]
                    for t in range(3):
                        tr(bank[:, t * P:(t + 1) * P], Pm[:, h, t * P:(t + 1) * P], full=b if t == 2 else None)
                    pe_eng.wait_ge(bank_free[b], pe.used(b))
                    ob = h // 2
                    if h % 2 == 0:
                        pe_eng.wait_ge(bank_free[ob], pe.reuse(ob))
                    o = banks[ob][HC * (h % 2):HC * (h % 2) + HC, :]
                    mm(o[:, 0:T], vn[:, 0, h, :], PT[:, h % 2, 0:T], stop=False, loose=True)
                    mm(o[:, P:T], vn[:, 1, h, :], PT[:, h % 2, T:T + P], start=False, full=ob if h % 2 else None, loose=True)

            def merge_values():
                w = v3(slot(), KM)
                pe_eng.wait_ge(bank_free[0], pe.used(0))
                pe_eng.wait_ge(bank_free[1], pe.used(1))
                pe_eng.wait_ge(bank_free[2], pe.used(2))
                pe_eng.wait_ge(bank_free[3], pe.used(3))
                for n in range(2):
                    proj(w, oT, (n, 2 + n), kt=KM, at=n * 512)

            def merge_gates():
                for n in range(2):
                    proj(wslot(), xT, (5, 6))

            for l in range(DEPTH):
                pe_eng.wait_ge(sem("h_ready2"), pe.next("h_ready2"))
                transpose_tokens(y_nat)
                pe_eng.wait_ge(sem("lora_loaded"), 32 * (l + 1))
                proj(v3(slot(KD * LAT), KD), xT, (0, 1), n=LAT)
                pe_eng.wait_ge(bank_free[4], pe.reuse(4))
                bank = banks[4]
                for tt in range(TT):
                    for k in range(KD):
                        mm(bank[:, tt * NH:(tt + 1) * NH], xT[:, k, tt * P:(tt + 1) * P], wff_sb[:, k, :],
                           start=k == 0, stop=k == KD - 1, full=4 if tt and k == KD - 1 else None)
                proj_T(wslot(), xT, (5, 6))
                pe_eng.wait_ge(sem("lat_ready"), pe.next("lat_ready"))
                for b, at, n in ((2, 0, 2), (3, 2, 1)):
                    pe_eng.wait_ge(bank_free[b], pe.reuse(b))
                    bank = banks[b]
                    for k in range(n):
                        for tt in range(TT):
                            tr(bank[:, k * T + tt * P:k * T + (tt + 1) * P], cnat[:, tt, (at + k) * P:(at + k + 1) * P],
                               full=b if tt and k == n - 1 else None)
                pe_eng.wait_ge(bank_free[2], pe.used(2))
                pe_eng.wait_ge(bank_free[3], pe.used(3))
                w = v3(slot(1536), 2)
                for n in range(2):
                    for tt in range(TT):
                        b = 2 * n + tt
                        pe_eng.wait_ge(bank_free[b], pe.reuse(b))
                        bank = banks[b]
                        for k in range(2):
                            mm(bank[:, 0:4 * QK], cT[:, k, tt * P:(tt + 1) * P], w[:, k, n * 4 * QK:(n + 1) * 4 * QK],
                               start=k == 0, stop=k == 1, full=b if k else None)
                w = slot(1024)
                for n in range(2):
                    for tt in range(TT):
                        b = 5 + (2 * n + tt) % 3
                        pe_eng.wait_ge(bank_free[b], pe.reuse(b))
                        bank = banks[b]
                        mm(bank[:, 0:256], cT[:, 2, tt * P:(tt + 1) * P], w[:, n * 512:n * 512 + 256])
                        mm(bank[:, 256:512], cT[:, 2, tt * P:(tt + 1) * P], w[:, n * 512 + 256:(n + 1) * 512], full=b)
                proj_T(wslot(), xT, (5, 6))
                proj_T(wslot(), xT, (5, 6))
                turn_qk(QK)
                scores(QK)
                pe_eng.wait_ge(sem("logf_ready"), pe.next("logf_ready"))
                lf = ffn[:, 0:TT * NH]
                pe_eng.wait_ge(bank_free[4], pe.reuse(4))
                bank = banks[4]
                mm(bank[:, 0:NH], mat(C_TRI), lf[:, 0:NH])
                mm(bank[:, NH:2 * NH], mat(C_ONES), lf[:, 0:NH], stop=False)
                mm(bank[:, NH:2 * NH], mat(C_TRI), lf[:, NH:2 * NH], start=False, full=4)
                proj(wslot(), xT, (0, 1))
                proj(wslot(), xT, (2, 3))
                proj(wslot(), xT, (5, 6))
                proj_T(wslot(), xT, (5, 6))
                apply(vn2[0])
                proj_T(wslot(), xT, (5, 6))
                proj_T(v3(slot(KD * P), KD), xT, (7,), tiles=1)
                turn_qk(FOXK)
                scores(FOXK)
                merge_values()
                merge_gates()
                apply(vn2[1])
                proj_T(wslot(), xT, (5, 6))
                merge_values()
                merge_gates()

                pe_eng.wait_ge(sem("shift_ready"), pe.next("shift_ready"))
                if l:
                    pe_eng.wait_ge(bank_free[4], pe.reuse(4))
                    bank = banks[4]
                    for k in range(4):
                        mm(bank[0:32, 0:T], vdown[:, k, :], vlT[:, k, :], start=k == 0, stop=k == 3, full=4 if k == 3 else None)
                    pe_eng.wait_ge(bank_free[4], pe.used(4))
                    for g in range(2):
                        pe_eng.wait_ge(bank_free[g], pe.reuse(g))
                        bank = banks[g]
                        for j in range(2):
                            mm(bank[:, j * T:(j + 1) * T], vup[0:32, (2 * g + j) * P:(2 * g + j + 1) * P], v_mid,
                               full=g if j else None)
                for tt in range(TT):
                    tok = slice(tt * P, (tt + 1) * P)
                    pe_eng.wait_ge(sem("tw_ready"), pe.next("tw_ready"))
                    pe_eng.wait_ge(bank_free[0], pe.reuse(0))
                    bank = banks[0]
                    for j in range(4):
                        mm(bank[:, j * P:(j + 1) * P], wup[0:64, j * P:(j + 1) * P], tw[0:64, :], full=0 if j == 3 else None)
                    pe_eng.wait_ge(bank_free[1], pe.reuse(1))
                    bank = banks[1]
                    for j in range(4):
                        mm(bank[:, j * P:(j + 1) * P], wup[64:128, j * P:(j + 1) * P], sh[64:128, 12, tok], full=1 if j == 3 else None)
                    pe_eng.wait_ge(sem("ksq_ready"), pe.next("ksq_ready"))
                    pe_eng.wait_ge(bank_free[2], pe.reuse(2))
                    bank = banks[2]
                    mm(bank[:, :], mat(C_BLOCK), flat2(t1), full=2)
                    pe_eng.wait_ge(sem("rows_ready"), pe.next("rows_ready"))
                    for par in range(2):
                        hs = slice(64 * par, 64 * par + 64)
                        for b, left, right in ((0, aa, pex), (1, pinv, pex), (2, pinv, pp), (3, aa, pp)):
                            pe_eng.wait_ge(bank_free[b], pe.reuse(b))
                            bank = banks[b]
                            for j in range(4):
                                mm(bank[:, j * P:(j + 1) * P], left[hs, j, :], right[hs, j, :], full=b if j == 3 else None)
                    pe_eng.wait_ge(bank_free[4], pe.reuse(4))
                    bank = banks[4]
                    for j in range(4):
                        mm(bank[:, 0:NH], rk[:, j, :], cst[:, C_SEL + j * NH:C_SEL + (j + 1) * NH], start=j == 0, stop=j == 3)
                    for par in range(2):
                        mm(bank[0:64, 64 + 8 * par:72 + 8 * par], mat(C_ID)[:, 64 * par:64 * par + 64], pcs, full=4 if par else None)
                    for b, src in ((5, vlT[:, :, tok]), (6, pex), (7, pp), (5, cum), (3, lw)):
                        pe_eng.wait_ge(bank_free[b], pe.reuse(b))
                        bank = banks[b]
                        for j in range(4):
                            tr(bank[:, j * P:(j + 1) * P], src[:, j, :], full=b if j == 3 else None)
                    for par in range(2):
                        pe_eng.wait_ge(sem("level_ready"), pe.next("level_ready"))
                        pe_eng.wait_ge(bank_free[par], pe.reuse(par))
                        bank = banks[par]
                        for j in range(4):
                            tr(bank[:, j * P:(j + 1) * P], TTm[:, par, j, :], full=par if j == 3 else None)
                    for lev in range(1, LEVELS):
                        for par in range(2):
                            pe_eng.wait_ge(sem("level_ready"), pe.next("level_ready"))
                            b = 5 + par
                            pe_eng.wait_ge(bank_free[b], pe.reuse(b))
                            bank = banks[b]
                            for j in range(4):
                                mm(bank[:, j * P:(j + 1) * P], Nl[:, par, j, :], Tm[:, par, j, :], full=b if j == 3 else None)
                        for par in range(2):
                            pe_eng.wait_ge(bank_free[5 + par], pe.used(5 + par))
                            if lev < LEVELS - 1:
                                pe_eng.wait_ge(bank_free[2 * par], pe.reuse(2 * par))
                                bank = banks[2 * par]
                                for j in range(4):
                                    mm(bank[:, j * P:(j + 1) * P], TTm[:, par, j, :], Xm[:, par, j, :], full=2 * par if j == 3 else None)
                            pe_eng.wait_ge(bank_free[2 * par + 1], pe.reuse(2 * par + 1))
                            bank = banks[2 * par + 1]
                            for j in range(4):
                                mm(bank[:, j * P:(j + 1) * P], Xm[:, par, j, :], TTm[:, par, j, :], full=2 * par + 1 if j == 3 else None)
                    pe_eng.wait_ge(bank_free[1], pe.used(1))
                    pe_eng.wait_ge(bank_free[3], pe.used(3))
                    pe_eng.wait_ge(bank_free[5], pe.used(5))
                    pe_eng.wait_ge(bank_free[6], pe.used(6))
                    pe_eng.wait_ge(bank_free[7], pe.used(7))
                    pe_eng.wait_ge(bank_free[2], pe.reuse(2))
                    bank = banks[2]
                    for h in range(NH):
                        mm(hc(bank, h), TTm[:, h % 2, h // 2, :], hc(Kn, h), full=2 if h == NH - 1 else None)
                    pe_eng.wait_ge(bank_free[3], pe.reuse(3))
                    bank = banks[3]
                    for h in range(NH):
                        mm(hc(bank, h), MTm[:, h % 2, h // 2, :], hc(Vn, h), full=3 if h == NH - 1 else None)
                    pe_eng.wait_ge(bank_free[3], pe.used(3))
                    pe_eng.wait_ge(bank_free[4], pe.reuse(4))
                    bank = banks[4]
                    for h in range(NH):
                        mm(hc(bank, h), TTm[:, h % 2, h // 2, :], hc(mv, h), full=4 if h == NH - 1 else None)
                    pe_eng.wait_ge(bank_free[2], pe.used(2))
                    pe_eng.wait_ge(bank_free[4], pe.used(4))
                    chunks = (0, 1) if tt == 0 else (0,)
                    for c in chunks:
                        rowsc = slice(64 * c, 64 * c + 64)
                        if 2 * tt + c:
                            pe_eng.wait_ge(bank_free[c], pe.reuse(c))
                            bank = banks[c]
                            for h in range(NH):
                                mm(hc(bank[0:64, :], h), hc(Wn[rowsc, :], h), hc(Bn[rowsc, :], h), full=c if h == NH - 1 else None)
                        pe_eng.wait_ge(bank_free[2 + c], pe.reuse(2 + c))
                        bank = banks[2 + c]
                        for h in range(NH):
                            mm(hc(bank[0:64, :], h), hc(Kp[rowsc, :], h), hc(Vn[rowsc, :], h), stop=False)
                            mm(hc(bank[0:64, :], h), hc(Bn[rowsc, :], h), hc(uv[rowsc, :], h), start=False, full=2 + c if h == NH - 1 else None)
                    for par in range(2):
                        b = 5 + par
                        pe_eng.wait_ge(bank_free[b], pe.reuse(b))
                        bank = banks[b]
                        for j in range(4):
                            h = 2 * j + par
                            mm(bank[0:64, j * P:(j + 1) * P], hc(Rn, h), ident, stop=False)
                            mm(bank[0:64, j * P:(j + 1) * P], hc(Wn, h), AbT[:, par, j, :], start=False, full=b if j == 3 else None)
                    for c in chunks:
                        g = 2 * tt + c
                        if g == 0:
                            continue
                        pe_eng.wait_ge(bank_free[c], pe.used(c))
                        pe_eng.wait_ge(bank_free[2], pe.used(2))
                        pe_eng.wait_ge(bank_free[3], pe.used(3))
                        pe_eng.wait_ge(bank_free[4], pe.used(4))
                        pe_eng.wait_ge(bank_free[4], pe.reuse(4))
                        bank = banks[4]
                        for h in range(NH):
                            mm(hc(bank[0:64, :], h), GT[0:64, c, h, :], hc(states[g - 1][0:64, :], h), full=4 if h == NH - 1 else None)
                    pe_eng.wait_ge(bank_free[5], pe.used(5))
                    pe_eng.wait_ge(bank_free[6], pe.used(6))
                    pe_eng.wait_ge(bank_free[4], pe.reuse(4))
                    bank = banks[4]
                    for h in range(NH):
                        par, j = h % 2, h // 2
                        o = hc(bank, h)
                        mm(o, AkT[:, par, j, :], hc(Vn, h), stop=False, loose=True)
                        mm(o, AbT[:, par, j, :], hc(uv, h), start=False, stop=False, loose=True)
                        for c in range(2):
                            g = 2 * tt + c
                            if g:
                                mm(o[64 * c:64 * c + 64, :], QT[0:64, par, j, c * CH:(c + 1) * CH], hc(states[g - 1][0:64, :], h),
                                   start=False, full=4 if h == NH - 1 and c else None, loose=True)
                    pe_eng.wait_ge(sem("y_ready"), pe.next("y_ready"))
                    pe_eng.wait_ge(bank_free[0], pe.reuse(0))
                    bank = banks[0]
                    for j in range(4):
                        tr(bank[:, j * P:(j + 1) * P], yv[:, j * P:(j + 1) * P], full=0 if j == 3 else None)
                merge_values()
                merge_gates()
                pe_eng.wait_ge(sem("merged_ready"), pe.next("merged_ready"))
                transpose_tokens(merged)
                for n in range(2):
                    proj(wslot(), xT, (n, 2 + n))
                pe.close()

        @block.scalar
        def _(act_eng):
            act = Counts()
            act.shifts = 0

            def copy_out(o, b, bank_ap, func=ACT.Copy):
                act_eng.wait_ge(bank_full[b], act.next(("full", b)))
                nc.scalar.activation(o, bank_ap, func).then_inc(bank_free[b], act.sends(bank_free[b]))

            def roots(n):
                act_eng.wait_ge(sem("var_ready"), act.next("var_ready"))
                nc.scalar.activation(S_VAR[:, 0:n], S_VAR[:, 0:n], ACT.Sqrt).then_inc(sem("std_ready"), act.sends(sem("std_ready")))

            def turned_x():
                for g, b in ((1, 5), (3, 6)):
                    copy_out(xT[:, 4:8, (g // 2) * P:(g // 2 + 1) * P], b, v3(banks[b][:, :], 4))

            def two_tiles(dst, b, m, func=ACT.Copy):
                copy_out(dst[:, 2 * m:2 * m + 2, :], b, v3(banks[b][:, :], 2), func)

            for i in range(DEPTH):
                if i:
                    turned_x()
                two_tiles(kT, 5, 1)
                copy_out(vmem[:, 1, :], 6, banks[6][:, :])
                if i == 0:
                    two_tiles(uT, 5, 0, ACT.Gelu)
                    two_tiles(uT, 6, 1, ACT.Gelu)
                    copy_out(vv[:, 0, :], 7, banks[7][:, :], ACT.Gelu)
                    act_eng.wait_ge(bank_full[5], act.next(("full", 5)))
                    nc.scalar.activation(vv[:, 1, :], banks[5][:, :], ACT.Gelu).then_inc(bank_free[5], act.sends(bank_free[5]))
                    act_eng.wait_ge(act.last, act.value)
                    nc.scalar.activation(S_MARK[:, 0:1], vv[:, 1, 0:1], ACT.Copy).then_inc(sem("gelu_done"), act.sends(sem("gelu_done")))
                    roots(2)
                else:
                    two_tiles(bgT, 5, 0)
                    two_tiles(bgT, 6, 1)
                    two_tiles(cgT, 7, 0)
                    two_tiles(cgT, 5, 1)
                    act_eng.wait_ge(act.last, act.value)
                    nc.scalar.activation(S_MARK[:, 0:1], cgT[:, 3, 0:1], ACT.Copy).then_inc(sem("gelu_done"), act.sends(sem("gelu_done")))
                for h in range(NHX):
                    act_eng.wait_ge(sem("max_ready"), act.next("max_ready"))
                    for tt in range(TT):
                        ins = nc.scalar.activation(xsc[:, h, tt, :], xsc[:, h, tt, :], ACT.Exp, bias=S_NM[:, h * TT + tt:h * TT + tt + 1],
                                                   scale=XSCALE, accum_out=S_SUM[:, h * TT + tt:h * TT + tt + 1])
                    ins.then_inc(sem("exp_done"), act.sends(sem("exp_done")))
                for h in range(NHX):
                    b = 5 + h % 3
                    copy_out(xPT[:, h, :, :], b, v3(banks[b][:, :], 2))
                roots(2)
                turned_x()
                act_eng.wait_ge(bank_full[5], act.next(("full", 5)))
                nc.scalar.activation(S_SC, banks[5][:, 0:TT * NE], ACT.Sigmoid).then_inc(bank_free[5], act.sends(bank_free[5]))
                act_eng.wait_ge(act.last, act.value)
                nc.scalar.activation(S_MARK[:, 1:2], S_SC[:, 0:1], ACT.Copy).then_inc(sem("scores_ready"), act.sends(sem("scores_ready")))
                for k, b in ((1, 5), (3, 6), (5, 7), (7, 5)):
                    copy_out(xg[:, :, k, :], b, v3(banks[b][:, :], NG))
                for tt in range(TT):
                    copy_out(put[:, tt, :, :], 6 + tt, v3(banks[6 + tt][:, :], NG))
                act_eng.wait_ge(sem("spill_known"), i + 1)
                spilt = act_eng.value_load(spill_info[0:1, 0:1], min_val=0, max_val=NG)
                nc.scalar.activation(S_MARK[:, 2:3], S_SC[:, 0:1], ACT.Silu).then_inc(sem("silu_done"), 1)
                nc.scalar.activation(S_MARK[:, 3:4], S_SC[:, 0:1], ACT.Copy).then_inc(sem("og0_ready"), 1)

                def group_gates(kind, j, layer, sums):
                    before = j * GS + NE * layer

                    def silu(e):
                        act_eng.wait_ge(sem(kind + "gate_full"), before + (e + 1))
                        act_eng.wait_ge(sem(kind + "h_ready"), before + (layer + 1 + e))
                        nc.scalar.activation(sg, banks[5][:, :], ACT.Silu).then_inc(sem(kind + "silu_done"), 1)

                    def turned(e):
                        act_eng.wait_ge(sem(kind + "hT_full"), before + (e + 1))
                        nc.scalar.activation(hT[:, e % 2, :, :], v3(banks[6][:, :], KM), ACT.Copy).then_inc(sem(kind + "hT_ready"), 1)

                    silu(0)
                    for e in range(1, GS):
                        silu(e)
                        turned(e - 1)
                    turned(GS - 1)
                    act_eng.wait_ge(sem(kind + "down_full"), j + (NG * layer + 1))
                    nc.scalar.activation(sums, banks[7][:, :], ACT.Copy).then_inc(sem(kind + "og0_ready"), 1)

                og_flat = flat2(og)
                with act_eng.Fori(0, NG) as j:
                    group_gates("", j, i, og_flat[:, bass.ds(j * D, 512)])
                with act_eng.If(spilt > 0):
                    kind = f"spill{i}_"
                    act_eng.wait_ge(sem(kind + "gathered"), 1)
                    for half in range(2):
                        nc.scalar.activation(xg_now[:, 4 * half:4 * half + 4, :], v3(banks[4 + half][:, :], 4), ACT.Copy).then_inc(sem(kind + "copied"), 1)
                    nc.scalar.activation(S_CGS, banks[6][:, 0:GS], ACT.Copy).then_inc(sem(kind + "copied"), 1)
                    nc.scalar.activation(S_MARK[:, 2:3], S_SC[:, 0:1], ACT.Silu).then_inc(sem(kind + "silu_done"), 1)
                    nc.scalar.activation(S_MARK[:, 3:4], S_SC[:, 0:1], ACT.Copy).then_inc(sem(kind + "og0_ready"), 1)
                    nc.scalar.activation(put_spill, v3(banks[7][:, 0:T], TT), ACT.Copy).then_inc(sem(kind + "tokens_ready"), 1)
                    group_gates(kind, 0, 0, og_spill[:, 0:512])
                roots(2)

            def shifted_in(n):
                for m in range(2):
                    act_shift(5 + m, 2)

            def act_shift(b, tiles):
                if act.shifts:
                    act_eng.wait_ge(sem("shift_done"), act.next("shift_done"))
                act.shifts += 1
                act_eng.wait_ge(bank_full[b], act.next(("full", b)))
                nc.scalar.activation(pcol[:, 0:tiles, 1:T + 1], v3(banks[b][:, 0:tiles * T], tiles), ACT.Copy).then_inc(bank_free[b], act.sends(bank_free[b]))
                act_eng.wait_ge(act.last, act.value)
                nc.scalar.activation(S_MARK[:, 0:1], pcol[:, tiles - 1, T:T + 1], ACT.Copy).then_inc(sem("shift_in"), act.sends(sem("shift_in")))

            def silu_gate(g):
                for m in range(2):
                    two_tiles(gates[:, g, :, :], 5 + m, m, ACT.Silu)

            def turned_qk(kdim):
                for dst, g, b in ((qTt, 2, 5), (qTt, 3, 6), (kTt, 2, 7), (kTt, 3, 5)):
                    hg = g % 2
                    copy_out(dst[0:kdim, 4 * hg:4 * hg + 4, P:T], b, v3(banks[b][0:kdim, :], 4))

            def softmax():
                for half in range(2):
                    act_eng.wait_ge(sem("max_ready"), act.next("max_ready"))
                    for h in range(4):
                        for tt in range(TT):
                            at = half * 8 + tt * 4 + h
                            span = Pm[:, half * 4 + h, 0:P] if tt == 0 else Pm[:, half * 4 + h, P:3 * P]
                            ins = nc.scalar.activation(span, span, ACT.Exp, bias=S_NM[:, at:at + 1], accum_out=S_SUM[:, at:at + 1])
                    ins.then_inc(sem("exp_done"), act.sends(sem("exp_done")))

            def turned_p():
                for h in range(NH):
                    b = 5 + h % 2
                    copy_out(PT[:, h % 2, :], b, banks[b][:, 0:3 * P])

            def merge_sigmoid():
                for n in range(2):
                    for tt in range(TT):
                        copy_out(sgm[:, tt, n * 512:(n + 1) * 512], 5 + tt, banks[5 + tt][:, :], ACT.Sigmoid)
                act_eng.wait_ge(act.last, act.value)
                nc.scalar.activation(S_MARK[:, 0:1], sgm[:, 1, D - 1:D], ACT.Copy).then_inc(sem("sgm_ready"), act.sends(sem("sgm_ready")))

            for l in range(DEPTH):
                roots(2)
                turned_x()
                silu_gate(0)
                roots(6)
                act_eng.wait_ge(sem("gates_neg"), act.next("gates_neg"))
                lfe = ffn[:, TT * NH:2 * TT * NH]
                nc.scalar.activation(lfe, lfe, ACT.Exp).then_inc(act_step, act.sends(act_step))
                act_eng.wait_ge(act.last, act.value)
                nc.scalar.activation(lfe, lfe, ACT.Ln, bias=1.0).then_inc(sem("gates_ln"), act.sends(sem("gates_ln")))
                for n in range(2):
                    for tt in range(TT):
                        b = 5 + (2 * n + tt) % 3
                        act_eng.wait_ge(bank_full[b], act.next(("full", b)))
                        kv = v3(banks[b][:, :], 4)
                        nc.scalar.activation(kn[:, tt, 4 * n:4 * n + 4, 0:NOPE], kv[:, :, 0:NOPE], ACT.Copy).then_inc(act_step, act.sends(act_step))
                        nc.scalar.activation(vn2[0][:, tt, 4 * n:4 * n + 4, :], kv[:, :, NOPE:P], ACT.Copy).then_inc(bank_free[b], act.sends(bank_free[b]))
                act_eng.wait_ge(act.last, act.value)
                nc.scalar.activation(S_MARK[:, 0:1], vn2[0][:, 1, 7, 0:1], ACT.Copy).then_inc(sem("kv_ready"), act.sends(sem("kv_ready")))
                roots(32)
                shifted_in(0)
                shifted_in(1)
                turned_qk(QK)
                softmax()
                for tt in range(TT):
                    copy_out(vn2[1][:, tt, :, :], 5 + tt, v3(banks[5 + tt][:, :], NH))
                silu_gate(1)
                roots(32)
                turned_p()
                shifted_in(2)
                act_shift(7, 1)
                turned_qk(FOXK)
                softmax()
                merge_sigmoid()
                turned_p()
                silu_gate(0)
                merge_sigmoid()
                if l:
                    act_eng.wait_ge(sem("nu_in"), act.next("nu_in"))
                    nc.scalar.activation(nuT, nuT, ACT.Sigmoid).then_inc(sem("nu_ready"), act.sends(sem("nu_ready")))
                for tt in range(TT):
                    tok = slice(tt * P, (tt + 1) * P)
                    act_eng.wait_ge(sem("shift_all"), act.next("shift_all"))
                    nc.scalar.activation(tw[0:64, :], sh[0:64, 12, tok], ACT.Tanh).then_inc(sem("tw_ready"), act.sends(sem("tw_ready")))
                    act_eng.wait_ge(sem("wa_in"), act.next("wa_in"))
                    nc.scalar.activation(flat2(lw), flat2(lw), ACT.Sigmoid).then_inc(act_step, act.sends(act_step))
                    nc.scalar.activation(flat2(aa), flat2(aa), ACT.Sigmoid).then_inc(sem("wa_ready"), act.sends(sem("wa_ready")))
                    act_eng.wait_ge(sem("ksum_ready"), act.next("ksum_ready"))
                    nc.scalar.activation(flat2(t1), flat2(t1), ACT.Sqrt).then_inc(sem("knorm_ready"), act.sends(sem("knorm_ready")))
                    act_eng.wait_ge(sem("cum_ready"), act.next("cum_ready"))
                    nc.scalar.activation(flat2(pp), flat2(cum), ACT.Exp).then_inc(act_step, act.sends(act_step))
                    nc.scalar.activation(flat2(pinv), flat2(cum), ACT.Exp, scale=-1.0).then_inc(act_step, act.sends(act_step))
                    nc.scalar.activation(flat2(pex), flat2(pex), ACT.Exp).then_inc(sem("decay_ready"), act.sends(sem("decay_ready")))
                    for b, dst in ((5, Vn), (6, Kn), (7, Rn), (5, Bn)):
                        copy_out(dst, b, banks[b][:, :])
                    for lev in range(1, LEVELS):
                        for par in range(2):
                            copy_out(Xm[:, par, :, :], 5 + par, v3(banks[5 + par][:, :], 4))
                    for par in range(2):
                        copy_out(QT[0:64, par, :, :], 5 + par, v3(banks[5 + par][0:64, :], 4))
                    roots(8)
                merge_sigmoid()
                turned_x()

        @block.vector
        def _(dve_eng):
            dve = Counts()
            v = nc.vector
            for b in range(8):
                v.memset(banks[b][:, 0:1], 0.0).then_inc(bank_free[b], 1)

            def copy_out(o, b, bank_ap):
                dve_eng.wait_ge(bank_full[b], dve.next(("full", b)))
                v.tensor_copy(o, bank_ap).then_inc(bank_free[b], dve.sends(bank_free[b]))

            def turned_x():
                for g, b in ((0, 0), (2, 1)):
                    copy_out(xT[:, 0:4, (g // 2) * P:(g // 2 + 1) * P], b, v3(banks[b][:, :], 4))

            def roots(n):
                dve_eng.wait_ge(sem("std_ready"), dve.next("std_ready"))
                v.reciprocal(S_RSTD[:, 0:n], S_VAR[:, 0:n]).then_inc(dve_step, dve.sends(dve_step))
                dve_eng.wait_ge(dve.last, dve.value)

            def mean_var(src):
                n = src.shape[2] // 512
                for tt in range(TT):
                    for s in range(n):
                        v.bn_stats(S_BN[:, (tt * n + s) * 6:(tt * n + s + 1) * 6], src[:, tt, s * 512:(s + 1) * 512]).then_inc(dve_step, dve.sends(dve_step))
                dve_eng.wait_ge(dve.last, dve.value)
                for tt in range(TT):
                    v.bn_aggr(S_MV[:, 2 * tt:2 * tt + 2], S_BN[:, tt * n * 6:(tt + 1) * n * 6]).then_inc(dve_step, dve.sends(dve_step))
                dve_eng.wait_ge(dve.last, dve.value)
                v.tensor_scalar(S_VAR[:, 0:TT], S_MV[:, 1:4:2], LN_EPS, None, ADD).then_inc(sem("var_ready"), dve.sends(sem("var_ready")))
                roots(TT)

            def layer_norm(src, dst, g, b, end):
                mean_var(src)
                for tt in range(TT):
                    v.tensor_scalar(dst[:, tt, :], src[:, tt, :], S_MV[:, 2 * tt:2 * tt + 1], S_RSTD[:, tt:tt + 1], SUB, MUL).then_inc(dve_step, dve.sends(dve_step))
                n = dst.shape[2]
                dve_eng.wait_ge(dve.last, dve.value)
                v.tensor_tensor(dst, dst, per_column(g, TT), MUL).then_inc(dve_step, dve.sends(dve_step))
                dve_eng.wait_ge(dve.last, dve.value)
                v.tensor_tensor(dst, dst, per_column(b, TT), ADD).then_inc(sem(end), dve.sends(sem(end)))

            def two_tiles(dst, b, m):
                copy_out(dst[:, 2 * m:2 * m + 2, :], b, v3(banks[b][:, :], 2))

            dve_eng.wait_ge(sem("cst_loaded"), 16)
            dve_eng.wait_ge(sem("par_loaded"), 64)
            v.tensor_tensor(sgw, sgw, mat4(C_SGU), MUL).then_inc(dve_step, dve.sends(dve_step))
            dve_eng.wait_ge(dve.last, dve.value)
            v.tensor_copy(S_BIG[:, 0:1], sgw[:, 0, 0:1]).then_inc(sem("sgu_w_ready"), dve.sends(sem("sgu_w_ready")))
            for i in range(DEPTH):
                if i:
                    turned_x()
                two_tiles(kT, 0, 0)
                copy_out(vmem[:, 0, :], 1, banks[1][:, :])
                if i == 0:
                    for m in range(2):
                        two_tiles(qT, 2 + m, m)
                    dve_eng.wait_ge(sem("gelu_done"), dve.next("gelu_done"))
                    layer_norm(vv, vv, rowa_sb[:, R_SGUG:R_SGUG + MIX], rowa_sb[:, R_SGUB:R_SGUB + MIX], "sgu_v_ready")
                    for c in range(TT):
                        dve_eng.wait_ge(bank_full[c], dve.next(("full", c)))
                        t = tmpT[:, :, c * P:(c + 1) * P]
                        v.tensor_tensor(t, v3(banks[c][:, :], 4), v3(rowa_sb[:, R_SGUBIAS:R_SGUBIAS + 512], 4), ADD).then_inc(bank_free[c], dve.sends(bank_free[c]))
                    dve_eng.wait_ge(dve.last, dve.value)
                    v.tensor_tensor(catT[:, 0:4, :], uT, tmpT, MUL).then_inc(sem("tok_ready"), dve.sends(sem("tok_ready")))
                else:
                    v.memset(hpad[:, :, 0:2], 0.0).then_inc(dve_step, dve.sends(dve_step))
                    dve_eng.wait_ge(dve.last, dve.value)
                    dve_eng.wait_ge(sem("gelu_done"), dve.next("gelu_done"))
                    for m in range(2):
                        dve_eng.wait_ge(bank_full[m], dve.next(("full", m)))
                        v.tensor_tensor(hpad[:, 2 * m:2 * m + 2, 2:], cgT[:, 2 * m:2 * m + 2, :], v3(banks[m][:, :], 2), MUL).then_inc(bank_free[m], dve.sends(bank_free[m]))
                    for m in range(2):
                        two_tiles(qT, 2 + m, m)
                    dve_eng.wait_ge(dve.last, dve.value)
                    for k in range(4):
                        cw = col[:, 3 * k:3 * k + 3]
                        v.tensor_scalar(tmpT[:, k, :], hpad[:, k, 0:T], cw[:, 0:1], None, MUL).then_inc(dve_step, dve.sends(dve_step))
                    for tap in range(1, 3):
                        dve_eng.wait_ge(dve.last, dve.value)
                        for k in range(4):
                            v.scalar_tensor_tensor(tmpT[:, k, :], hpad[:, k, tap:tap + T], col[:, 3 * k + tap:3 * k + tap + 1],
                                                      tmpT[:, k, :], MUL, ADD).then_inc(dve_step, dve.sends(dve_step))
                    dve_eng.wait_ge(dve.last, dve.value)
                    v.tensor_tensor(catT[:, 0:4, :], bgT, tmpT, MUL).then_inc(sem("tok_ready"), dve.sends(sem("tok_ready")))
                for h in range(NHX):
                    copy_out(xsc[:, h, :, :], h, v3(banks[h][:, :], 2))
                    dve_eng.wait_ge(dve.last, dve.value)
                    v.tensor_reduce(S_MX[:, 2 * h:2 * h + 2], xsc[:, h, :, :], AX, MAX).then_inc(dve_step, dve.sends(dve_step))
                    dve_eng.wait_ge(dve.last, dve.value)
                    v.tensor_scalar(S_NM[:, 2 * h:2 * h + 2], S_MX[:, 2 * h:2 * h + 2], -XSCALE, None, MUL).then_inc(sem("max_ready"), dve.sends(sem("max_ready")))
                for h in range(NHX):
                    dve_eng.wait_ge(sem("exp_done"), dve.next("exp_done"))
                    v.reciprocal(S_RS[:, 2 * h:2 * h + 2], S_SUM[:, 2 * h:2 * h + 2]).then_inc(dve_step, dve.sends(dve_step))
                    dve_eng.wait_ge(dve.last, dve.value)
                    v.tensor_tensor(xsc[:, h, :, :], xsc[:, h, :, :], per_channel(S_RS[:, 2 * h:2 * h + 2], T), MUL).then_inc(sem("p_ready"), dve.sends(sem("p_ready")))
                for h in range(NHX):
                    copy_out(catT[:, 4 + h, :], 4, banks[4][:, 0:T])
                if i == 0:
                    dve_eng.wait_ge(sem("x_loaded"), 16)
                for n in range(2):
                    for tt in range(TT):
                        b = n + 2 * tt
                        dve_eng.wait_ge(bank_full[b], dve.next(("full", b)))
                        v.scalar_tensor_tensor(y_nat[:, tt, n * 512:(n + 1) * 512], x_nat[:, tt, n * 512:(n + 1) * 512], ALPHA,
                                                        banks[b][:, :], MUL, ADD).then_inc(bank_free[b], dve.sends(bank_free[b]))
                dve_eng.wait_ge(dve.last, dve.value)
                dve_eng.wait_ge(sem("rows_loaded"), 16 * (2 * i + 1))
                layer_norm(y_nat, x_nat, rows[:, 0:D], rows[:, D:2 * D], "x_ready")
                turned_x()
                dve_eng.wait_ge(sem("scores_ready"), dve.next("scores_ready"))
                sel4 = v3(S_SEL, TT * NG)
                v.tensor_tensor(v3(S_SEL, TT), v3(S_SC, TT), per_column(rowa_sb[:, R_RB:R_RB + NE], TT), ADD).then_inc(dve_step, dve.sends(dve_step))
                dve_eng.wait_ge(dve.last, dve.value)
                pairs = v3(S_BIG[:, 0:48], TT * NG)
                v.tensor_tensor(pairs[:, :, 0:3], sel4[:, :, 1:4], bc(sel4[:, :, 0:1], P, TT * NG, 3), ADD).then_inc(dve_step, dve.sends(dve_step))
                v.tensor_tensor(pairs[:, :, 3:5], sel4[:, :, 2:4], bc(sel4[:, :, 1:2], P, TT * NG, 2), ADD).then_inc(dve_step, dve.sends(dve_step))
                v.tensor_tensor(pairs[:, :, 5:6], sel4[:, :, 3:4], sel4[:, :, 2:3], ADD).then_inc(dve_step, dve.sends(dve_step))
                dve_eng.wait_ge(dve.last, dve.value)
                v.tensor_reduce(S_GSC, pairs, AX, MAX).then_inc(dve_step, dve.sends(dve_step))
                dve_eng.wait_ge(dve.last, dve.value)

                def ranks(vals, a, dst):
                    other = bc(vals.unsqueeze(2), P, a, GS, GS)
                    own = bc(vals.unsqueeze(3), P, a, GS, GS)
                    n = a * GS * GS
                    gt, eq = S_BIG[:, 0:n], S_BIG2[:, 0:n]
                    v.tensor_tensor(v4(gt, a, GS), other, own, ALU.is_gt).then_inc(dve_step, dve.sends(dve_step))
                    v.tensor_tensor(v4(eq, a, GS), other, own, ALU.is_equal).then_inc(dve_step, dve.sends(dve_step))
                    dve_eng.wait_ge(dve.last, dve.value)
                    v.tensor_tensor(v3(eq, a), v3(eq, a), per_column(cst[:, C_TIE:C_TIE + GS * GS], a), MUL).then_inc(dve_step, dve.sends(dve_step))
                    dve_eng.wait_ge(dve.last, dve.value)
                    v.tensor_tensor(gt, gt, eq, ADD).then_inc(dve_step, dve.sends(dve_step))
                    dve_eng.wait_ge(dve.last, dve.value)
                    v.tensor_reduce(dst, v3(gt, a * GS), AX, ADD).then_inc(dve_step, dve.sends(dve_step))
                    dve_eng.wait_ge(dve.last, dve.value)

                ranks(v3(S_GSC, TT), TT, S_GRANK)
                v.tensor_scalar(S_GRANK, S_GRANK, 0.5, None, ALU.is_lt).then_inc(sem("group_ready"), dve.sends(sem("group_ready")))
                ranks(sel4, TT * NG, S_RANK)
                v.tensor_scalar(S_RANK, S_RANK, 1.5, None, ALU.is_lt).then_inc(dve_step, dve.sends(dve_step))
                dve_eng.wait_ge(bank_full[0], dve.next(("full", 0)))
                v.tensor_tensor(S_KEY, banks[0][:, 0:TT * NG], S_GRANK, MUL).then_inc(dve_step, dve.sends(dve_step))
                v.tensor_scalar(S_CNT, banks[0][:, TT * NG:TT * NG + NG], P + 0.5, None, ALU.is_gt).then_inc(bank_free[0], dve.sends(bank_free[0]))
                dve_eng.wait_ge(dve.last, dve.value)
                v.tensor_tensor(pick.rearrange("p a g t -> p (a g) t"), per_column(cst[:, C_IOTA:C_IOTA + P], TT * NG), per_channel(S_KEY, P),
                                ALU.is_equal).then_inc(sem("slots_ready"), dve.sends(sem("slots_ready")))
                v.tensor_tensor(v3(S_RANK, TT * NG), v3(S_RANK, TT * NG), per_channel(S_GRANK, GS), MUL).then_inc(dve_step, dve.sends(dve_step))
                dve_eng.wait_ge(dve.last, dve.value)
                v.tensor_tensor(S_COMB, S_SC, S_RANK, MUL).then_inc(dve_step, dve.sends(dve_step))
                dve_eng.wait_ge(dve.last, dve.value)
                v.tensor_reduce(v3(S_C4, TT), v4(S_COMB, TT, NG).rearrange("p a g e -> p a e g"), AX, ADD).then_inc(dve_step, dve.sends(dve_step))
                dve_eng.wait_ge(dve.last, dve.value)
                v.tensor_reduce(S_RS[:, 0:TT], v3(S_C4, TT), AX, ADD).then_inc(dve_step, dve.sends(dve_step))
                dve_eng.wait_ge(dve.last, dve.value)
                v.reciprocal(S_RS[:, 0:TT], S_RS[:, 0:TT]).then_inc(dve_step, dve.sends(dve_step))
                dve_eng.wait_ge(dve.last, dve.value)
                v.tensor_tensor(v3(S_C4, TT), v3(S_C4, TT), per_channel(S_RS[:, 0:TT], GS), MUL).then_inc(sem("comb_ready"), dve.sends(sem("comb_ready")))
                v.tensor_tensor(S_CNT, S_CNT, cst[:, C_IOTA:C_IOTA + NG], MUL).then_inc(dve_step, dve.sends(dve_step))
                dve_eng.wait_ge(dve.last, dve.value)
                v.tensor_reduce(S_CNT[:, 0:1], S_CNT, AX, ADD).then_inc(dve_step, dve.sends(dve_step))
                dve_eng.wait_ge(dve.last, dve.value)
                v.tensor_copy(spill_info[:, 0:1], S_CNT[:, 0:1]).then_inc(dve_step, dve.sends(dve_step))
                v.tensor_scalar(S_CNT[:, 1:2], S_CNT[:, 0:1], -1.0, 0.0, ADD, MAX).then_inc(dve_step, dve.sends(dve_step))
                dve_eng.wait_ge(dve.last, dve.value)
                v.tensor_copy(spill_info[:, 1:2], S_CNT[:, 1:2]).then_inc(sem("spill_known"), dve.sends(sem("spill_known")))
                for k, b in ((0, 0), (2, 1), (4, 2), (6, 3)):
                    copy_out(xg[:, :, k, :], b, v3(banks[b][:, :], NG))
                copy_out(S_CG, 4, banks[4][:, 0:NE])
                dve_eng.wait_ge(dve.last, dve.value)
                v.tensor_copy(S_BIG[:, 0:1], S_CG[:, 0:1]).then_inc(sem("h_ready"), 1)
                v.tensor_copy(S_BIG2[:, 0:1], S_CG[:, 0:1]).then_inc(sem("og1_ready"), 1)
                dve_eng.wait_ge(sem("spill_known"), i + 1)
                spilt = dve_eng.value_load(spill_info[0:1, 0:1], min_val=0, max_val=NG)

                def group_sums(kind, j, layer, used, weight, sums):
                    before = j * GS + NE * layer
                    for e in range(GS):
                        dve_eng.wait_ge(sem(kind + "up_full"), before + (e + 1))
                        dve_eng.wait_ge(sem(kind + "silu_done"), before + (layer + 2 + e))
                        v.scalar_tensor_tensor(hh, banks[4][:, :], weight(e), sg, MUL, MUL).then_inc(sem(kind + "h_ready"), 1)
                    dve_eng.wait_ge(sem(kind + "ring_free"), j * per_body + used)
                    v.tensor_copy(sums, banks[3][:, :]).then_inc(sem(kind + "og1_ready"), 1)

                slots_before = sum(len(LOADS_FIRST[k]) for k in range(i + 1)) + NE * PER_EXPERT * i
                og_flat = flat2(og)
                with dve_eng.Fori(0, NG) as j:
                    group_sums("", j, i, slots_before + per_body, lambda e: S_CG[:, bass.ds(j * GS + e, 1)], og_flat[:, bass.ds(j * D + 512, 512)])
                with dve_eng.If(spilt > 0):
                    kind = f"spill{i}_"
                    v.tensor_reduce(S_KMAX, v3(S_KEY, TT), AX, MAX).then_inc(sem(kind + "places"), 1)
                    dve_eng.wait_ge(sem(kind + "places"), 1)
                    v.tensor_tensor(pick[:, :, 0, :], per_column(cst[:, C_IOTA + P:C_IOTA + T], TT), per_channel(S_KMAX, P),
                                    ALU.is_equal).then_inc(sem(kind + "slots_ready"), 1)
                    v.tensor_copy(S_BIG[:, 0:1], S_KEY[:, 0:1]).then_inc(sem(kind + "h_ready"), 1)
                    v.tensor_copy(S_BIG2[:, 0:1], S_KEY[:, 0:1]).then_inc(sem(kind + "og1_ready"), 1)
                    dve_eng.wait_ge(sem(kind + "copied"), 3)
                    group_sums(kind, 0, 0, per_body, lambda e: S_CGS[:, e:e + 1], og_spill[:, 512:D])
                for b in range(4):
                    half = slice((b % 2) * 512, (b % 2 + 1) * 512)
                    dve_eng.wait_ge(bank_full[b], dve.next(("full", b)))
                    v.scalar_tensor_tensor(y_nat[:, b // 2, half], x_nat[:, b // 2, half], ALPHA, banks[b][:, :], MUL, ADD).then_inc(bank_free[b], dve.sends(bank_free[b]))
                dve_eng.wait_ge(dve.last, dve.value)
                dve_eng.wait_ge(sem("rows_loaded"), 16 * (2 * i + 2))
                layer_norm(y_nat, x_nat, rows[:, 0:D], rows[:, D:2 * D], "x_ready")

            dve_eng.wait_ge(dve.last, dve.value)

            def squares(src, a, n, dst):
                s = v3(sq[:, 0:a * n], a)
                v.tensor_tensor(s, src, src, MUL).then_inc(dve_step, dve.sends(dve_step))
                dve_eng.wait_ge(dve.last, dve.value)
                v.tensor_reduce(dst, s, AX, ADD).then_inc(dve_step, dve.sends(dve_step))

            def mean_eps(at, n, width, eps, last):
                ins = v.tensor_scalar(S_VAR[:, at:at + n], S_VAR[:, at:at + n], 1.0 / width, eps, MUL, ADD)
                if last:
                    ins.then_inc(sem("var_ready"), dve.sends(sem("var_ready")))
                else:
                    ins.then_inc(dve_step, dve.sends(dve_step))

            def scaled(view, r, gain, a, n):
                v.tensor_tensor(view, view, per_channel(r, n), MUL).then_inc(dve_step, dve.sends(dve_step))
                dve_eng.wait_ge(dve.last, dve.value)
                v.tensor_tensor(view, view, per_column(gain, a), MUL).then_inc(dve_step, dve.sends(dve_step))
                dve_eng.wait_ge(dve.last, dve.value)

            def rope(src, dst, nh):
                cos = bc(v3(cst[:, C_COS:C_COS + TT * HALF], TT).unsqueeze(2), P, TT, nh, HALF)
                sin = bc(v3(cst[:, C_SIN:C_SIN + TT * HALF], TT).unsqueeze(2), P, TT, nh, HALF)
                n = TT * nh * HALF
                t = [v4(sq[:, k * n:(k + 1) * n], TT, nh) for k in range(4)]
                lo, hi = src[:, :, :, 0:HALF], src[:, :, :, HALF:ROPE]
                v.tensor_tensor(t[0], lo, cos, MUL).then_inc(dve_step, dve.sends(dve_step))
                v.tensor_tensor(t[1], hi, sin, MUL).then_inc(dve_step, dve.sends(dve_step))
                v.tensor_tensor(t[2], hi, cos, MUL).then_inc(dve_step, dve.sends(dve_step))
                v.tensor_tensor(t[3], lo, sin, MUL).then_inc(dve_step, dve.sends(dve_step))
                dve_eng.wait_ge(dve.last, dve.value)
                if nh != NH:
                    t = [bc(s, P, TT, NH, HALF) for s in t]
                v.tensor_tensor(dst[:, :, :, 0:HALF], t[0], t[1], SUB).then_inc(dve_step, dve.sends(dve_step))
                return v.tensor_tensor(dst[:, :, :, HALF:ROPE], t[2], t[3], ADD)

            def flat3(ap):
                return ap.rearrange("p a b c -> p (a b) c")

            def shift(l, first, tiles):
                dve_eng.wait_ge(sem("shift_in"), dve.next("shift_in"))
                v.tensor_tensor(dcol[:, 0:tiles, :], pcol[:, 0:tiles, 0:T], pcol[:, 0:tiles, 1:T + 1], SUB).then_inc(dve_step, dve.sends(dve_step))
                dve_eng.wait_ge(dve.last, dve.value)
                for m in range(tiles):
                    mu = 12 + l * CP_LAYER + first + m
                    ins = v.scalar_tensor_tensor(sh[:, first + m, :], dcol[:, m, :], col[:, mu:mu + 1], pcol[:, m, 1:T + 1], MUL, ADD)
                    if m == tiles - 1:
                        ins.then_inc(sem("shift_done"), dve.sends(sem("shift_done")))
                    else:
                        ins.then_inc(dve_step, dve.sends(dve_step))

            def turned_qk(kdim):
                for dst, g, b in ((qTt, 0, 0), (qTt, 1, 1), (kTt, 0, 2), (kTt, 1, 3)):
                    copy_out(dst[0:kdim, 4 * g:4 * g + 4, 0:P], b, v3(banks[b][0:kdim, :], 4))

            def softmax(scale):
                for half in range(2):
                    for h in range(4 * half, 4 * half + 4):
                        b = h % NDB
                        dve_eng.wait_ge(bank_full[b], dve.next(("full", b)))
                        v.scalar_tensor_tensor(Pm[:, h, :], banks[b][:, 0:3 * P], scale, cst[:, C_CAUSAL:C_CAUSAL + 3 * P], MUL, ADD).then_inc(bank_free[b], dve.sends(bank_free[b]))
                    dve_eng.wait_ge(dve.last, dve.value)
                    hs, at = slice(4 * half, 4 * half + 4), 8 * half
                    v.tensor_reduce(S_MX[:, at:at + 4], Pm[:, hs, 0:P], AX, MAX).then_inc(dve_step, dve.sends(dve_step))
                    v.tensor_reduce(S_MX[:, at + 4:at + 8], Pm[:, hs, P:3 * P], AX, MAX).then_inc(dve_step, dve.sends(dve_step))
                    dve_eng.wait_ge(dve.last, dve.value)
                    v.tensor_scalar(S_NM[:, at:at + 8], S_MX[:, at:at + 8], -1.0, None, MUL).then_inc(sem("max_ready"), dve.sends(sem("max_ready")))

            def normalise():
                for half in range(2):
                    hs, at = slice(4 * half, 4 * half + 4), 8 * half
                    dve_eng.wait_ge(sem("exp_done"), dve.next("exp_done"))
                    v.reciprocal(S_RS[:, at:at + 8], S_SUM[:, at:at + 8]).then_inc(dve_step, dve.sends(dve_step))
                    dve_eng.wait_ge(dve.last, dve.value)
                    v.tensor_tensor(Pm[:, hs, 0:P], Pm[:, hs, 0:P], per_channel(S_RS[:, at:at + 4], P), MUL).then_inc(dve_step, dve.sends(dve_step))
                    v.tensor_tensor(Pm[:, hs, P:3 * P], Pm[:, hs, P:3 * P], per_channel(S_RS[:, at + 4:at + 8], T), MUL).then_inc(sem("p_ready"), dve.sends(sem("p_ready")))

            def gated_out(g):
                for j in range(4):
                    dve_eng.wait_ge(bank_full[j], dve.next(("full", j)))
                    v.tensor_tensor(oT[:, j, :], banks[j][:, 0:T], gates[:, g, j, :], MUL).then_inc(bank_free[j], dve.sends(bank_free[j]))

            def merge(first):
                dve_eng.wait_ge(sem("sgm_ready"), dve.next("sgm_ready"))
                for n in range(2):
                    for tt in range(TT):
                        b = n + 2 * tt
                        dve_eng.wait_ge(bank_full[b], dve.next(("full", b)))
                        half = slice(n * 512, (n + 1) * 512)
                        o = merged[:, tt, half] if first else sgm[:, tt, half]
                        v.tensor_tensor(o, banks[b][:, :], sgm[:, tt, half], MUL).then_inc(bank_free[b], dve.sends(bank_free[b]))
                dve_eng.wait_ge(dve.last, dve.value)
                if not first:
                    v.tensor_tensor(merged, merged, sgm, ADD).then_inc(dve_step, dve.sends(dve_step))

            for l in range(DEPTH):
                for tt in range(TT):
                    v.tensor_tensor_reduce(out=y_nat[:, tt, :], in0=x_nat[:, tt, :], in1=x_nat[:, tt, :], scale=1.0, scalar=0.0,
                                              op0=MUL, op1=ADD, accum_out=S_VAR[:, tt:tt + 1]).then_inc(dve_step, dve.sends(dve_step))
                dve_eng.wait_ge(dve.last, dve.value)
                mean_eps(0, TT, D, RMS_EPS, True)
                roots(TT)
                dve_eng.wait_ge(sem("rows_loaded"), 16 * (2 * DEPTH + l + 1))
                for tt in range(TT):
                    ins = v.scalar_tensor_tensor(y_nat[:, tt, :], x_nat[:, tt, :], S_RSTD[:, tt:tt + 1], rowv("norm"), MUL, MUL)
                    if tt:
                        ins.then_inc(sem("h_ready2"), dve.sends(sem("h_ready2")))
                    else:
                        ins.then_inc(dve_step, dve.sends(dve_step))
                turned_x()
                for tt in range(TT):
                    copy_out(cnat[:, tt, :], tt, banks[tt][:, 0:LAT])
                dve_eng.wait_ge(dve.last, dve.value)
                for at, a, n in ((0, 0, 256), (2, 256, 128), (4, 384, ROPE)):
                    squares(cnat[:, :, a:a + n], TT, n, S_VAR[:, at:at + 2])
                    dve_eng.wait_ge(dve.last, dve.value)
                mean_eps(0, 2, 256, RMS_EPS, False)
                mean_eps(2, 2, 128, RMS_EPS, False)
                mean_eps(4, 2, ROPE, RMS_EPS, True)
                roots(6)
                scaled(cnat[:, :, 384:LAT], S_RSTD[:, 4:6], rowv("kr"), TT, ROPE)
                scaled(cnat[:, :, 0:256], S_RSTD[:, 0:2], rowv("qa"), TT, 256)
                v.tensor_tensor(cnat[:, :, 256:384], cnat[:, :, 256:384], per_channel(S_RSTD[:, 2:4], 128), MUL).then_inc(dve_step, dve.sends(dve_step))
                dve_eng.wait_ge(dve.last, dve.value)
                v.tensor_tensor(cnat[:, :, 256:384], cnat[:, :, 256:384], per_column(rowv("kva"), TT), MUL).then_inc(sem("lat_ready"), dve.sends(sem("lat_ready")))
                n = TT * NH
                lf, lfe, neg = ffn[:, 0:n], ffn[:, n:2 * n], ffn[:, 2 * n:3 * n]
                dve_eng.wait_ge(bank_full[4], dve.next(("full", 4)))
                v.tensor_tensor(v3(lf, TT), v3(banks[4][:, 0:n], TT), per_column(rowv("bf"), TT), ADD).then_inc(bank_free[4], dve.sends(bank_free[4]))
                dve_eng.wait_ge(dve.last, dve.value)
                v.tensor_scalar(neg, lf, -1.0, None, MUL).then_inc(dve_step, dve.sends(dve_step))
                dve_eng.wait_ge(dve.last, dve.value)
                v.tensor_tensor(lfe, lf, neg, MIN).then_inc(sem("gates_neg"), dve.sends(sem("gates_neg")))
                v.tensor_scalar(lf, lf, 0.0, None, MIN).then_inc(dve_step, dve.sends(dve_step))
                dve_eng.wait_ge(dve.last, dve.value)
                copy_out(cT[:, 0:2, :], 2, v3(banks[2][:, :], 2))
                copy_out(cT[:, 2, :], 3, banks[3][:, 0:T])
                dve_eng.wait_ge(dve.last, dve.value)
                dve_eng.wait_ge(sem("gates_ln"), dve.next("gates_ln"))
                v.tensor_tensor(lf, lf, lfe, SUB).then_inc(sem("logf_ready"), dve.sends(sem("logf_ready")))
                for n4 in range(2):
                    for tt in range(TT):
                        b = 2 * n4 + tt
                        copy_out(qn[:, tt, 4 * n4:4 * n4 + 4, :], b, v3(banks[b][:, 0:4 * QK], 4))
                dve_eng.wait_ge(dve.last, dve.value)
                dve_eng.wait_ge(sem("kv_ready"), dve.next("kv_ready"))
                qf, kf = flat3(qn), flat3(kn)
                squares(qf, TT * NH, QK, S_VAR[:, 0:16])
                dve_eng.wait_ge(dve.last, dve.value)
                squares(kf[:, :, 0:NOPE], TT * NH, NOPE, S_VAR[:, 16:32])
                dve_eng.wait_ge(dve.last, dve.value)
                mean_eps(0, 16, QK, RMS_EPS, False)
                mean_eps(16, 16, NOPE, RMS_EPS, True)
                roots(32)
                scaled(qf, S_RSTD[:, 0:16], rowv("q"), TT * NH, QK)
                scaled(kf[:, :, 0:NOPE], S_RSTD[:, 16:32], rowv("kn"), TT * NH, NOPE)
                rope(qn[:, :, :, NOPE:QK], qn[:, :, :, NOPE:QK], NH).then_inc(dve_step, dve.sends(dve_step))
                dve_eng.wait_ge(dve.last, dve.value)
                krope = rope(cnat[:, :, 384:LAT].unsqueeze(2), kn[:, :, :, NOPE:QK], 1)
                krope.then_inc(sem("qk_ready"), dve.sends(sem("qk_ready")))
                v.memset(pcol[:, :, 0:1], 0.0).then_inc(dve_step, dve.sends(dve_step))
                dve_eng.wait_ge(dve.last, dve.value)
                for t in range(0, 8, 2):
                    shift(l, t, 2)
                turned_qk(QK)
                softmax(QK ** -0.5)
                cum_sb = neg
                copy_out(cum_sb, 4, banks[4][:, 0:TT * NH])
                for tt in range(TT):
                    copy_out(qn[:, tt, :, 0:HC], tt, v3(banks[tt][:, :], NH))
                for tt in range(TT):
                    copy_out(kn[:, tt, :, 0:HC], 2 + tt, v3(banks[2 + tt][:, :], NH))
                normalise()
                dve_eng.wait_ge(dve.last, dve.value)
                sqf = flat2(sgm)
                for src, at in ((qf, 0), (kf, 16)):
                    s = v3(sqf[:, 0:TT * NH * HC], TT * NH)
                    v.tensor_tensor(s, src[:, :, 0:HC], src[:, :, 0:HC], MUL).then_inc(dve_step, dve.sends(dve_step))
                    dve_eng.wait_ge(dve.last, dve.value)
                    v.tensor_reduce(S_VAR[:, at:at + 16], s, AX, ADD).then_inc(dve_step, dve.sends(dve_step))
                    dve_eng.wait_ge(dve.last, dve.value)
                mean_eps(0, 32, HC, RMS_EPS, True)
                roots(32)
                scaled(qf[:, :, 0:HC], S_RSTD[:, 0:16], rowv("fq"), TT * NH, HC)
                scaled(kf[:, :, 0:HC], S_RSTD[:, 16:32], rowv("fk"), TT * NH, HC)
                v.tensor_scalar(qf[:, :, 0:HC], qf[:, :, 0:HC], HC ** -0.5, None, MUL).then_inc(dve_step, dve.sends(dve_step))
                cum3 = cum_sb.unsqueeze(2)
                v.tensor_copy(qf[:, :, HC:HC + 1], cum3).then_inc(dve_step, dve.sends(dve_step))
                v.memset(qf[:, :, HC + 1:HC + 2], 1.0).then_inc(dve_step, dve.sends(dve_step))
                v.memset(kf[:, :, HC:HC + 1], 1.0).then_inc(dve_step, dve.sends(dve_step))
                v.tensor_scalar(kf[:, :, HC + 1:HC + 2], cum3, -1.0, None, MUL).then_inc(sem("qk_ready"), dve.sends(sem("qk_ready")))
                gated_out(0)
                for t in range(8, 12, 2):
                    shift(l, t, 2)
                shift(l, 12, 1)
                dve_eng.wait_ge(dve.last, dve.value)
                turned_qk(FOXK)
                softmax(1.0)
                merge(True)
                normalise()
                gated_out(1)
                merge(False)
                dve_eng.wait_ge(dve.last, dve.value)
                v.tensor_copy(S_BIG[:, 0:1], sh[:, 12, 0:1]).then_inc(sem("shift_ready"), dve.sends(sem("shift_ready")))
                if l == 0:
                    v.tensor_copy(vfirst, vlT).then_inc(dve_step, dve.sends(dve_step))
                    dve_eng.wait_ge(dve.last, dve.value)
                else:
                    copy_out(v_mid, 4, banks[4][0:32, 0:T])
                    for g in range(2):
                        dve_eng.wait_ge(bank_full[g], dve.next(("full", g)))
                        v.tensor_tensor(nuT[:, 2 * g:2 * g + 2, :], v3(banks[g][:, :], 2), per_channel(colv(l, V0)[:, 2 * g:2 * g + 2], T), ADD).then_inc(bank_free[g], dve.sends(bank_free[g]))
                    dve_eng.wait_ge(dve.last, dve.value)
                    v.tensor_tensor(vdiff, vfirst, vlT, SUB).then_inc(sem("nu_in"), dve.sends(sem("nu_in")))
                    dve_eng.wait_ge(sem("nu_ready"), dve.next("nu_ready"))
                    dve_eng.wait_ge(dve.last, dve.value)
                    v.tensor_tensor(vdiff, vdiff, nuT, MUL).then_inc(dve_step, dve.sends(dve_step))
                    dve_eng.wait_ge(dve.last, dve.value)
                    v.tensor_tensor(vlT, vlT, vdiff, ADD).then_inc(dve_step, dve.sends(dve_step))
                    dve_eng.wait_ge(dve.last, dve.value)
                for tt in range(TT):
                    tok = slice(tt * P, (tt + 1) * P)
                    r_, k_, v_ = rlT[:, :, tok], klT[:, :, tok], vlT[:, :, tok]
                    v.tensor_copy(S_BIG[:, 0:1], sh[:, 12, 0:1]).then_inc(sem("shift_all"), dve.sends(sem("shift_all")))
                    v.tensor_tensor(kk, k_, per_channel(colv(l, KK), P), MUL).then_inc(dve_step, dve.sends(dve_step))
                    dve_eng.wait_ge(dve.last, dve.value)
                    v.tensor_tensor(t1, kk, kk, MUL).then_inc(sem("ksq_ready"), dve.sends(sem("ksq_ready")))
                    dve_eng.wait_ge(bank_full[0], dve.next(("full", 0)))
                    v.tensor_tensor(lw, v3(banks[0][:, :], 4), per_channel(colv(l, W0), P), ADD).then_inc(bank_free[0], dve.sends(bank_free[0]))
                    dve_eng.wait_ge(bank_full[1], dve.next(("full", 1)))
                    v.tensor_tensor(aa, v3(banks[1][:, :], 4), per_channel(colv(l, A0), P), ADD).then_inc(bank_free[1], dve.sends(bank_free[1]))
                    dve_eng.wait_ge(dve.last, dve.value)
                    v.tensor_copy(S_BIG[:, 0:1], sh[:, 12, 0:1]).then_inc(sem("wa_in"), dve.sends(sem("wa_in")))
                    dve_eng.wait_ge(bank_full[2], dve.next(("full", 2)))
                    v.tensor_scalar(flat2(t1), banks[2][:, :], 1e-24, None, MAX).then_inc(bank_free[2], dve.sends(bank_free[2]))
                    dve_eng.wait_ge(dve.last, dve.value)
                    v.tensor_copy(S_BIG[:, 0:1], sh[:, 12, 0:1]).then_inc(sem("ksum_ready"), dve.sends(sem("ksum_ready")))
                    dve_eng.wait_ge(sem("wa_ready"), dve.next("wa_ready"))
                    v.tensor_scalar(flat2(lw), flat2(lw), DECAY, None, MUL).then_inc(dve_step, dve.sends(dve_step))
                    dve_eng.wait_ge(dve.last, dve.value)
                    v.tensor_tensor_scan(flat2(cum), cst[:, C_SCAN:C_SCAN + 4 * P], flat2(lw), 0.0, MUL, ADD).then_inc(dve_step, dve.sends(dve_step))
                    dve_eng.wait_ge(dve.last, dve.value)
                    v.tensor_tensor(pex, cum, lw, SUB).then_inc(sem("cum_ready"), dve.sends(sem("cum_ready")))
                    dve_eng.wait_ge(sem("knorm_ready"), dve.next("knorm_ready"))
                    v.reciprocal(flat2(t1), flat2(t1)).then_inc(dve_step, dve.sends(dve_step))
                    dve_eng.wait_ge(dve.last, dve.value)
                    v.tensor_tensor(kk, kk, t1, MUL).then_inc(dve_step, dve.sends(dve_step))
                    dve_eng.wait_ge(dve.last, dve.value)
                    v.tensor_scalar(flat2(t1), flat2(aa), -1.0, None, ADD).then_inc(dve_step, dve.sends(dve_step))
                    dve_eng.wait_ge(dve.last, dve.value)
                    v.tensor_tensor(t1, t1, per_channel(colv(l, KA), P), MUL).then_inc(dve_step, dve.sends(dve_step))
                    dve_eng.wait_ge(dve.last, dve.value)
                    v.tensor_scalar(flat2(t1), flat2(t1), 1.0, None, ADD).then_inc(dve_step, dve.sends(dve_step))
                    dve_eng.wait_ge(dve.last, dve.value)
                    v.tensor_tensor(km, t1, k_, MUL).then_inc(dve_step, dve.sends(dve_step))
                    dve_eng.wait_ge(dve.last, dve.value)
                    v.tensor_tensor(rk, km, r_, MUL).then_inc(dve_step, dve.sends(dve_step))
                    dve_eng.wait_ge(dve.last, dve.value)
                    v.tensor_tensor(rk, rk, per_channel(colv(l, RK), P), MUL).then_inc(dve_step, dve.sends(dve_step))
                    dve_eng.wait_ge(dve.last, dve.value)
                    v.tensor_scalar(flat2(aa), flat2(aa), -1.0, None, MUL).then_inc(dve_step, dve.sends(dve_step))
                    dve_eng.wait_ge(sem("decay_ready"), dve.next("decay_ready"))
                    v.tensor_copy(pcs.unsqueeze(2), pp.rearrange("p a (c t) -> p (a c) t", c=2)[:, :, CH - 1:CH]).then_inc(dve_step, dve.sends(dve_step))
                    dve_eng.wait_ge(dve.last, dve.value)
                    v.tensor_tensor(aa, aa, kk, MUL).then_inc(dve_step, dve.sends(dve_step))
                    dve_eng.wait_ge(dve.last, dve.value)
                    v.tensor_tensor(pex, pex, kk, MUL).then_inc(dve_step, dve.sends(dve_step))
                    v.tensor_tensor(aa, aa, pinv, MUL).then_inc(dve_step, dve.sends(dve_step))
                    dve_eng.wait_ge(dve.last, dve.value)
                    v.tensor_tensor(pinv, pinv, km, MUL).then_inc(dve_step, dve.sends(dve_step))
                    dve_eng.wait_ge(dve.last, dve.value)

                    def to_end(dst, src):
                        return v.tensor_tensor(dst.rearrange("p a (c t) -> p (a c) t", c=2), src.rearrange("p a (c t) -> p (a c) t", c=2),
                                               per_channel(pcs, CH), MUL)

                    to_end(cum, aa).then_inc(dve_step, dve.sends(dve_step))
                    to_end(lw, pinv).then_inc(dve_step, dve.sends(dve_step))
                    v.tensor_tensor(pp, pp, r_, MUL).then_inc(sem("rows_ready"), dve.sends(sem("rows_ready")))
                    for par in range(2):
                        copy_out(NTm[:, par, :, :], 0, v3(banks[0][:, :], 4))
                        for b, dst, mask in ((1, MTm, C_STRICT), (2, AkT, C_INCL), (3, AbT, C_INCL)):
                            dve_eng.wait_ge(bank_full[b], dve.next(("full", b)))
                            v.tensor_tensor(dst[:, par, :, :], v3(banks[b][:, :], 4), mat4(mask), MUL).then_inc(bank_free[b], dve.sends(bank_free[b]))
                    dve_eng.wait_ge(bank_full[4], dve.next(("full", 4)))
                    v.tensor_copy(S_RS[:, 0:NH], banks[4][:, 0:NH]).then_inc(dve_step, dve.sends(dve_step))
                    v.tensor_copy(pc0[0:64, :], banks[4][0:64, 64:80]).then_inc(bank_free[4], dve.sends(bank_free[4]))
                    copy_out(Kp, 3, banks[3][:, :])
                    dve_eng.wait_ge(dve.last, dve.value)
                    for par in range(2):
                        v.tensor_tensor(Nl[:, par, :, :], NTm[:, par, :, :], mat4(C_LEV), MUL).then_inc(dve_step, dve.sends(dve_step))
                        dve_eng.wait_ge(dve.last, dve.value)
                        v.tensor_tensor(TTm[:, par, :, :], Nl[:, par, :, :], mat4(C_ID), ADD).then_inc(sem("level_ready"), dve.sends(sem("level_ready")))
                    for par in range(2):
                        copy_out(Tm[:, par, :, :], par, v3(banks[par][:, :], 4))
                        dve_eng.wait_ge(dve.last, dve.value)
                        v.tensor_tensor(Nl[:, par, :, :], NTm[:, par, :, :], mat4(C_LEV + P), MUL).then_inc(sem("level_ready"), dve.sends(sem("level_ready")))
                    for lev in range(1, LEVELS):
                        for par in range(2):
                            if lev < LEVELS - 1:
                                dve_eng.wait_ge(bank_full[2 * par], dve.next(("full", 2 * par)))
                                v.tensor_tensor(Tm[:, par, :, :], Tm[:, par, :, :], v3(banks[2 * par][:, :], 4), ADD).then_inc(bank_free[2 * par], dve.sends(bank_free[2 * par]))
                            dve_eng.wait_ge(bank_full[2 * par + 1], dve.next(("full", 2 * par + 1)))
                            v.tensor_tensor(TTm[:, par, :, :], TTm[:, par, :, :], v3(banks[2 * par + 1][:, :], 4), ADD).then_inc(bank_free[2 * par + 1], dve.sends(bank_free[2 * par + 1]))
                            if lev < LEVELS - 1:
                                v.tensor_tensor(Nl[:, par, :, :], NTm[:, par, :, :], mat4(C_LEV + (lev + 1) * P), MUL).then_inc(sem("level_ready"), dve.sends(sem("level_ready")))
                    copy_out(Wn, 2, banks[2][:, :])
                    copy_out(mv, 3, banks[3][:, :])
                    copy_out(uv, 4, banks[4][:, :])
                    chunks = (0, 1) if tt == 0 else (0,)
                    for c in chunks:
                        g = 2 * tt + c
                        if g:
                            shape = [64, 4, 2, HC]
                            diag = ysq[0:64, :]
                            dec = pc0[0:64, :].rearrange("p (b a c) -> p a b c", b=2, c=2)[:, :, :, c:c + 1]
                            v.tensor_tensor(v4(diag, 4, 2), bc(mat(C_ID)[0:64, 0:64].unsqueeze(1).unsqueeze(1), *shape), bc(dec, *shape), MUL).then_inc(dve_step, dve.sends(dve_step))
                            dve_eng.wait_ge(dve.last, dve.value)
                            dve_eng.wait_ge(bank_full[c], dve.next(("full", c)))
                            v.tensor_tensor(GT[0:64, c, :, :], v3(banks[c][0:64, :], NH), v3(diag, NH), ADD).then_inc(bank_free[c], dve.sends(bank_free[c]))
                            copy_out(Hs[0:64, c, :], 2 + c, banks[2 + c][0:64, :])
                        else:
                            copy_out(states[0][0:64, :], 2, banks[2][0:64, :])
                    dve_eng.wait_ge(dve.last, dve.value)
                    for c in chunks:
                        g = 2 * tt + c
                        if g:
                            dve_eng.wait_ge(bank_full[4], dve.next(("full", 4)))
                            v.tensor_tensor(states[g][0:64, :], banks[4][0:64, :], Hs[0:64, c, :], ADD).then_inc(bank_free[4], dve.sends(bank_free[4]))
                    copy_out(yv, 4, banks[4][:, :])
                    dve_eng.wait_ge(dve.last, dve.value)
                    y3, q3 = v3(yv, NH), v3(ysq, NH)
                    v.tensor_reduce(S_MX[:, 0:NH], y3, AX, ADD).then_inc(dve_step, dve.sends(dve_step))
                    dve_eng.wait_ge(dve.last, dve.value)
                    v.tensor_scalar(S_MX[:, 0:NH], S_MX[:, 0:NH], 1.0 / HC, None, MUL).then_inc(dve_step, dve.sends(dve_step))
                    dve_eng.wait_ge(dve.last, dve.value)
                    v.tensor_tensor(y3, y3, per_channel(S_MX[:, 0:NH], HC), SUB).then_inc(dve_step, dve.sends(dve_step))
                    dve_eng.wait_ge(dve.last, dve.value)
                    v.tensor_tensor(ysq, yv, yv, MUL).then_inc(dve_step, dve.sends(dve_step))
                    dve_eng.wait_ge(dve.last, dve.value)
                    v.tensor_reduce(S_VAR[:, 0:NH], q3, AX, ADD).then_inc(dve_step, dve.sends(dve_step))
                    dve_eng.wait_ge(dve.last, dve.value)
                    mean_eps(0, NH, HC, GN_EPS, True)
                    roots(NH)
                    v.tensor_tensor(y3, y3, per_channel(S_RSTD[:, 0:NH], HC), MUL).then_inc(dve_step, dve.sends(dve_step))
                    dve_eng.wait_ge(dve.last, dve.value)
                    v.tensor_tensor(yv, yv, rowv("lg"), MUL).then_inc(dve_step, dve.sends(dve_step))
                    dve_eng.wait_ge(dve.last, dve.value)
                    v.tensor_tensor(q3, v3(Vn, NH), per_channel(S_RS[:, 0:NH], HC), MUL).then_inc(dve_step, dve.sends(dve_step))
                    v.tensor_tensor(yv, yv, rowv("lb"), ADD).then_inc(dve_step, dve.sends(dve_step))
                    dve_eng.wait_ge(dve.last, dve.value)
                    v.tensor_tensor(yv, yv, ysq, ADD).then_inc(sem("y_ready"), dve.sends(sem("y_ready")))
                    dve_eng.wait_ge(bank_full[0], dve.next(("full", 0)))
                    v.tensor_tensor(oT[:, :, tok], v3(banks[0][:, :], 4), gates[:, 0, :, tok], MUL).then_inc(bank_free[0], dve.sends(bank_free[0]))
                merge(False)
                dve_eng.wait_ge(dve.last, dve.value)
                v.tensor_copy(S_BIG[:, 0:1], merged[:, 1, D - 1:D]).then_inc(sem("merged_ready"), dve.sends(sem("merged_ready")))
                turned_x()
                for n in range(2):
                    for tt in range(TT):
                        b = n + 2 * tt
                        dve_eng.wait_ge(bank_full[b], dve.next(("full", b)))
                        half = slice(n * 512, (n + 1) * 512)
                        v.tensor_tensor(x_nat[:, tt, half], x_nat[:, tt, half], banks[b][:, :], ADD).then_inc(bank_free[b], dve.sends(bank_free[b]))
                dve_eng.wait_ge(dve.last, dve.value)
                v.tensor_copy(S_BIG[:, 0:1], x_nat[:, 1, D - 1:D]).then_inc(sem("x_ready"), dve.sends(sem("x_ready")))


def constants():
    import numpy as np
    c = np.zeros((P, NCONST), np.float32)
    i, t = np.arange(P)[:, None], np.arange(P)[None, :]
    same = i // CH == t // CH
    c[:, C_ID:C_ID + P] = i == t
    c[:, C_STRICT:C_STRICT + P] = (i < t) & same
    c[:, C_INCL:C_INCL + P] = (i <= t) & same
    c[:, C_BLOCK:C_BLOCK + P] = same
    c[:, C_TRI:C_TRI + P] = i <= t
    c[:, C_ONES:C_ONES + P] = 1
    c[:, C_ALPHA:C_ALPHA + P] = (i == t) * ALPHA
    for n in range(LEVELS):
        b = 1 << n
        c[:, C_LEV + n * P:C_LEV + (n + 1) * P] = (i // (2 * b) == t // (2 * b)) & (i % (2 * b) < b) & (t % (2 * b) >= b)
    causal = np.where(t <= i, 0.0, -1e30)
    c[:, C_CAUSAL:C_CAUSAL + P] = causal
    c[:, C_CAUSAL + 2 * P:C_CAUSAL + 3 * P] = causal
    c[:, C_SCAN:C_SCAN + 4 * P] = np.arange(4 * P)[None, :] % CH != 0
    c[:, C_SGU:C_SGU + P] = t // CH >= i // CH
    inv = np.float32(10000.0) ** (-np.arange(0, ROPE, 2, dtype=np.float32) / ROPE)
    ang = np.arange(T, dtype=np.float32)[:, None] * inv[None, :].astype(np.float32)
    for at, f in ((C_COS, np.cos), (C_SIN, np.sin)):
        c[:, at:at + TT * HALF] = f(ang).reshape(TT, P, HALF).transpose(1, 0, 2).reshape(P, -1)
    for j in range(4):
        for m in range(2):
            c[64 * m:64 * m + 64, C_SEL + j * NH + 2 * j + m] = 1
    own, other = np.arange(GS)[:, None], np.arange(GS)[None, :]
    c[:, C_TIE:C_TIE + GS * GS] = (other < own).reshape(1, -1)
    c[:, C_IOTA:C_IOTA + T] = np.arange(1, T + 1)[None, :]
    return c


def kernel(**inputs):
    import numpy as np
    import concourse.bacc as bacc
    from concourse import mybir
    from concourse.bass_utils import run_bass_kernel_spmd

    a = {k: np.asarray(v) for k, v in inputs.items()}

    def tiles(w):
        k, n = w.shape
        return w.reshape(k // P, P, n).transpose(1, 0, 2).reshape(P, -1)

    def cut(w, edges):
        return [tiles(w[:, lo:hi]) for lo, hi in zip(edges[:-1], edges[1:])]

    def chan(w):
        return w.reshape(-1, P).T

    def cat(parts):
        return np.ascontiguousarray(np.concatenate(parts, axis=1))

    halves, half3, half4 = (0, 512, 1024), (0, 512, 1024, 1536), (0, 512, 1024, 1536, 2048)
    first = [cat(cut(a["w_kv"][i], halves) + cut(w, e) + cut(a["w_out"][i], halves))
             for i, (w, e) in enumerate(((a["w_in_a"][0], half3), (a["w_in_b"][0], half4)))]
    moe = np.empty((DEPTH, NG, GS * PER_EXPERT, P, SLOT), np.float32)
    for s, (name, e) in enumerate(GROUP_SLOTS):
        w = a["w_" + name][:, e::GS]
        moe[:, :, s] = w.reshape(DEPTH, NG, -1, P, w.shape[-1]).transpose(0, 1, 3, 2, 4).reshape(DEPTH, NG, P, SLOT)

    at = np.cumsum([0, LAT, MIX, MIX, MIX, MIX, NH, MIX, MIX, MIX, MIX, 128, MIX])
    c_lat, c_ga, c_fq, c_fk, c_fv, c_ff, c_gb, c_r, c_k, c_v, c_wa, c_gc, c_mg = at
    second, ff, lora, cols, rows2 = [], [], [], [], []
    colp = [a["conv_w"][0].reshape(3, 4, P).transpose(2, 1, 0).reshape(P, 12)]
    for l in range(DEPTH):
        w = a["w_in_2"][l]

        def c(lo, n=MIX):
            return tiles(w[:, lo:lo + n])

        parts = [c(c_lat, LAT), c(c_ga), tiles(a["mla_w_uq_2"][l]), tiles(a["mla_w_ukv_2"][l]), c(c_r), c(c_k), c(c_fq), c(c_fk),
                 c(c_fv), c(c_gb), c(c_v), c(c_wa, P)]
        parts += [tiles(a["w_pa_2"][l]), c(c_mg), c(c_mg + 512), c(c_gc), tiles(a["w_pb_2"][l]), c(c_mg + 1024), c(c_mg + 1536),
                  tiles(a["w_pc_2"][l]), c(c_mg + 2048), c(c_mg + 2560)] + cut(a["w_out_2"][l], halves)
        assert [p.shape[1] for p in parts] == LOADS_SECOND
        second.append(cat(parts))
        ff.append(c(c_ff, NH).reshape(P, KD, NH))
        lo = np.zeros((P, 1152), np.float32)
        lo[0:64, 0:512], lo[64:128, 0:512] = a["rwkv_w_up_2"][l], a["rwkv_a_up_2"][l]
        lo[:, 512:640] = tiles(a["rwkv_v_down_2"][0])
        lo[0:32, 640:1152] = a["rwkv_v_up_2"][0]
        lora.append(lo)
        colp += [chan(a[n + "_2"][l].reshape(-1)) for n in ("rwkv_mu", "rwkv_w0", "rwkv_a0", "rwkv_k_k", "rwkv_k_a", "rwkv_r_k")]
        colp.append(chan(a["rwkv_v0_2"][0]))
        rows2.append(np.concatenate([a[n + "_2"][l] for n in ("norm_g", "mla_qa_g", "mla_kva_g", "mla_q_g", "mla_knope_g", "mla_krope_g",
                                                             "fox_q_g", "fox_k_g", "fox_b_f", "rwkv_lnx_g", "rwkv_lnx_b")]))
    tokens = a["x"][0]
    arrays = {
        "x0": tokens.reshape(TT, P, D).transpose(1, 0, 2), "x0T": tokens.T.reshape(KD, P, T).transpose(1, 0, 2),
        "memT0": a["mem"][0].T.reshape(KD, P, T).transpose(1, 0, 2), "sguT": a["sgu_w"][0].transpose(2, 0, 1),
        "wfirst0": first[0], "wfirst1": first[1], "wmoe": moe, "wsecond": np.stack(second), "wff": np.stack(ff),
        "lora": np.stack(lora), "rw": tiles(a["router_w"]).reshape(P, KD, NE), "consts": constants(), "colp": np.concatenate(colp, axis=1),
        "rowa": np.concatenate([a["sgu_ln_g"][0], a["sgu_ln_b"][0], a["sgu_b"][0].reshape(-1), a["router_b"]])[None],
        "lnrows": np.stack([np.concatenate([a[g][i], a[b][i]]) for i in range(DEPTH) for g, b in (("ln1_g", "ln1_b"), ("ln2_g", "ln2_b"))]),
        "rows2": np.stack(rows2),
    }
    arrays = {k: np.ascontiguousarray(v) for k, v in arrays.items()}
    nc = bacc.Bacc("TRN2", target_bir_lowering=False, num_devices=1)
    aps = [nc.dram_tensor(k, v.shape, mybir.dt.float32, kind="ExternalInput").ap() for k, v in arrays.items()]
    out = nc.dram_tensor("out", (P, TT, D), mybir.dt.float32, kind="ExternalOutput").ap()
    two_blocks(nc, *aps, out)
    r = run_bass_kernel_spmd(nc, [arrays], core_ids=[0])
    got = r.results[0]["out"]
    return got.transpose(1, 0, 2).reshape(1, T, D)
```

```python
import concourse.bass as bass
from concourse import mybir
from contextlib import ExitStack

P = 128
T = 256
TT = T // P
D = 1024
KD = D // P
MIX = 512
KM = MIX // P
NHX = 4
XSCALE = P ** -0.5
NE, NG, GS = 16, 4, 4
F = 512
DEPTH = 2
ALPHA = (2 * DEPTH) ** 0.25
LN_EPS, RMS_EPS, GN_EPS = 1e-5, 1e-6, 64e-5
NH = 8
HC = 64
NOPE, ROPE, QK = 64, 32, 96
HALF = ROPE // 2
FOXK = 66
LAT = 416
CH = 64
DECAY = -0.606531
SLOT = 4096
RING = 4
PER_EXPERT = 3
HSIGS = NE + 1
GSIGS = 2 * (NG + 1)
TSIGS = NG
HALF_SLOT = SLOT // 2
SPLITS = 3
RAW = 4
UNITS = 2 * NE * PER_EXPERT
USIGS = UNITS + SPLITS
LSIGS = UNITS + RAW
GROUP_SLOTS = (("gate", 0), ("up", 0), ("gate", 1), ("up", 1), ("down", 0), ("gate", 2), ("up", 2), ("down", 1),
               ("gate", 3), ("up", 3), ("down", 2), ("down", 3))
NDB = 5

LOADS_FIRST = [[SLOT] * 9, [SLOT] * 6]
LOADS_SECOND = ([KD * LAT, SLOT, SLOT, 1536, 1024, SLOT, SLOT, SLOT, SLOT, SLOT, SLOT, KD * P] + [SLOT] * 4 +
                [SLOT // 2, SLOT] * 2 + [SLOT] * 5)

C_ID, C_STRICT, C_INCL, C_BLOCK, C_TRI, C_ONES, C_LEV = [P * n for n in range(7)]
LEVELS = 6
C_CAUSAL = C_LEV + LEVELS * P
C_SCAN = C_CAUSAL + 3 * P
C_COS = C_SCAN + 4 * P
C_SIN = C_COS + TT * HALF
C_SEL = C_SIN + TT * HALF
C_TIE = C_SEL + 4 * NH
C_IOTA = C_TIE + GS * GS
NCONST = C_IOTA + T

CP_CONV = 0
CP_LAYER = 13 + 6 * 4
NCOLP = 12 + DEPTH * CP_LAYER
W0, A0, KK, KA, RK, V0 = range(6)

R_SGUG, R_SGUB, R_SGUBIAS, R_RB = 0, MIX, 2 * MIX, 3 * MIX
NROWA = R_RB + NE
ROWS = {}
NROWS = 0
for _name, _n in (("norm", D), ("qa", 256), ("kva", 128), ("q", QK), ("kn", NOPE), ("kr", ROPE), ("fq", HC),
                  ("fk", HC), ("bf", NH), ("lg", MIX), ("lb", MIX)):
    ROWS[_name] = (NROWS, _n)
    NROWS += _n


def two_blocks(nc, x0, x0T, memT0, sguT, wfirst0, wfirst1, wmoe, wsecond, wff, lora, rw, consts, colp, rowa, lnrows, rows2, out):
    wspill = wmoe.rearrange("l h (g s) p n -> l (h g) s p n", g=2)
    f32 = mybir.dt.float32
    ALU = mybir.AluOpType
    ACT = mybir.ActivationFunctionType
    AX = mybir.AxisListType.X
    MUL, ADD, SUB, MAX, MIN = ALU.mult, ALU.add, ALU.subtract, ALU.max, ALU.min

    ctx = ExitStack()
    with ctx:
        def sb(name, n):
            return ctx.enter_context(nc.sbuf_tensor(name, [P, n], f32))[:, :]

        semaphores = {}

        def sem(name):
            if name not in semaphores:
                semaphores[name] = ctx.enter_context(nc.semaphore(name))
            return semaphores[name]

        def v3(ap, a):
            return ap.rearrange("p (a b) -> p a b", a=a)

        def v4(ap, a, b):
            return ap.rearrange("p (a b c) -> p a b c", a=a, b=b)

        f32r = mybir.dt.float32r

        def reduced(name, at, *shape):
            n = 1
            for d in shape:
                n *= d
            ap = nc.alloc_sbuf_tensor_at(name, [P, n], f32r, offset=at)[:, :]
            return v3(ap, shape[0]) if len(shape) == 2 else ap

        ring_at = -(-nc.sbuf_base // 32) * 32
        ring = sb("ring", RING * SLOT)
        cst = sb("cst", NCONST)
        col = sb("col", NCOLP)
        x_nat = v3(sb("x_nat", TT * D), TT)
        wide_at = -(-nc.sbuf_base // 32) * 32
        wide = sb("wide", SLOT)
        y_nat = v3(wide[:, 0:TT * D], TT)
        xT = v3(wide[:, TT * D:SLOT], KD)
        rows = sb("rows", NROWS)
        rwt = v3(sb("rwt", KD * NE), KD)
        small = sb("small", 640)
        ARENA = 24240
        arena_at = -(-nc.sbuf_base // 32) * 32
        arena = sb("arena", ARENA)
        banks = [ctx.enter_context(nc.psum_tensor(f"bank{b}", [P, 512], f32)) for b in range(8)]

        class Carve:
            def __init__(self, at=0):
                self.at = at

            def __call__(self, *shape):
                n = 1
                for s in shape:
                    n *= s
                ap = arena[:, self.at:self.at + n]
                self.at += n
                assert self.at <= ARENA, self.at
                if len(shape) == 2:
                    return v3(ap, shape[0])
                if len(shape) == 3:
                    return v4(ap, shape[0], shape[1])
                return ap

        def bc(ap, *shape):
            return ap.to_broadcast(list(shape))

        def mat(c):
            return cst[:, c:c + P]

        def mat4(c):
            return bc(mat(c).unsqueeze(1), P, 4, P)

        ident = mat(C_ID)

        def per_channel(ap, n):
            return bc(ap.unsqueeze(2), P, ap.shape[1], n)

        def per_column(ap, n):
            return bc(ap.unsqueeze(1), P, n, ap.shape[1])

        S_BN, S_MV, S_VAR, S_RSTD = small[:, 0:24], small[:, 24:28], small[:, 28:60], small[:, 60:92]
        S_MX, S_NM, S_SUM, S_RS = small[:, 92:108], small[:, 108:124], small[:, 124:140], small[:, 140:156]
        S_SC, S_SEL, S_COMB = small[:, 160:192], small[:, 192:224], small[:, 224:256]
        S_GSC, S_GRANK, S_RANK = small[:, 256:264], small[:, 264:272], small[:, 272:304]
        S_BIG, S_BIG2 = small[:, 304:432], small[:, 432:560]
        S_KEY, S_C4, S_CG, S_CNT = small[:, 560:568], small[:, 568:576], small[:, 576:592], small[:, 592:596]
        S_CGS, S_KMAX = small[:, 596:600], small[:, 604:606]
        spill_info = ctx.enter_context(nc.sbuf_tensor("spill_info", [P, 2], mybir.dt.int32))[:, :]
        S_POOL = small[:, 608:610]
        S_MARK = small[:, 600:604]

        c1 = Carve()
        memT = c1(KD, T)
        rowa_sb = c1(NROWA)
        mem_at = c1.at
        kT, vmem = c1(4, T), c1(TT, MIX)
        base1 = c1.at
        qT = c1(4, T)
        catT = c1(KD, T)
        uT = c1(4, T)
        vv = c1(TT, MIX)
        cgT, tmpT = c1(4, T), c1(4, T)
        hpad = c1(4, T + 2)
        sgw = c1(4, P)
        xsc, xPT = c1(NHX, TT, T), c1(NHX, TT, T)
        bgT = uT
        ce = Carve(base1)
        xg = ce(NG, KD, P)
        og_at = ce.at
        og_spill = ce(D)
        og = ce(NG, D)
        og_flat = arena[:, og_at:ce.at]
        pick = ce(TT, NG, P)
        put = ce(TT, NG, P)
        put_spill = ce(TT, P)
        sg, hh = ce(F), ce(F)
        pick_r = reduced("pick_r", arena_at + 4 * ce.at, TT, NG * P)
        ce.at += TT * NG * P
        x_hi = [reduced(f"x_hi{tt}", arena_at + 4 * (og_at + D + tt * D), D) for tt in range(TT)]
        x_lo = [reduced(f"x_lo{tt}", arena_at + 4 * (og_at + 3 * D + tt * D), D) for tt in range(TT)]
        hT_at = ce.at
        hT_spill = ce(2, KM, P)
        ce.at += 2 * F
        hT_hi = [reduced(f"hT_hi{b}", arena_at + 4 * (hT_at + b * F), KM, P) for b in range(2)]
        hT_lo = [reduced(f"hT_lo{b}", arena_at + 4 * (hT_at + (2 + b) * F), KM, P) for b in range(2)]
        now_at = (0, ce.at)
        ce.at += 2 * KD * P
        assert ce.at <= ARENA
        now_hi = [reduced(f"now_hi{b}", arena_at + 4 * now_at[b], KD, P) for b in range(2)]
        now_lo = [reduced(f"now_lo{b}", arena_at + 4 * (now_at[b] + KD * P), KD, P) for b in range(2)]
        spill_now = v3(arena[:, 0:KD * P], KD)
        spill_w = (wide, xg.rearrange("p g k t -> p (g k t)"))
        split_at = (ring_at + 4 * RAW * HALF_SLOT, ring_at + 4 * (RAW * HALF_SLOT + SLOT), wide_at)
        w_hi = [reduced(f"w_hi{b}", split_at[b], HALF_SLOT) for b in range(SPLITS)]
        w_lo = [reduced(f"w_lo{b}", split_at[b] + 4 * HALF_SLOT, HALF_SLOT) for b in range(SPLITS)]

        c2 = Carve()
        gates = c2(2, 4, T)
        sh = c2(13, T)
        rlT, klT, vlT = sh[:, 0:4, :], sh[:, 4:8, :], sh[:, 8:12, :]
        norm_row = arena[:, mem_at:mem_at + D]
        assert mem_at + D <= base1 and mem_at + D <= c2.at
        lora_sb = c2(1152)
        wup, vdown, vup = lora_sb[:, 0:512], v3(lora_sb[:, 512:640], 4), lora_sb[:, 640:1152]
        wff_sb = c2(KD, NH)
        oT = c2(4, T)
        vfirst = c2(4, T)
        merged = y_nat
        base2 = c2.at
        ca = Carve(base2)
        pcol = ca(2, T + 1)
        cnat = ca(TT, LAT)
        dcol = v3(arena[:, ca.at - TT * LAT:ca.at - TT * LAT + 2 * T], 2)
        cT = ca(3, T)
        PT = v3(arena[:, ca.at - 3 * T:ca.at], 2)
        qn, kn = ca(TT, NH, QK), ca(TT, NH, QK)
        vn2 = [ca(TT, NH, HC), ca(TT, NH, HC)]
        qTt, kTt = ca(NH, T), ca(NH, T)
        Pm = ca(NH, 3 * P)
        ffn = ca(3 * TT * NH)
        sq = Pm.rearrange("p a b -> p (a b)")
        sgm = v3(qTt.rearrange("p a b -> p (a b)"), TT)
        cr = Carve(base2)
        t_at = cr.at
        lw, cum, pp, pinv, pex, aa, kk, km, t1 = (cr(4, P) for _ in range(9))
        ci = Carve(t_at)
        Tm, TTm, Xm, Nl = (ci(2, 4, P) for _ in range(4))
        rk = cr(4, P)
        tw = cr(P)
        NTm, MTm, AkT, AbT = (cr(2, 4, P) for _ in range(4))
        Vn, Kn, Rn, Bn, Kp = (cr(MIX) for _ in range(5))
        Hs = cr(2, MIX)
        states = [cr(MIX) for _ in range(3)]
        oT_c = cr(4, T)
        sgm_half = v3(arena[:, cr.at - 1024 - 3 * MIX - 2 * MIX - 4 * MIX:cr.at - 1024 - 3 * MIX - 2 * MIX - 2 * MIX], TT)
        pcs, pc0 = cr(8), cr(16)

        def flat2(ap):
            return ap.rearrange("p a b -> p (a b)")

        v_mid = flat2(t1)[0:32, 0:T]
        nuT = v3(arena[:, t_at + 5 * 512:t_at + 7 * 512], 4)
        vdiff = v3(arena[:, t_at:t_at + 2 * 512], 4)
        Wn, mv = flat2(Xm[:, 0, :, :]), flat2(Xm[:, 1, :, :])
        uv, yv = flat2(Nl[:, 0, :, :]), flat2(Nl[:, 1, :, :])
        QT = NTm
        GT = v4(MTm.rearrange("p a b c -> p (a b c)"), 2, NH)
        ysq = flat2(Tm[:, 0, :, :])

        def rowv(name):
            a, n = ROWS[name]
            return rows[:, a:a + n]

        def colv(l, which):
            a = 12 + l * CP_LAYER + 13 + 4 * which
            return col[:, a:a + 4]

        def hc(ap, h):
            return ap[:, h * HC:(h + 1) * HC]

        bank_full = [sem(f"bank_full{b}") for b in range(8)]
        bank_free = [sem(f"bank_free{b}") for b in range(8)]
        dve_step, act_step = sem("dve_step"), sem("act_step")

        class Counts:
            def __init__(self):
                self.seen, self.sent = {}, {}
                self.last, self.value = None, 0

            def next(self, name):
                self.seen[name] = self.seen.get(name, 0) + 1
                return self.seen[name]

            def sends(self, s):
                first = 1 if s in bank_free else 0
                self.sent[s.name] = self.sent.get(s.name, first) + 1
                self.last, self.value = s, self.sent[s.name]
                return 1

        class TensorCounts(Counts):
            def __init__(self):
                super().__init__()
                self.uses = [0] * 8
                self.slots = 0
                self.open = False
                self.pending = 0

            def reuse(self, b):
                self.uses[b] += 1
                return self.uses[b]

            def used(self, b):
                return self.uses[b] + 1

            def close(self):
                if self.open:
                    self.pending += 1
                    self.open = False

        block = ctx.enter_context(nc.Block())
        per_body = GS * PER_EXPERT

        @block.sync
        def _(sp):
            n = 0

            def load(src, width):
                nonlocal n
                if n >= RING:
                    sp.wait_ge(sem("ring_free"), n - RING + 1)
                s = n % RING
                sp.dma_start(ring[:, s * SLOT:s * SLOT + width], src).then_inc(sem(f"ring_full{s}"), 16)
                n += 1

            sp.dma_start(memT, memT0).then_inc(sem("memT_loaded"), 16)
            for i in range(DEPTH):
                at = 0
                for width in LOADS_FIRST[i]:
                    load((wfirst0, wfirst1)[i][:, at:at + width], width)
                    at += width
                    if n == 1:
                        sp.dma_start(xT, x0T).then_inc(sem("xT_loaded"), 16)
                    if n == RING:
                        sp.dma_start(x_nat, x0).then_inc(sem("x_loaded"), 16)
                sp.wait_ge(sem("ring_free"), n)
                with sp.Fori(0, NG // 2) as j:
                    for s in range(4 * per_body):
                        sp.wait_ge(sem("lo_ready"), j * (4 * per_body) + (LSIGS * i + s + 1))
                        r, half = s % RAW, s % 2
                        sp.dma_start(ring[:, r * HALF_SLOT:(r + 1) * HALF_SLOT],
                                     wmoe[i, j, s // 2, :, half * HALF_SLOT:(half + 1) * HALF_SLOT]).then_inc(sem(f"raw_full{r}"), 16)
                sp.wait_ge(sem("split_free"), USIGS * (i + 1))
                sp.wait_ge(sem("spill_known"), i + 1)
                spilt = sp.value_load(spill_info[0:1, 0:1], min_val=0, max_val=NG)
                group = sp.value_load(spill_info[0:1, 1:2], min_val=0, max_val=NG - 1)
                with sp.If(spilt > 0):
                    for s in range(per_body):
                        if s == 1:
                            sp.wait_ge(sem(f"spill{i}_gathered"), 1)
                        elif s:
                            sp.wait_ge(sem(f"spill{i}_ring_free"), s - 1)
                        sp.dma_start(spill_w[s % 2], wspill[i, bass.ds(group, 1), s, :, :]).then_inc(sem(f"spill{i}_ring_full{s % 2}"), 16)
            for l in range(DEPTH):
                at = 0
                for width in LOADS_SECOND:
                    load(wsecond[l, :, at:at + width], width)
                    at += width
            sp.wait_ge(sem("x_ready"), 2 * DEPTH + DEPTH)
            sp.dma_start(out, x_nat).then_inc(sem("out_stored"), 16)
            sp.wait_ge(sem("out_stored"), 16)

        @block.gpsimd
        def _(pool):
            pool.wait_ge(sem("ring_full1"), 16)
            pool.dma_start(cst, consts).then_inc(sem("cst_loaded"), 16)
            pool.dma_start(sgw, sguT).then_inc(sem("par_loaded"), 16)
            pool.dma_start(rowa_sb, rowa[0, :].partition_broadcast(P)).then_inc(sem("par_loaded"), 16)
            pool.dma_start(col, colp).then_inc(sem("par_loaded"), 16)
            pool.dma_start(rwt, rw).then_inc(sem("par_loaded"), 16)
            for n in range(2 * DEPTH):
                if n:
                    pool.wait_ge(sem("x_ready"), n)
                pool.dma_start(rows[:, 0:2 * D], lnrows[n, :].partition_broadcast(P)).then_inc(sem("rows_loaded"), 16)
                if n % 2 == 0:
                    i = n // 2
                    pool.wait_ge(sem("h_ready"), HSIGS * i + 1)
                    pool.wait_ge(sem("silu_done"), HSIGS * i + 1)
                    nc.gpsimd.memset(S_POOL[:, 0:1], 0.0).then_inc(sem("tokens_ready"), 1)
                    for g in range(1, NG):
                        pool.wait_ge(sem("h_ready"), HSIGS * i + 1 + GS * (g - 1))
                        nc.gpsimd.tensor_copy(now_hi[g % 2], xg[:, g, :, :]).then_inc(sem("pool_step"), 1)
                        pool.wait_ge(sem("pool_step"), (NG - 1) * i + g)
                        nc.gpsimd.tensor_tensor(now_lo[g % 2], xg[:, g, :, :], now_hi[g % 2], SUB).then_inc(sem("tokens_ready"), 1)
            for l in range(DEPTH):
                if l == 0:
                    pool.wait_ge(sem("x_ready"), 2 * DEPTH - 1)
                else:
                    pool.wait_ge(sem("y_ready"), TT * l)
                pool.dma_start(norm_row, rows2[l, 0:D].partition_broadcast(P)).then_inc(sem("norm_loaded"), 16)
                pool.wait_ge(sem("x_ready"), 2 * DEPTH + l)
                pool.dma_start(rows[:, D:NROWS], rows2[l, D:NROWS].partition_broadcast(P)).then_inc(sem("rows_loaded"), 16)
                pool.dma_start(lora_sb, lora[l, :, :]).then_inc(sem("lora_loaded"), 16)
                pool.dma_start(wff_sb, wff[l, :, :, :]).then_inc(sem("lora_loaded"), 16)

        @block.tensor
        def _(pe_eng):
            pe = TensorCounts()

            def mark(ins, full):
                if full is not None:
                    ins.then_inc(bank_full[full], 1)
                elif pe.pending:
                    pe.pending -= 1
                    ins.then_inc(sem("ring_free"), 1)

            def mm(o, lhsT, rhs, start=True, stop=True, full=None, loose=False):
                mark(nc.tensor.matmul(o, lhsT, rhs, start=start, stop=stop, skip_group_check=loose), full)

            def tr(o, i, full=None):
                mark(nc.tensor.transpose(o, i, ident), full)

            def slot(width=SLOT):
                pe.close()
                n = pe.slots
                pe.slots, pe.open = n + 1, True
                pe_eng.wait_ge(sem(f"ring_full{n % RING}"), 16 * (n // RING + 1))
                return ring[:, (n % RING) * SLOT:(n % RING) * SLOT + width]

            def transpose_tokens(src, first, second):
                for g, b in enumerate((0, 5, 1, 6)):
                    tt, half = g // 2, g % 2
                    if g == 0:
                        pe_eng.wait_ge(sem(first), pe.next(first))
                    elif g == 2 and second != first:
                        pe_eng.wait_ge(sem(second), pe.next(second))
                    pe_eng.wait_ge(bank_free[b], pe.reuse(b))
                    bank = banks[b]
                    for k in range(4):
                        tr(bank[:, k * P:(k + 1) * P], src[:, tt, (4 * half + k) * P:(4 * half + k + 1) * P],
                           full=b if k == 3 else None)
                pe_eng.wait_ge(bank_free[0], pe.used(0))
                pe_eng.wait_ge(bank_free[5], pe.used(5))
                pe_eng.wait_ge(bank_free[1], pe.used(1))
                pe_eng.wait_ge(bank_free[6], pe.used(6))

            def proj_T(w, rhsT, bs, tiles=4):
                for m in range(tiles):
                    b = bs[m // 2]
                    if m % 2 == 0:
                        pe_eng.wait_ge(bank_free[b], pe.reuse(b))
                        bank = banks[b]
                    for k in range(KD):
                        end = k == KD - 1 and (m % 2 == 1 or m == tiles - 1)
                        mm(bank[:, (m % 2) * T:(m % 2 + 1) * T], w[:, k, m * P:(m + 1) * P], rhsT[:, k, :],
                           start=k == 0, stop=k == KD - 1, full=b if end else None)

            def proj(w, lT, bs, n=512, kt=KD, at=0):
                for tt in range(TT):
                    pe_eng.wait_ge(bank_free[bs[tt]], pe.reuse(bs[tt]))
                    bank = banks[bs[tt]]
                    for k in range(kt):
                        mm(bank[:, 0:n], lT[:, k, tt * P:(tt + 1) * P], w[:, k, at:at + n], start=k == 0, stop=k == kt - 1,
                           full=bs[tt] if k == kt - 1 else None)

            def wslot():
                return v3(slot(), KD)

            pe_eng.wait_ge(sem("memT_loaded"), 16)
            for i in range(DEPTH):
                if i == 0:
                    proj_T(wslot(), memT, (0, 5))
                    pe_eng.wait_ge(sem("xT_loaded"), 16)
                else:
                    transpose_tokens(x_nat, "x_first", "x_ready")
                proj_T(wslot(), xT, (2, 3))
                pe_eng.wait_ge(bank_free[0], pe.used(0))
                pe_eng.wait_ge(bank_free[2], pe.used(2))
                pe_eng.wait_ge(bank_free[3], pe.used(3))
                pe_eng.wait_ge(bank_free[5], pe.used(5))
                for h in range(NHX):
                    pe_eng.wait_ge(bank_free[h], pe.reuse(h))
                    bank = banks[h]
                    for tt in range(TT):
                        mm(bank[:, tt * T:(tt + 1) * T], qT[:, h, tt * P:(tt + 1) * P], kT[:, h, :],
                           full=h if tt else None)
                if i == 0:
                    proj_T(wslot(), xT, (5, 6))
                    proj(wslot(), xT, (7, 5))
                    proj(wslot(), memT, (1, 6))
                    pe_eng.wait_ge(sem("cst_loaded"), 16)
                    pe_eng.wait_ge(sem("sgu_v_ready"), TT)
                    pe_eng.wait_ge(sem("sgu_w_ready"), pe.next("sgu_w_ready"))
                    for c in range(TT):
                        pe_eng.wait_ge(bank_free[c], pe.reuse(c))
                        bank = banks[c]
                        for h in range(4):
                            mm(bank[:, h * P:(h + 1) * P], vv[:, c, h * P:(h + 1) * P], sgw[:, h, :],
                               full=c if h == 3 else None)
                    proj_T(wslot(), memT, (5, 6))
                else:
                    proj_T(wslot(), xT, (5, 6))
                    proj_T(wslot(), xT, (7, 5))
                    proj_T(wslot(), xT, (0, 1))
                pe.close()

                def turn_px(h):
                    pe_eng.wait_ge(sem("p_ready"), pe.next("p_ready"))
                    b = 5 + h % 3
                    pe_eng.wait_ge(bank_free[b], pe.reuse(b))
                    for m in range(TT):
                        for tt in range(TT):
                            tr(banks[b][:, m * T + tt * P:m * T + (tt + 1) * P], xsc[:, h, tt, m * P:(m + 1) * P],
                               full=b if m and tt else None)

                turn_px(0)
                for h in range(NHX):
                    if h + 1 < NHX:
                        turn_px(h + 1)
                    if h == 0:
                        pe_eng.wait_ge(bank_free[1], pe.used(1))
                    pe_eng.wait_ge(bank_free[5 + h % 3], pe.used(5 + h % 3))
                    b = (4, 2)[h % 2]
                    pe_eng.wait_ge(bank_free[b], pe.reuse(b))
                    for m in range(TT):
                        mm(banks[b][:, 0:T], vmem[:, m, h * P:(h + 1) * P], xPT[:, h, m, :], start=m == 0, stop=m == 1,
                           full=b if m else None)
                pe_eng.wait_ge(bank_free[0], pe.used(0))
                pe_eng.wait_ge(bank_free[1], pe.used(1))
                pe_eng.wait_ge(bank_free[2], pe.used(2))
                pe_eng.wait_ge(bank_free[3], pe.used(3))
                pe_eng.wait_ge(bank_free[4], pe.used(4))
                pe_eng.wait_ge(sem("tok_ready"), pe.next("tok_ready"))
                for n in range(2):
                    proj(wslot(), catT, (n, 2 + n))
                if i + 1 < DEPTH:
                    proj(wslot(), memT, (7, 5))
                pe.close()
                transpose_tokens(x_nat, "x_first", "x_ready")
                if i == 0:
                    pe_eng.wait_ge(sem("par_loaded"), 64)
                pe_eng.wait_ge(bank_free[5], pe.reuse(5))
                bank = banks[5]
                for tt in range(TT):
                    for k in range(KD):
                        mm(bank[:, tt * NE:(tt + 1) * NE], xT[:, k, tt * P:(tt + 1) * P], rwt[:, k, :],
                           start=k == 0, stop=k == KD - 1, full=5 if tt and k == KD - 1 else None)
                pe_eng.wait_ge(sem("group_ready"), pe.next("group_ready"))
                pe_eng.wait_ge(bank_free[0], pe.reuse(0))
                bank = banks[0]
                chosen = [S_GRANK[:, tt * NG:(tt + 1) * NG] for tt in range(TT)]
                nc.tensor.matmul(bank[:, 0:NG], mat(C_TRI), chosen[0], start=True, stop=True).then_inc(sem("split_free"), SPLITS)
                for at, second in ((NG, C_TRI), (2 * NG, C_ONES)):
                    mm(bank[:, at:at + NG], mat(C_ONES), chosen[0], stop=False)
                    mm(bank[:, at:at + NG], mat(second), chosen[1], start=False, full=0 if at > NG else None)
                pe_eng.wait_ge(sem("slots_ready"), pe.next("slots_ready"))
                for k, b in enumerate((0, 5, 1, 6, 2, 7, 3, 5)):
                    pe_eng.wait_ge(bank_free[b], pe.reuse(b))
                    for tt in range(TT):
                        mm(banks[b][:, :], x_hi[tt][:, k * P:(k + 1) * P], pick_r[:, tt, :], start=tt == 0, stop=False)
                        mm(banks[b][:, :], x_lo[tt][:, k * P:(k + 1) * P], pick_r[:, tt, :], start=False, stop=tt == 1,
                           full=b if tt else None)
                pe_eng.wait_ge(sem("comb_ready"), pe.next("comb_ready"))
                pe_eng.wait_ge(bank_free[4], pe.reuse(4))
                for g in range(NG):
                    for tt in range(TT):
                        mm(banks[4][:, g * GS:(g + 1) * GS], pick[:, tt, g, :], S_C4[:, tt * GS:(tt + 1) * GS],
                           start=tt == 0, stop=tt == 1, full=4 if tt and g == NG - 1 else None)
                for tt in range(TT):
                    b = 6 + tt
                    pe_eng.wait_ge(bank_free[b], pe.reuse(b))
                    for g in range(NG):
                        tr(banks[b][:, g * P:(g + 1) * P], pick[:, tt, g, :], full=b if g == NG - 1 else None)
                pe_eng.wait_ge(sem("spill_known"), i + 1)
                spilt = pe_eng.value_load(spill_info[0:1, 0:1], min_val=0, max_val=NG)
                for b in range(8):
                    pe_eng.wait_ge(bank_free[b], pe.used(b))

                def split_products(j, par):
                    one = j * (2 * GS) + (HSIGS * i + GS * par + 1)
                    place = [0]

                    def unit():
                        u = place[0]
                        place[0] += 1
                        pe_eng.wait_ge(sem("lo_ready"), j * (4 * per_body) + (LSIGS * i + RAW + 2 * per_body * par + u + 1))
                        return w_hi[u % SPLITS], w_lo[u % SPLITS]

                    def free_before(ins):
                        if place[0] > 1:
                            ins.then_inc(sem("split_free"), 1)

                    def three(o, hi, lo, k, whi, wlo, first, last):
                        a = nc.tensor.matmul(o, hi[:, k, :], whi, start=first, stop=False)
                        nc.tensor.matmul(o, hi[:, k, :], wlo, start=False, stop=False)
                        return a, nc.tensor.matmul(o, lo[:, k, :], whi, start=False, stop=last)

                    def hidden(bank):
                        for half in range(2):
                            whi, wlo = unit()
                            for k in range(KM):
                                cols = slice(k * F, (k + 1) * F)
                                a, ins = three(bank[:, :], now_hi[par], now_lo[par], KM * half + k, whi[:, cols], wlo[:, cols],
                                               half == 0 and k == 0, half == 1 and k == KM - 1)
                                if k == 0:
                                    free_before(a)
                        return ins

                    def gate(e):
                        if e == 0:
                            pe_eng.wait_ge(sem("tokens_ready"), j * 2 + (TSIGS * i + par + 1))
                        pe_eng.wait_ge(sem("silu_done"), one + e)
                        hidden(banks[5]).then_inc(sem("gate_full"), 1)

                    def up(e):
                        pe_eng.wait_ge(sem("h_ready"), one + e)
                        hidden(banks[4]).then_inc(sem("up_full"), 1)

                    def turn(e):
                        pe_eng.wait_ge(sem("h_ready"), one + (e + 1))
                        for k in range(KM):
                            ins = nc.tensor.transpose(banks[6][:, k * P:(k + 1) * P], hh[:, k * P:(k + 1) * P], ident)
                        ins.then_inc(sem("hT_full"), 1)

                    def down(e, half):
                        if half == 0:
                            pe_eng.wait_ge(sem("hT_ready"), j * (2 * GS) + (NE * i + GS * par + e + 1))
                            if e == 0:
                                pe_eng.wait_ge(sem("og_ready"), j * 4 + (GSIGS * i + 2 * par + 2))
                        whi, wlo = unit()
                        for n in range(2):
                            for k in range(KM // 2):
                                cols = slice(k * D + n * 512, k * D + (n + 1) * 512)
                                kt = KM // 2 * half + k
                                a, ins = three(banks[(7, 3)[n]][:, :], hT_hi[e % 2], hT_lo[e % 2], kt, whi[:, cols], wlo[:, cols],
                                               e == 0 and kt == 0, e == GS - 1 and kt == KM - 1)
                                if n == 0 and k == 0:
                                    free_before(a)
                        if e == GS - 1 and half == 1:
                            ins.then_inc(sem("split_free"), 1)

                    gate(0)
                    up(0)
                    for e in range(1, GS):
                        gate(e)
                        turn(e - 1)
                        up(e)
                        down(e - 1, 0)
                        if e == GS - 1:
                            turn(e)
                        down(e - 1, 1)
                    down(GS - 1, 0)
                    down(GS - 1, 1)

                def spill_products(kind, slot_ready):
                    one = 1

                    def gate(e):
                        w = slot_ready(GROUP_SLOTS.index(("gate", e)), KD)
                        if e == 0:
                            pe_eng.wait_ge(sem(kind + "tokens_ready"), 1)
                        pe_eng.wait_ge(sem(kind + "silu_done"), one + e)
                        for k in range(KD):
                            ins = nc.tensor.matmul(banks[5][:, :], spill_now[:, k, :], w[:, k, :], start=k == 0, stop=k == KD - 1)
                            if e == 1 and k == 0:
                                ins.then_inc(sem(kind + "ring_free"), 1)
                        ins.then_inc(sem(kind + "gate_full"), 1)

                    def up(e):
                        w = slot_ready(GROUP_SLOTS.index(("up", e)), KD)
                        pe_eng.wait_ge(sem(kind + "h_ready"), one + e)
                        for k in range(KD):
                            ins = nc.tensor.matmul(banks[4][:, :], spill_now[:, k, :], w[:, k, :], start=k == 0, stop=k == KD - 1)
                            if e == 0 and k == 0:
                                ins.then_inc(sem(kind + "ring_free"), 1)
                        ins.then_inc(sem(kind + "up_full"), 1)

                    def turn(e):
                        pe_eng.wait_ge(sem(kind + "h_ready"), one + (e + 1))
                        for k in range(KM):
                            ins = nc.tensor.transpose(banks[6][:, k * P:(k + 1) * P], hh[:, k * P:(k + 1) * P], ident)
                            if e < GS - 1 and k == 0:
                                ins.then_inc(sem(kind + "ring_free"), 1)
                        ins.then_inc(sem(kind + "hT_full"), 1)

                    def down(e, n):
                        if n == 0:
                            down.w = slot_ready(GROUP_SLOTS.index(("down", e)), KM)
                            pe_eng.wait_ge(sem(kind + "hT_ready"), e + 1)
                        for k in range(KM):
                            ins = nc.tensor.matmul(banks[(7, 3)[n]][:, :], hT_spill[:, e % 2, k, :], down.w[:, k, n * 512:(n + 1) * 512],
                                                   start=e == 0 and k == 0, stop=e == GS - 1 and k == KM - 1)
                            if n == 0 and k == 0 and e < GS - 1:
                                ins.then_inc(sem(kind + "ring_free"), 1)
                        if n == 1:
                            ins.then_inc(sem(kind + "ring_free"), 1)
                        elif e == GS - 1:
                            ins.then_inc(sem(kind + "down_full"), 1)

                    gate(0)
                    up(0)
                    for e in range(1, GS):
                        gate(e)
                        turn(e - 1)
                        up(e)
                        down(e - 1, 0)
                        if e == GS - 1:
                            turn(e)
                        down(e - 1, 1)
                    down(GS - 1, 0)
                    down(GS - 1, 1)

                pe_eng.wait_ge(sem("first_tokens"), i + 1)
                with pe_eng.Fori(0, NG // 2) as j:
                    split_products(j, 0)
                    split_products(j, 1)
                pe_eng.wait_ge(sem("og_ready"), GSIGS * (i + 1))
                with pe_eng.If(spilt > 0):
                    kind = f"spill{i}_"
                    pe_eng.wait_ge(sem(kind + "slots_ready"), 1)
                    for k in range(KD):
                        for tt in range(TT):
                            nc.tensor.matmul(banks[4 + k // 4][:, (k % 4) * P:(k % 4 + 1) * P], x_nat[:, tt, k * P:(k + 1) * P],
                                             pick[:, tt, 0, :], start=tt == 0, stop=tt == 1)
                    for tt in range(TT):
                        nc.tensor.matmul(banks[6][:, 0:GS], pick[:, tt, 0, :], S_C4[:, tt * GS:(tt + 1) * GS], start=tt == 0, stop=tt == 1)
                    for tt in range(TT):
                        ins = nc.tensor.transpose(banks[7][:, tt * P:(tt + 1) * P], pick[:, tt, 0, :], ident)
                    ins.then_inc(sem(kind + "gathered"), 1)
                    def spill_slot(s, kt):
                        pe_eng.wait_ge(sem(f"spill{i}_ring_full{s % 2}"), 16 * (s // 2 + 1))
                        return v3(spill_w[s % 2], kt)

                    spill_products(kind, spill_slot)
                    pe_eng.wait_ge(sem(kind + "og0_ready"), 1)
                    pe_eng.wait_ge(sem(kind + "og1_ready"), 1)

                for b in range(4):
                    pe_eng.wait_ge(bank_free[b], pe.reuse(b))
                    for g in range(NG - 1 - b // 2):
                        mm(banks[b][:, :], put[:, b // 2, g, :], og[:, g, (b % 2) * 512:(b % 2 + 1) * 512], start=g == 0, stop=False, loose=True)
                with pe_eng.If(spilt > 0):
                    for b in range(4):
                        nc.tensor.matmul(banks[b][:, :], put_spill[:, b // 2, :], og_spill[:, (b % 2) * 512:(b % 2 + 1) * 512],
                                         start=False, stop=False, skip_group_check=True)
                for b in range(4):
                    for g in range(NG - 1 - b // 2, NG):
                        mm(banks[b][:, :], put[:, b // 2, g, :], og[:, g, (b % 2) * 512:(b % 2 + 1) * 512], start=False,
                           full=b if g == NG - 1 else None, loose=True)

            def turn_qk(kdim):
                pe_eng.wait_ge(sem("qk_ready"), pe.next("qk_ready"))
                for src, bs in ((qn, (0, 1, 5, 6)), (kn, (2, 3, 7, 5))):
                    for g in range(4):
                        tt, hg = g // 2, g % 2
                        pe_eng.wait_ge(bank_free[bs[g]], pe.reuse(bs[g]))
                        bank = banks[bs[g]]
                        for h in range(4):
                            tr(bank[0:kdim, h * P:(h + 1) * P], src[:, tt, hg * 4 + h, 0:kdim], full=bs[g] if h == 3 else None)
                pe_eng.wait_ge(bank_free[0], pe.used(0))
                pe_eng.wait_ge(bank_free[1], pe.used(1))
                pe_eng.wait_ge(bank_free[2], pe.used(2))
                pe_eng.wait_ge(bank_free[3], pe.used(3))
                pe_eng.wait_ge(bank_free[5], pe.used(5))
                pe_eng.wait_ge(bank_free[6], pe.used(6))
                pe_eng.wait_ge(bank_free[7], pe.used(7))

            def scores(kdim):
                for h in range(NH):
                    b = h % NDB
                    pe_eng.wait_ge(bank_free[b], pe.reuse(b))
                    bank = banks[b]
                    mm(bank[:, 0:P], qTt[0:kdim, h, 0:P], kTt[0:kdim, h, 0:P])
                    mm(bank[:, P:3 * P], qTt[0:kdim, h, P:T], kTt[0:kdim, h, :], full=b)

            def apply(vn):
                def turn_p(h):
                    if h % 4 == 0:
                        pe_eng.wait_ge(sem("p_ready"), pe.next("p_ready"))
                    b = 5 + h % 2
                    pe_eng.wait_ge(bank_free[b], pe.reuse(b))
                    for t in range(3):
                        tr(banks[b][:, t * P:(t + 1) * P], Pm[:, h, t * P:(t + 1) * P], full=b if t == 2 else None)

                turn_p(0)
                for h in range(NH):
                    if h + 1 < NH:
                        turn_p(h + 1)
                    pe_eng.wait_ge(bank_free[5 + h % 2], pe.used(5 + h % 2))
                    ob = h // 2
                    if h % 2 == 0:
                        pe_eng.wait_ge(bank_free[ob], pe.reuse(ob))
                    o = banks[ob][HC * (h % 2):HC * (h % 2) + HC, :]
                    mm(o[:, 0:T], vn[:, 0, h, :], PT[:, h % 2, 0:T], stop=False, loose=True)
                    mm(o[:, P:T], vn[:, 1, h, :], PT[:, h % 2, T:T + P], start=False, full=ob if h % 2 else None, loose=True)

            def merge_values(oT):
                w = v3(slot(), KM)
                pe_eng.wait_ge(bank_free[0], pe.used(0))
                pe_eng.wait_ge(bank_free[1], pe.used(1))
                pe_eng.wait_ge(bank_free[2], pe.used(2))
                pe_eng.wait_ge(bank_free[3], pe.used(3))
                for n in range(2):
                    proj(w, oT, (n, 2 + n), kt=KM, at=n * 512)

            def merge_gates():
                for n in range(2):
                    proj(wslot(), xT, (5, 6))

            for l in range(DEPTH):
                transpose_tokens(y_nat, "h_first", "h_ready2")
                proj(v3(slot(KD * LAT), KD), xT, (0, 1), n=LAT)
                pe_eng.wait_ge(sem("lora_loaded"), 32 * (l + 1))
                pe_eng.wait_ge(bank_free[4], pe.reuse(4))
                bank = banks[4]
                for tt in range(TT):
                    for k in range(KD):
                        mm(bank[:, tt * NH:(tt + 1) * NH], xT[:, k, tt * P:(tt + 1) * P], wff_sb[:, k, :],
                           start=k == 0, stop=k == KD - 1, full=4 if tt and k == KD - 1 else None)
                proj_T(wslot(), xT, (5, 6))
                proj_T(wslot(), xT, (5, 6))
                pe_eng.wait_ge(sem("lat_ready"), pe.next("lat_ready"))
                for b, at, n in ((2, 0, 2), (3, 2, 1)):
                    pe_eng.wait_ge(bank_free[b], pe.reuse(b))
                    bank = banks[b]
                    for k in range(n):
                        for tt in range(TT):
                            tr(bank[:, k * T + tt * P:k * T + (tt + 1) * P], cnat[:, tt, (at + k) * P:(at + k + 1) * P],
                               full=b if tt and k == n - 1 else None)
                pe_eng.wait_ge(bank_free[2], pe.used(2))
                pe_eng.wait_ge(bank_free[3], pe.used(3))
                w = v3(slot(1536), 2)
                for n in range(2):
                    for tt in range(TT):
                        b = 2 * n + tt
                        pe_eng.wait_ge(bank_free[b], pe.reuse(b))
                        bank = banks[b]
                        for k in range(2):
                            mm(bank[:, 0:4 * QK], cT[:, k, tt * P:(tt + 1) * P], w[:, k, n * 4 * QK:(n + 1) * 4 * QK],
                               start=k == 0, stop=k == 1, full=b if k else None)
                w = slot(1024)
                for n in range(2):
                    for tt in range(TT):
                        b = 5 + (2 * n + tt) % 3
                        pe_eng.wait_ge(bank_free[b], pe.reuse(b))
                        bank = banks[b]
                        mm(bank[:, 0:256], cT[:, 2, tt * P:(tt + 1) * P], w[:, n * 512:n * 512 + 256])
                        mm(bank[:, 256:512], cT[:, 2, tt * P:(tt + 1) * P], w[:, n * 512 + 256:(n + 1) * 512], full=b)
                proj_T(wslot(), xT, (5, 6))
                turn_qk(QK)
                scores(QK)
                pe_eng.wait_ge(sem("logf_ready"), pe.next("logf_ready"))
                lf = ffn[:, 0:TT * NH]
                pe_eng.wait_ge(bank_free[4], pe.reuse(4))
                bank = banks[4]
                mm(bank[:, 0:NH], mat(C_TRI), lf[:, 0:NH])
                mm(bank[:, NH:2 * NH], mat(C_ONES), lf[:, 0:NH], stop=False)
                mm(bank[:, NH:2 * NH], mat(C_TRI), lf[:, NH:2 * NH], start=False, full=4)
                proj(wslot(), xT, (0, 1))
                proj(wslot(), xT, (2, 3))
                proj(wslot(), xT, (5, 6))
                proj_T(wslot(), xT, (5, 6))
                apply(vn2[0])
                proj_T(wslot(), xT, (5, 6))
                proj_T(v3(slot(KD * P), KD), xT, (7,), tiles=1)
                turn_qk(FOXK)
                scores(FOXK)
                merge_values(oT)
                merge_gates()
                if l:
                    pe_eng.wait_ge(sem("shift_ready"), pe.next("shift_ready"))
                    pe_eng.wait_ge(bank_free[4], pe.reuse(4))
                    bank = banks[4]
                    for k in range(4):
                        mm(bank[0:32, 0:T], vdown[:, k, :], vlT[:, k, :], start=k == 0, stop=k == 3, full=4 if k == 3 else None)
                proj_T(wslot(), xT, (5, 6))
                if l:
                    pe_eng.wait_ge(bank_free[4], pe.used(4))
                    for g in range(2):
                        pe_eng.wait_ge(bank_free[g], pe.reuse(g))
                        bank = banks[g]
                        for j in range(2):
                            mm(bank[:, j * T:(j + 1) * T], vup[0:32, (2 * g + j) * P:(2 * g + j + 1) * P], v_mid,
                               full=g if j else None)
                apply(vn2[1])

                def values_b(n):
                    w = v3(slot(SLOT // 2), KM)
                    pe_eng.wait_ge(bank_free[0], pe.used(0))
                    pe_eng.wait_ge(bank_free[1], pe.used(1))
                    pe_eng.wait_ge(bank_free[2], pe.used(2))
                    pe_eng.wait_ge(bank_free[3], pe.used(3))
                    proj(w, oT, (3, 4), kt=KM)

                def turn_y():
                    pe_eng.wait_ge(sem("y_ready"), pe.next("y_ready"))
                    pe_eng.wait_ge(bank_free[0], pe.reuse(0))
                    for j in range(4):
                        tr(banks[0][:, j * P:(j + 1) * P], yv[:, j * P:(j + 1) * P], full=0 if j == 3 else None)

                values_b(0)
                for tt in range(TT):
                    tok = slice(tt * P, (tt + 1) * P)
                    if tt:
                        values_b(1)
                        turn_y()
                    pe_eng.wait_ge(sem("tw_ready"), pe.next("tw_ready"))
                    pe_eng.wait_ge(bank_free[0], pe.reuse(0))
                    bank = banks[0]
                    for j in range(4):
                        mm(bank[:, j * P:(j + 1) * P], wup[0:64, j * P:(j + 1) * P], tw[0:64, :], full=0 if j == 3 else None)
                    pe_eng.wait_ge(bank_free[1], pe.reuse(1))
                    bank = banks[1]
                    for j in range(4):
                        mm(bank[:, j * P:(j + 1) * P], wup[64:128, j * P:(j + 1) * P], sh[64:128, 12, tok], full=1 if j == 3 else None)
                    pe_eng.wait_ge(sem("ksq_ready"), pe.next("ksq_ready"))
                    pe_eng.wait_ge(bank_free[2], pe.reuse(2))
                    bank = banks[2]
                    mm(bank[:, :], mat(C_BLOCK), flat2(t1), full=2)
                    proj(wslot(), xT, (5, 6))
                    pe_eng.wait_ge(sem("rows_ready"), pe.next("rows_ready"))
                    for par in range(2):
                        hs = slice(64 * par, 64 * par + 64)
                        for b, left, right in ((0, aa, pex), (1, pinv, pex), (2, pinv, pp), (3, aa, pp)):
                            pe_eng.wait_ge(bank_free[b], pe.reuse(b))
                            bank = banks[b]
                            for j in range(4):
                                mm(bank[:, j * P:(j + 1) * P], left[hs, j, :], right[hs, j, :], full=b if j == 3 else None)
                    pe_eng.wait_ge(bank_free[4], pe.reuse(4))
                    bank = banks[4]
                    pe_eng.wait_ge(sem("ends_ready"), pe.next("ends_ready"))
                    for j in range(4):
                        mm(bank[:, 0:NH], rk[:, j, :], cst[:, C_SEL + j * NH:C_SEL + (j + 1) * NH], start=j == 0, stop=j == 3)
                    for par in range(2):
                        mm(bank[0:64, 64 + 8 * par:72 + 8 * par], mat(C_ID)[:, 64 * par:64 * par + 64], pcs, full=4 if par else None)
                    for b, src in ((5, vlT[:, :, tok]), (6, pex), (7, pp), (5, cum), (3, lw)):
                        pe_eng.wait_ge(bank_free[b], pe.reuse(b))
                        bank = banks[b]
                        for j in range(4):
                            tr(bank[:, j * P:(j + 1) * P], src[:, j, :], full=b if j == 3 else None)
                    for par in range(2):
                        pe_eng.wait_ge(sem("level_ready"), pe.next("level_ready"))
                        pe_eng.wait_ge(bank_free[par], pe.reuse(par))
                        bank = banks[par]
                        for j in range(4):
                            tr(bank[:, j * P:(j + 1) * P], TTm[:, par, j, :], full=par if j == 3 else None)
                    for lev in range(1, LEVELS):
                        for par in range(2):
                            pe_eng.wait_ge(sem("level_ready"), pe.next("level_ready"))
                            b = 5 + par
                            pe_eng.wait_ge(bank_free[b], pe.reuse(b))
                            bank = banks[b]
                            for j in range(4):
                                mm(bank[:, j * P:(j + 1) * P], Nl[:, par, j, :], Tm[:, par, j, :], full=b if j == 3 else None)
                        for par in range(2):
                            pe_eng.wait_ge(bank_free[5 + par], pe.used(5 + par))
                            if lev < LEVELS - 1:
                                pe_eng.wait_ge(bank_free[2 * par], pe.reuse(2 * par))
                                bank = banks[2 * par]
                                for j in range(4):
                                    mm(bank[:, j * P:(j + 1) * P], TTm[:, par, j, :], Xm[:, par, j, :], full=2 * par if j == 3 else None)
                            pe_eng.wait_ge(bank_free[2 * par + 1], pe.reuse(2 * par + 1))
                            bank = banks[2 * par + 1]
                            for j in range(4):
                                mm(bank[:, j * P:(j + 1) * P], Xm[:, par, j, :], TTm[:, par, j, :], full=2 * par + 1 if j == 3 else None)
                    pe_eng.wait_ge(bank_free[1], pe.used(1))
                    pe_eng.wait_ge(bank_free[3], pe.used(3))
                    pe_eng.wait_ge(bank_free[5], pe.used(5))
                    pe_eng.wait_ge(bank_free[6], pe.used(6))
                    pe_eng.wait_ge(bank_free[7], pe.used(7))
                    pe_eng.wait_ge(bank_free[2], pe.reuse(2))
                    bank = banks[2]
                    for h in range(NH):
                        mm(hc(bank, h), TTm[:, h % 2, h // 2, :], hc(Kn, h), full=2 if h == NH - 1 else None)
                    pe_eng.wait_ge(bank_free[3], pe.reuse(3))
                    bank = banks[3]
                    for h in range(NH):
                        mm(hc(bank, h), MTm[:, h % 2, h // 2, :], hc(Vn, h), full=3 if h == NH - 1 else None)
                    pe_eng.wait_ge(bank_free[3], pe.used(3))
                    pe_eng.wait_ge(bank_free[4], pe.reuse(4))
                    bank = banks[4]
                    for h in range(NH):
                        mm(hc(bank, h), TTm[:, h % 2, h // 2, :], hc(mv, h), full=4 if h == NH - 1 else None)
                    pe_eng.wait_ge(bank_free[2], pe.used(2))
                    pe_eng.wait_ge(bank_free[4], pe.used(4))
                    chunks = (0, 1) if tt == 0 else (0,)
                    for c in chunks:
                        rowsc = slice(64 * c, 64 * c + 64)
                        if 2 * tt + c:
                            pe_eng.wait_ge(bank_free[c], pe.reuse(c))
                            bank = banks[c]
                            for h in range(NH):
                                mm(hc(bank[0:64, :], h), hc(Wn[rowsc, :], h), hc(Bn[rowsc, :], h), full=c if h == NH - 1 else None)
                        pe_eng.wait_ge(bank_free[2 + c], pe.reuse(2 + c))
                        bank = banks[2 + c]
                        for h in range(NH):
                            mm(hc(bank[0:64, :], h), hc(Kp[rowsc, :], h), hc(Vn[rowsc, :], h), stop=False)
                            mm(hc(bank[0:64, :], h), hc(Bn[rowsc, :], h), hc(uv[rowsc, :], h), start=False, full=2 + c if h == NH - 1 else None)
                    for par in range(2):
                        b = 5 + par
                        pe_eng.wait_ge(bank_free[b], pe.reuse(b))
                        bank = banks[b]
                        for j in range(4):
                            h = 2 * j + par
                            mm(bank[0:64, j * P:(j + 1) * P], hc(Rn, h), ident, stop=False)
                            mm(bank[0:64, j * P:(j + 1) * P], hc(Wn, h), AbT[:, par, j, :], start=False, full=b if j == 3 else None)
                    for c in chunks:
                        g = 2 * tt + c
                        if g == 0:
                            continue
                        pe_eng.wait_ge(bank_free[c], pe.used(c))
                        pe_eng.wait_ge(bank_free[2], pe.used(2))
                        pe_eng.wait_ge(bank_free[3], pe.used(3))
                        pe_eng.wait_ge(bank_free[4], pe.used(4))
                        pe_eng.wait_ge(bank_free[4], pe.reuse(4))
                        bank = banks[4]
                        for h in range(NH):
                            mm(hc(bank[0:64, :], h), GT[0:64, c, h, :], hc(states[g - 1][0:64, :], h), full=4 if h == NH - 1 else None)
                    pe_eng.wait_ge(bank_free[5], pe.used(5))
                    pe_eng.wait_ge(bank_free[6], pe.used(6))
                    pe_eng.wait_ge(bank_free[4], pe.reuse(4))
                    bank = banks[4]
                    for h in range(NH):
                        par, j = h % 2, h // 2
                        o = hc(bank, h)
                        mm(o, AkT[:, par, j, :], hc(Vn, h), stop=False, loose=True)
                        mm(o, AbT[:, par, j, :], hc(uv, h), start=False, stop=False, loose=True)
                        for c in range(2):
                            g = 2 * tt + c
                            if g:
                                mm(o[64 * c:64 * c + 64, :], QT[0:64, par, j, c * CH:(c + 1) * CH], hc(states[g - 1][0:64, :], h),
                                   start=False, full=4 if h == NH - 1 and c else None, loose=True)
                merge_gates()
                turn_y()
                merge_values(oT_c)
                transpose_tokens(merged, "merged_ready", "merged_ready")
                for n in range(2):
                    proj(wslot(), xT, (n, 2 + n))
                pe.close()

        @block.scalar
        def _(act_eng):
            act = Counts()
            act.shifts = 0

            def copy_out(o, b, bank_ap, func=ACT.Copy):
                act_eng.wait_ge(bank_full[b], act.next(("full", b)))
                nc.scalar.activation(o, bank_ap, func).then_inc(bank_free[b], act.sends(bank_free[b]))

            def roots(n):
                act_eng.wait_ge(sem("var_ready"), act.next("var_ready"))
                nc.scalar.activation(S_VAR[:, 0:n], S_VAR[:, 0:n], ACT.Sqrt).then_inc(sem("std_ready"), act.sends(sem("std_ready")))

            def turned_x():
                for g, b in ((1, 5), (3, 6)):
                    copy_out(xT[:, 4:8, (g // 2) * P:(g // 2 + 1) * P], b, v3(banks[b][:, :], 4))

            def two_tiles(dst, b, m, func=ACT.Copy):
                copy_out(dst[:, 2 * m:2 * m + 2, :], b, v3(banks[b][:, :], 2), func)

            for i in range(DEPTH):
                if i:
                    turned_x()
                else:
                    two_tiles(kT, 5, 1)
                for h in range(NHX):
                    act_eng.wait_ge(sem("max_ready"), act.next("max_ready"))
                    for tt in range(TT):
                        ins = nc.scalar.activation(xsc[:, h, tt, :], xsc[:, h, tt, :], ACT.Exp, bias=S_NM[:, h * TT + tt:h * TT + tt + 1],
                                                   scale=XSCALE, accum_out=S_SUM[:, h * TT + tt:h * TT + tt + 1])
                    ins.then_inc(sem("exp_done"), act.sends(sem("exp_done")))
                if i == 0:
                    two_tiles(uT, 5, 0, ACT.Gelu)
                    two_tiles(uT, 6, 1, ACT.Gelu)
                    copy_out(vv[:, 0, :], 7, banks[7][:, :], ACT.Gelu)
                    copy_out(vv[:, 1, :], 5, banks[5][:, :], ACT.Gelu)
                    act_eng.wait_ge(act.last, act.value)
                    nc.scalar.activation(S_MARK[:, 0:1], vv[:, 1, 0:1], ACT.Copy).then_inc(sem("gelu_done"), act.sends(sem("gelu_done")))
                    roots(2)
                    copy_out(vmem[:, 1, :], 6, banks[6][:, :])
                    two_tiles(kT, 5, 0)
                    two_tiles(kT, 6, 1)
                else:
                    two_tiles(bgT, 5, 0)
                    two_tiles(bgT, 6, 1)
                    two_tiles(cgT, 7, 0)
                    two_tiles(cgT, 5, 1)
                    act_eng.wait_ge(act.last, act.value)
                    nc.scalar.activation(S_MARK[:, 0:1], cgT[:, 3, 0:1], ACT.Copy).then_inc(sem("gelu_done"), act.sends(sem("gelu_done")))
                for h in range(NHX):
                    b = 5 + h % 3
                    copy_out(xPT[:, h, :, :], b, v3(banks[b][:, :], 2))
                roots(2)
                if i + 1 < DEPTH:
                    for tt, b in ((0, 7), (1, 5)):
                        copy_out(vmem[:, tt, :], b, banks[b][:, :])
                turned_x()
                act_eng.wait_ge(bank_full[5], act.next(("full", 5)))
                nc.scalar.activation(S_SC, banks[5][:, 0:TT * NE], ACT.Sigmoid).then_inc(bank_free[5], act.sends(bank_free[5]))
                act_eng.wait_ge(act.last, act.value)
                nc.scalar.activation(S_MARK[:, 1:2], S_SC[:, 0:1], ACT.Copy).then_inc(sem("scores_ready"), act.sends(sem("scores_ready")))
                for tt in range(TT):
                    nc.scalar.activation(x_hi[tt], x_nat[:, tt, :], ACT.Copy).then_inc(sem("x_hi_ready"), 1)
                nc.scalar.activation(S_MARK[:, 2:3], S_SC[:, 0:1], ACT.Silu).then_inc(act_step, act.sends(act_step))
                for k, b in ((1, 5), (3, 6), (5, 7), (7, 5)):
                    copy_out(xg[:, :, k, :], b, v3(banks[b][:, :], NG))
                act_eng.wait_ge(act.last, act.value)
                nc.scalar.activation(S_MARK[:, 2:3], S_SC[:, 0:1], ACT.Copy).then_inc(sem("silu_done"), 1)
                act_eng.wait_ge(sem("h_ready"), HSIGS * i + 1)
                nc.scalar.activation(now_hi[0], xg[:, 0, :, :], ACT.Copy).then_inc(sem("first_hi"), 1)
                for tt in range(TT):
                    copy_out(put[:, tt, :, :], 6 + tt, v3(banks[6 + tt][:, :], NG))

                def split_gates(j, par):
                    before = j * (2 * GS) + (NE * i + GS * par)
                    units = j * (4 * per_body) + (USIGS * i + 2 * per_body * par)

                    def high(u):
                        r = u % RAW
                        act_eng.wait_ge(sem(f"raw_full{r}"), j * (16 * per_body) + 16 * (UNITS // RAW * i + 2 * per_body // RAW * par + u // RAW + 1))
                        act_eng.wait_ge(sem("split_free"), units + (u + 1))
                        nc.scalar.activation(w_hi[u % SPLITS], ring[:, r * HALF_SLOT:(r + 1) * HALF_SLOT],
                                             ACT.Copy).then_inc(sem("hi_ready"), 1)

                    def silu(e):
                        act_eng.wait_ge(sem("gate_full"), before + (e + 1))
                        act_eng.wait_ge(sem("h_ready"), before + (i + 1 + e))
                        nc.scalar.activation(sg, banks[5][:, :], ACT.Silu).then_inc(sem("silu_done"), 1)

                    def turned(e):
                        act_eng.wait_ge(sem("hT_full"), before + (e + 1))
                        nc.scalar.activation(hT_hi[e % 2], v3(banks[6][:, :], KM), ACT.Copy).then_inc(sem("hT_hi_ready"), 1)

                    def sums_before(e):
                        nc.scalar.activation(og_flat[:, bass.ds(j * (2 * D) + par * D, 512)], banks[7][:, :], ACT.Copy).then_inc(sem("og_ready"), 1)

                    steps = {4: ((silu, 0), (sums_before, 0)), 8: ((silu, 1), (turned, 0)), 14: ((silu, 2), (turned, 1)),
                             20: ((silu, 3), (turned, 2)), 23: ((turned, 3),)}
                    for u in range(2 * per_body):
                        for step, e in steps.get(u, ()):
                            step(e)
                        high(u)

                with act_eng.Fori(0, NG // 2) as j:
                    split_gates(j, 0)
                    split_gates(j, 1)
                act_eng.wait_ge(sem("split_free"), USIGS * (i + 1))
                nc.scalar.activation(og_flat[:, NG * D:NG * D + 512], banks[7][:, :], ACT.Copy).then_inc(sem("og_ready"), 1)

                act_eng.wait_ge(sem("spill_known"), i + 1)
                spilt = act_eng.value_load(spill_info[0:1, 0:1], min_val=0, max_val=NG)

                def spill_gates(kind, sums):
                    for e in range(GS):
                        act_eng.wait_ge(sem(kind + "gate_full"), e + 1)
                        act_eng.wait_ge(sem(kind + "h_ready"), e + 1)
                        nc.scalar.activation(sg, banks[5][:, :], ACT.Silu).then_inc(sem(kind + "silu_done"), 1)
                        if e:
                            act_eng.wait_ge(sem(kind + "hT_full"), e)
                            nc.scalar.activation(hT_spill[:, (e - 1) % 2, :, :], v3(banks[6][:, :], KM), ACT.Copy).then_inc(sem(kind + "hT_ready"), 1)
                    act_eng.wait_ge(sem(kind + "hT_full"), GS)
                    nc.scalar.activation(hT_spill[:, (GS - 1) % 2, :, :], v3(banks[6][:, :], KM), ACT.Copy).then_inc(sem(kind + "hT_ready"), 1)
                    act_eng.wait_ge(sem(kind + "down_full"), 1)
                    nc.scalar.activation(sums, banks[7][:, :], ACT.Copy).then_inc(sem(kind + "og0_ready"), 1)

                with act_eng.If(spilt > 0):
                    kind = f"spill{i}_"
                    act_eng.wait_ge(sem(kind + "gathered"), 1)
                    for half in range(2):
                        nc.scalar.activation(spill_now[:, 4 * half:4 * half + 4, :], v3(banks[4 + half][:, :], 4), ACT.Copy).then_inc(sem(kind + "copied"), 1)
                    nc.scalar.activation(S_CGS, banks[6][:, 0:GS], ACT.Copy).then_inc(sem(kind + "copied"), 1)
                    nc.scalar.activation(S_MARK[:, 2:3], S_SC[:, 0:1], ACT.Silu).then_inc(sem(kind + "silu_done"), 1)
                    nc.scalar.activation(put_spill, v3(banks[7][:, 0:T], TT), ACT.Copy).then_inc(sem(kind + "tokens_ready"), 1)
                    spill_gates(kind, og_spill[:, 0:512])
                roots(2)

            def shifted_in(n):
                for m in range(2):
                    act_shift(5 + m, 2)

            def act_shift(b, tiles):
                if act.shifts:
                    act_eng.wait_ge(sem("shift_done"), act.next("shift_done"))
                act.shifts += 1
                act_eng.wait_ge(bank_full[b], act.next(("full", b)))
                nc.scalar.activation(pcol[:, 0:tiles, 1:T + 1], v3(banks[b][:, 0:tiles * T], tiles), ACT.Copy).then_inc(bank_free[b], act.sends(bank_free[b]))
                act_eng.wait_ge(act.last, act.value)
                nc.scalar.activation(S_MARK[:, 0:1], pcol[:, tiles - 1, T:T + 1], ACT.Copy).then_inc(sem("shift_in"), act.sends(sem("shift_in")))

            def silu_gate(g):
                for m in range(2):
                    two_tiles(gates[:, g, :, :], 5 + m, m, ACT.Silu)

            def turned_qk(kdim):
                for dst, g, b in ((qTt, 2, 5), (qTt, 3, 6), (kTt, 2, 7), (kTt, 3, 5)):
                    hg = g % 2
                    copy_out(dst[0:kdim, 4 * hg:4 * hg + 4, P:T], b, v3(banks[b][0:kdim, :], 4))

            def softmax():
                for half in range(2):
                    act_eng.wait_ge(sem("max_ready"), act.next("max_ready"))
                    for h in range(4):
                        for tt in range(TT):
                            at = half * 8 + tt * 4 + h
                            span = Pm[:, half * 4 + h, 0:P] if tt == 0 else Pm[:, half * 4 + h, P:3 * P]
                            ins = nc.scalar.activation(span, span, ACT.Exp, bias=S_NM[:, at:at + 1], accum_out=S_SUM[:, at:at + 1])
                    ins.then_inc(sem("exp_done"), act.sends(sem("exp_done")))

            def turned_p():
                for h in range(NH):
                    b = 5 + h % 2
                    copy_out(PT[:, h % 2, :], b, banks[b][:, 0:3 * P])

            def merge_sigmoid():
                for n in range(2):
                    for tt in range(TT):
                        copy_out(sgm[:, tt, n * 512:(n + 1) * 512], 5 + tt, banks[5 + tt][:, :], ACT.Sigmoid)
                act_eng.wait_ge(act.last, act.value)
                nc.scalar.activation(S_MARK[:, 0:1], sgm[:, 1, D - 1:D], ACT.Copy).then_inc(sem("sgm_ready"), act.sends(sem("sgm_ready")))

            for l in range(DEPTH):
                act_eng.wait_ge(sem("x_first"), 2 * DEPTH + l)
                nc.scalar.activation(y_nat[:, 0, :], x_nat[:, 0, :], ACT.Square, accum_out=S_VAR[:, 0:1]).then_inc(sem("first_squares"), 1)
                roots(2)
                turned_x()
                silu_gate(0)
                roots(6)
                shifted_in(0)
                act_eng.wait_ge(sem("gates_neg"), act.next("gates_neg"))
                lfe = ffn[:, TT * NH:2 * TT * NH]
                nc.scalar.activation(lfe, lfe, ACT.Exp).then_inc(act_step, act.sends(act_step))
                act_eng.wait_ge(act.last, act.value)
                nc.scalar.activation(lfe, lfe, ACT.Ln, bias=1.0).then_inc(sem("gates_ln"), act.sends(sem("gates_ln")))
                for n in range(2):
                    for tt in range(TT):
                        b = 5 + (2 * n + tt) % 3
                        act_eng.wait_ge(bank_full[b], act.next(("full", b)))
                        kv = v3(banks[b][:, :], 4)
                        nc.scalar.activation(kn[:, tt, 4 * n:4 * n + 4, 0:NOPE], kv[:, :, 0:NOPE], ACT.Copy).then_inc(act_step, act.sends(act_step))
                        nc.scalar.activation(vn2[0][:, tt, 4 * n:4 * n + 4, :], kv[:, :, NOPE:P], ACT.Copy).then_inc(bank_free[b], act.sends(bank_free[b]))
                act_eng.wait_ge(act.last, act.value)
                nc.scalar.activation(S_MARK[:, 0:1], vn2[0][:, 1, 7, 0:1], ACT.Copy).then_inc(sem("kv_ready"), act.sends(sem("kv_ready")))
                roots(32)
                shifted_in(1)
                turned_qk(QK)
                softmax()
                for tt in range(TT):
                    copy_out(vn2[1][:, tt, :, :], 5 + tt, v3(banks[5 + tt][:, :], NH))
                silu_gate(1)
                roots(32)
                turned_p()
                shifted_in(2)
                act_shift(7, 1)
                turned_qk(FOXK)
                softmax()
                merge_sigmoid()
                silu_gate(0)
                if l:
                    act_eng.wait_ge(sem("nu_in"), act.next("nu_in"))
                    nc.scalar.activation(nuT, nuT, ACT.Sigmoid).then_inc(sem("nu_ready"), act.sends(sem("nu_ready")))
                turned_p()
                for tt in range(TT):
                    tok = slice(tt * P, (tt + 1) * P)
                    act_eng.wait_ge(sem("shift_all"), act.next("shift_all"))
                    nc.scalar.activation(tw[0:64, :], sh[0:64, 12, tok], ACT.Tanh).then_inc(sem("tw_ready"), act.sends(sem("tw_ready")))
                    act_eng.wait_ge(sem("wa_in"), act.next("wa_in"))
                    nc.scalar.activation(flat2(lw), flat2(lw), ACT.Sigmoid).then_inc(act_step, act.sends(act_step))
                    nc.scalar.activation(flat2(aa), flat2(aa), ACT.Sigmoid).then_inc(sem("wa_ready"), act.sends(sem("wa_ready")))
                    act_eng.wait_ge(sem("ksum_ready"), act.next("ksum_ready"))
                    nc.scalar.activation(flat2(t1), flat2(t1), ACT.Sqrt).then_inc(sem("knorm_ready"), act.sends(sem("knorm_ready")))
                    act_eng.wait_ge(sem("cum_ready"), act.next("cum_ready"))
                    nc.scalar.activation(flat2(pp), flat2(cum), ACT.Exp).then_inc(act_step, act.sends(act_step))
                    nc.scalar.activation(flat2(pinv), flat2(cum), ACT.Exp, scale=-1.0).then_inc(act_step, act.sends(act_step))
                    nc.scalar.activation(flat2(pex), flat2(pex), ACT.Exp).then_inc(sem("decay_ready"), act.sends(sem("decay_ready")))
                    for half in range(TT):
                        copy_out(sgm_half[:, half, :], 5 + half, banks[5 + half][:, :], ACT.Sigmoid)
                    act_eng.wait_ge(act.last, act.value)
                    nc.scalar.activation(S_MARK[:, 0:1], sgm_half[:, 1, 0:1], ACT.Copy).then_inc(sem("sgm_ready"), act.sends(sem("sgm_ready")))
                    copy_out(Vn, 5, banks[5][:, :])
                    act_eng.wait_ge(sem("half_merged"), act.next("half_merged"))
                    for b, dst in ((6, Kn), (7, Rn), (5, Bn)):
                        copy_out(dst, b, banks[b][:, :])
                    for lev in range(1, LEVELS):
                        for par in range(2):
                            copy_out(Xm[:, par, :, :], 5 + par, v3(banks[5 + par][:, :], 4))
                    for par in range(2):
                        copy_out(QT[0:64, par, :, :], 5 + par, v3(banks[5 + par][0:64, :], 4))
                    roots(8)
                merge_sigmoid()
                turned_x()

        @block.vector
        def _(dve_eng):
            dve = Counts()
            v = nc.vector
            for b in range(8):
                v.memset(banks[b][:, 0:1], 0.0).then_inc(bank_free[b], 1)

            def copy_out(o, b, bank_ap):
                dve_eng.wait_ge(bank_full[b], dve.next(("full", b)))
                v.tensor_copy(o, bank_ap).then_inc(bank_free[b], dve.sends(bank_free[b]))

            def turned_x():
                for g, b in ((0, 0), (2, 1)):
                    copy_out(xT[:, 0:4, (g // 2) * P:(g // 2 + 1) * P], b, v3(banks[b][:, :], 4))

            def roots(n):
                dve_eng.wait_ge(sem("std_ready"), dve.next("std_ready"))
                v.reciprocal(S_RSTD[:, 0:n], S_VAR[:, 0:n]).then_inc(dve_step, dve.sends(dve_step))
                dve_eng.wait_ge(dve.last, dve.value)

            def tile_stats(src, tt):
                n = src.shape[2] // 512
                dve_eng.wait_ge(dve.last, dve.value)
                for s in range(n):
                    v.bn_stats(S_BN[:, (tt * n + s) * 6:(tt * n + s + 1) * 6], src[:, tt, s * 512:(s + 1) * 512]).then_inc(dve_step, dve.sends(dve_step))

            def mean_var(n):
                dve_eng.wait_ge(dve.last, dve.value)
                for tt in range(TT):
                    v.bn_aggr(S_MV[:, 2 * tt:2 * tt + 2], S_BN[:, tt * n * 6:(tt + 1) * n * 6]).then_inc(dve_step, dve.sends(dve_step))
                dve_eng.wait_ge(dve.last, dve.value)
                v.tensor_scalar(S_VAR[:, 0:TT], S_MV[:, 1:4:2], LN_EPS, None, ADD).then_inc(sem("var_ready"), dve.sends(sem("var_ready")))

            def layer_norm(src, dst, g, b, first, end):
                mean_var(src.shape[2] // 512)
                for tt in range(TT):
                    v.scalar_tensor_tensor(src[:, tt, :], src[:, tt, :], S_MV[:, 2 * tt:2 * tt + 1], g, SUB, MUL).then_inc(dve_step, dve.sends(dve_step))
                roots(TT)
                v.scalar_tensor_tensor(dst[:, 0, :], src[:, 0, :], S_RSTD[:, 0:1], b, MUL, ADD).then_inc(sem(first), dve.sends(sem(first)))
                v.scalar_tensor_tensor(dst[:, 1, :], src[:, 1, :], S_RSTD[:, 1:2], b, MUL, ADD).then_inc(sem(end), dve.sends(sem(end)))

            def two_tiles(dst, b, m):
                copy_out(dst[:, 2 * m:2 * m + 2, :], b, v3(banks[b][:, :], 2))

            for i in range(DEPTH):
                if i:
                    turned_x()
                if i == 0:
                    two_tiles(kT, 0, 0)
                for m in range(2):
                    two_tiles(qT, 2 + m, m)
                for h in range(NHX):
                    copy_out(xsc[:, h, :, :], h, v3(banks[h][:, :], 2))
                    dve_eng.wait_ge(dve.last, dve.value)
                    v.tensor_reduce(S_MX[:, 2 * h:2 * h + 2], xsc[:, h, :, :], AX, MAX).then_inc(dve_step, dve.sends(dve_step))
                    dve_eng.wait_ge(dve.last, dve.value)
                    v.tensor_scalar(S_NM[:, 2 * h:2 * h + 2], S_MX[:, 2 * h:2 * h + 2], -XSCALE, None, MUL).then_inc(sem("max_ready"), dve.sends(sem("max_ready")))
                for h in range(NHX):
                    dve_eng.wait_ge(sem("exp_done"), dve.next("exp_done"))
                    v.reciprocal(S_RS[:, 2 * h:2 * h + 2], S_SUM[:, 2 * h:2 * h + 2]).then_inc(dve_step, dve.sends(dve_step))
                    dve_eng.wait_ge(dve.last, dve.value)
                    v.tensor_tensor(xsc[:, h, :, :], xsc[:, h, :, :], per_channel(S_RS[:, 2 * h:2 * h + 2], T), MUL).then_inc(sem("p_ready"), dve.sends(sem("p_ready")))
                if i == 0:
                    dve_eng.wait_ge(sem("cst_loaded"), 16)
                    dve_eng.wait_ge(sem("par_loaded"), 64)
                    v.tensor_tensor(S_BIG, mat(C_TRI), mat(C_BLOCK), MAX).then_inc(dve_step, dve.sends(dve_step))
                    dve_eng.wait_ge(dve.last, dve.value)
                    v.tensor_tensor(sgw, sgw, bc(S_BIG.unsqueeze(1), P, 4, P), MUL).then_inc(sem("sgu_w_ready"), dve.sends(sem("sgu_w_ready")))
                    dve_eng.wait_ge(sem("gelu_done"), dve.next("gelu_done"))
                    for tt in range(TT):
                        tile_stats(vv, tt)
                    layer_norm(vv, vv, rowa_sb[:, R_SGUG:R_SGUG + MIX], rowa_sb[:, R_SGUB:R_SGUB + MIX], "sgu_v_ready", "sgu_v_ready")
                    copy_out(vmem[:, 0, :], 1, banks[1][:, :])
                    for c in range(TT):
                        dve_eng.wait_ge(bank_full[c], dve.next(("full", c)))
                        t = tmpT[:, :, c * P:(c + 1) * P]
                        v.tensor_tensor(t, v3(banks[c][:, :], 4), v3(rowa_sb[:, R_SGUBIAS:R_SGUBIAS + 512], 4), ADD).then_inc(bank_free[c], dve.sends(bank_free[c]))
                    dve_eng.wait_ge(dve.last, dve.value)
                    v.tensor_tensor(catT[:, 0:4, :], uT, tmpT, MUL).then_inc(sem("tok_ready"), dve.sends(sem("tok_ready")))
                    for h in range(NHX):
                        copy_out(catT[:, 4 + h, :], (4, 2)[h % 2], banks[(4, 2)[h % 2]][:, 0:T])
                else:
                    v.memset(hpad[:, :, 0:2], 0.0).then_inc(dve_step, dve.sends(dve_step))
                    dve_eng.wait_ge(dve.last, dve.value)
                    dve_eng.wait_ge(sem("gelu_done"), dve.next("gelu_done"))
                    for m in range(2):
                        dve_eng.wait_ge(bank_full[m], dve.next(("full", m)))
                        v.tensor_tensor(hpad[:, 2 * m:2 * m + 2, 2:], cgT[:, 2 * m:2 * m + 2, :], v3(banks[m][:, :], 2), MUL).then_inc(bank_free[m], dve.sends(bank_free[m]))
                    dve_eng.wait_ge(dve.last, dve.value)
                    for k in range(4):
                        cw = col[:, 3 * k:3 * k + 3]
                        v.tensor_scalar(tmpT[:, k, :], hpad[:, k, 0:T], cw[:, 0:1], None, MUL).then_inc(dve_step, dve.sends(dve_step))
                        for tap in range(1, 3):
                            dve_eng.wait_ge(dve.last, dve.value)
                            v.scalar_tensor_tensor(tmpT[:, k, :], hpad[:, k, tap:tap + T], cw[:, tap:tap + 1], tmpT[:, k, :], MUL, ADD).then_inc(dve_step, dve.sends(dve_step))
                        copy_out(catT[:, 4 + k, :], (4, 2)[k % 2], banks[(4, 2)[k % 2]][:, 0:T])
                    dve_eng.wait_ge(dve.last, dve.value)
                    v.tensor_tensor(catT[:, 0:4, :], bgT, tmpT, MUL).then_inc(sem("tok_ready"), dve.sends(sem("tok_ready")))
                if i == 0:
                    dve_eng.wait_ge(sem("x_loaded"), 16)
                for n in range(2):
                    for tt in range(TT):
                        b = n + 2 * tt
                        dve_eng.wait_ge(bank_full[b], dve.next(("full", b)))
                        v.scalar_tensor_tensor(y_nat[:, tt, n * 512:(n + 1) * 512], x_nat[:, tt, n * 512:(n + 1) * 512], ALPHA,
                                                        banks[b][:, :], MUL, ADD).then_inc(bank_free[b], dve.sends(bank_free[b]))
                        if n:
                            tile_stats(y_nat, tt)
                dve_eng.wait_ge(sem("rows_loaded"), 16 * (2 * i + 1))
                layer_norm(y_nat, x_nat, rows[:, 0:D], rows[:, D:2 * D], "x_first", "x_ready")
                turned_x()
                v.memset(S_BIG2[:, 1:2], 0.0).then_inc(sem("lo_ready"), RAW)
                dve_eng.wait_ge(sem("scores_ready"), dve.next("scores_ready"))
                sel4 = v3(S_SEL, TT * NG)
                v.tensor_tensor(v3(S_SEL, TT), v3(S_SC, TT), per_column(rowa_sb[:, R_RB:R_RB + NE], TT), ADD).then_inc(dve_step, dve.sends(dve_step))
                dve_eng.wait_ge(dve.last, dve.value)
                pairs = v3(S_BIG[:, 0:48], TT * NG)
                v.tensor_tensor(pairs[:, :, 0:3], sel4[:, :, 1:4], bc(sel4[:, :, 0:1], P, TT * NG, 3), ADD).then_inc(dve_step, dve.sends(dve_step))
                v.tensor_tensor(pairs[:, :, 3:5], sel4[:, :, 2:4], bc(sel4[:, :, 1:2], P, TT * NG, 2), ADD).then_inc(dve_step, dve.sends(dve_step))
                v.tensor_tensor(pairs[:, :, 5:6], sel4[:, :, 3:4], sel4[:, :, 2:3], ADD).then_inc(dve_step, dve.sends(dve_step))
                dve_eng.wait_ge(dve.last, dve.value)
                v.tensor_reduce(S_GSC, pairs, AX, MAX).then_inc(dve_step, dve.sends(dve_step))
                dve_eng.wait_ge(dve.last, dve.value)

                def ranks(vals, a, dst):
                    other = bc(vals.unsqueeze(2), P, a, GS, GS)
                    own = bc(vals.unsqueeze(3), P, a, GS, GS)
                    n = a * GS * GS
                    gt, eq = S_BIG[:, 0:n], S_BIG2[:, 0:n]
                    v.tensor_tensor(v4(gt, a, GS), other, own, ALU.is_gt).then_inc(dve_step, dve.sends(dve_step))
                    v.tensor_tensor(v4(eq, a, GS), other, own, ALU.is_equal).then_inc(dve_step, dve.sends(dve_step))
                    dve_eng.wait_ge(dve.last, dve.value)
                    v.tensor_tensor(v3(eq, a), v3(eq, a), per_column(cst[:, C_TIE:C_TIE + GS * GS], a), MUL).then_inc(dve_step, dve.sends(dve_step))
                    dve_eng.wait_ge(dve.last, dve.value)
                    v.tensor_tensor(gt, gt, eq, ADD).then_inc(dve_step, dve.sends(dve_step))
                    dve_eng.wait_ge(dve.last, dve.value)
                    v.tensor_reduce(dst, v3(gt, a * GS), AX, ADD).then_inc(dve_step, dve.sends(dve_step))
                    dve_eng.wait_ge(dve.last, dve.value)

                ranks(v3(S_GSC, TT), TT, S_GRANK)
                v.tensor_scalar(S_GRANK, S_GRANK, 0.5, None, ALU.is_lt).then_inc(sem("group_ready"), dve.sends(sem("group_ready")))
                ranks(sel4, TT * NG, S_RANK)
                v.tensor_scalar(S_RANK, S_RANK, 1.5, None, ALU.is_lt).then_inc(dve_step, dve.sends(dve_step))
                for tt in range(TT):
                    dve_eng.wait_ge(sem("x_hi_ready"), TT * i + tt + 1)
                    v.tensor_tensor(x_lo[tt], x_nat[:, tt, :], x_hi[tt], SUB).then_inc(dve_step, dve.sends(dve_step))
                dve_eng.wait_ge(bank_full[0], dve.next(("full", 0)))
                v.tensor_tensor(S_KEY, banks[0][:, 0:TT * NG], S_GRANK, MUL).then_inc(dve_step, dve.sends(dve_step))
                v.tensor_scalar(S_CNT, banks[0][:, TT * NG:TT * NG + NG], P + 0.5, None, ALU.is_gt).then_inc(bank_free[0], dve.sends(bank_free[0]))
                dve_eng.wait_ge(dve.last, dve.value)
                chosen = pick_r.rearrange("p a (g t) -> p (a g) t", g=NG)
                v.tensor_tensor(chosen, per_column(cst[:, C_IOTA:C_IOTA + P], TT * NG), per_channel(S_KEY, P),
                                ALU.is_equal).then_inc(sem("slots_ready"), dve.sends(sem("slots_ready")))
                v.tensor_tensor(pick.rearrange("p a g t -> p (a g) t"), per_column(cst[:, C_IOTA:C_IOTA + P], TT * NG), per_channel(S_KEY, P),
                                ALU.is_equal).then_inc(dve_step, dve.sends(dve_step))
                v.tensor_tensor(v3(S_RANK, TT * NG), v3(S_RANK, TT * NG), per_channel(S_GRANK, GS), MUL).then_inc(dve_step, dve.sends(dve_step))
                dve_eng.wait_ge(dve.last, dve.value)
                v.tensor_tensor(S_COMB, S_SC, S_RANK, MUL).then_inc(dve_step, dve.sends(dve_step))
                dve_eng.wait_ge(dve.last, dve.value)
                v.tensor_reduce(v3(S_C4, TT), v4(S_COMB, TT, NG).rearrange("p a g e -> p a e g"), AX, ADD).then_inc(dve_step, dve.sends(dve_step))
                dve_eng.wait_ge(dve.last, dve.value)
                v.tensor_reduce(S_RS[:, 0:TT], v3(S_C4, TT), AX, ADD).then_inc(dve_step, dve.sends(dve_step))
                dve_eng.wait_ge(dve.last, dve.value)
                v.reciprocal(S_RS[:, 0:TT], S_RS[:, 0:TT]).then_inc(dve_step, dve.sends(dve_step))
                dve_eng.wait_ge(dve.last, dve.value)
                v.tensor_tensor(v3(S_C4, TT), v3(S_C4, TT), per_channel(S_RS[:, 0:TT], GS), MUL).then_inc(sem("comb_ready"), dve.sends(sem("comb_ready")))
                v.tensor_tensor(S_CNT, S_CNT, cst[:, C_IOTA:C_IOTA + NG], MUL).then_inc(dve_step, dve.sends(dve_step))
                dve_eng.wait_ge(dve.last, dve.value)
                v.tensor_reduce(S_CNT[:, 0:1], S_CNT, AX, ADD).then_inc(dve_step, dve.sends(dve_step))
                dve_eng.wait_ge(dve.last, dve.value)
                v.tensor_copy(spill_info[:, 0:1], S_CNT[:, 0:1]).then_inc(dve_step, dve.sends(dve_step))
                v.tensor_scalar(S_CNT[:, 1:2], S_CNT[:, 0:1], -1.0, 0.0, ADD, MAX).then_inc(dve_step, dve.sends(dve_step))
                dve_eng.wait_ge(dve.last, dve.value)
                v.tensor_copy(spill_info[:, 1:2], S_CNT[:, 1:2]).then_inc(sem("spill_known"), dve.sends(sem("spill_known")))
                for k, b in ((0, 0), (2, 1), (4, 2), (6, 3)):
                    copy_out(xg[:, :, k, :], b, v3(banks[b][:, :], NG))
                copy_out(S_CG, 4, banks[4][:, 0:NE])
                dve_eng.wait_ge(dve.last, dve.value)
                v.tensor_copy(S_BIG[:, 0:1], S_CG[:, 0:1]).then_inc(sem("h_ready"), 1)
                dve_eng.wait_ge(sem("silu_done"), HSIGS * i + 1)
                dve_eng.wait_ge(sem("first_hi"), i + 1)
                v.tensor_tensor(now_lo[0], xg[:, 0, :, :], now_hi[0], SUB).then_inc(sem("first_tokens"), 1)

                def split_sums(j, par):
                    before = j * (2 * GS) + (NE * i + GS * par)
                    units = j * (4 * per_body) + (UNITS * i + 2 * per_body * par)

                    def low(u):
                        r = u % RAW
                        dve_eng.wait_ge(sem("hi_ready"), units + (u + 1))
                        v.tensor_tensor(w_lo[u % SPLITS], ring[:, r * HALF_SLOT:(r + 1) * HALF_SLOT],
                                        w_hi[u % SPLITS], SUB).then_inc(sem("lo_ready"), 1)

                    def hidden(e):
                        dve_eng.wait_ge(sem("up_full"), before + (e + 1))
                        dve_eng.wait_ge(sem("silu_done"), before + (i + 2 + e))
                        v.scalar_tensor_tensor(hh, banks[4][:, :], S_CG[:, bass.ds(j * (2 * GS) + (GS * par + e), 1)], sg, MUL, MUL).then_inc(sem("h_ready"), 1)

                    def turned(e):
                        dve_eng.wait_ge(sem("hT_hi_ready"), before + (e + 1))
                        v.tensor_tensor(hT_lo[e % 2], v3(banks[6][:, :], KM), hT_hi[e % 2], SUB).then_inc(sem("hT_ready"), 1)

                    def sums_before(e):
                        v.tensor_copy(og_flat[:, bass.ds(j * (2 * D) + (par * D + 512), 512)], banks[3][:, :]).then_inc(sem("og_ready"), 1)

                    steps = {6: (hidden, 0), 7: (sums_before, 0), 8: (turned, 0), 10: (hidden, 1), 14: (turned, 1), 16: (hidden, 2), 20: (turned, 2),
                             22: (hidden, 3), 23: (turned, 3)}
                    for u in range(2 * per_body):
                        if u in steps:
                            step, e = steps[u]
                            step(e)
                        low(u)

                def spill_sums(kind, sums):
                    for e in range(GS):
                        dve_eng.wait_ge(sem(kind + "up_full"), e + 1)
                        dve_eng.wait_ge(sem(kind + "silu_done"), e + 2)
                        v.scalar_tensor_tensor(hh, banks[4][:, :], S_CGS[:, e:e + 1], sg, MUL, MUL).then_inc(sem(kind + "h_ready"), 1)
                    dve_eng.wait_ge(sem(kind + "ring_free"), per_body)
                    v.tensor_copy(sums, banks[3][:, :]).then_inc(sem(kind + "og1_ready"), 1)

                with dve_eng.Fori(0, NG // 2) as j:
                    split_sums(j, 0)
                    split_sums(j, 1)
                dve_eng.wait_ge(sem("split_free"), USIGS * (i + 1))
                v.tensor_copy(og_flat[:, NG * D + 512:(NG + 1) * D], banks[3][:, :]).then_inc(sem("og_ready"), 1)
                dve_eng.wait_ge(sem("spill_known"), i + 1)
                spilt = dve_eng.value_load(spill_info[0:1, 0:1], min_val=0, max_val=NG)
                with dve_eng.If(spilt > 0):
                    kind = f"spill{i}_"
                    v.tensor_reduce(S_KMAX, v3(S_KEY, TT), AX, MAX).then_inc(sem(kind + "places"), 1)
                    dve_eng.wait_ge(sem(kind + "places"), 1)
                    v.tensor_tensor(pick[:, :, 0, :], per_column(cst[:, C_IOTA + P:C_IOTA + T], TT), per_channel(S_KMAX, P),
                                    ALU.is_equal).then_inc(sem(kind + "slots_ready"), 1)
                    v.tensor_copy(S_BIG[:, 0:1], S_KEY[:, 0:1]).then_inc(sem(kind + "h_ready"), 1)
                    dve_eng.wait_ge(sem(kind + "copied"), 3)
                    spill_sums(kind, og_spill[:, 512:D])
                for b in range(4):
                    half = slice((b % 2) * 512, (b % 2 + 1) * 512)
                    dve_eng.wait_ge(bank_full[b], dve.next(("full", b)))
                    v.scalar_tensor_tensor(y_nat[:, b // 2, half], x_nat[:, b // 2, half], ALPHA, banks[b][:, :], MUL, ADD).then_inc(bank_free[b], dve.sends(bank_free[b]))
                    if b % 2:
                        tile_stats(y_nat, b // 2)
                dve_eng.wait_ge(sem("rows_loaded"), 16 * (2 * i + 2))
                layer_norm(y_nat, x_nat, rows[:, 0:D], rows[:, D:2 * D], "x_first", "x_ready")

            dve_eng.wait_ge(dve.last, dve.value)

            def squares(src, a, n, dst):
                s = v3(sq[:, 0:a * n], a)
                v.tensor_tensor(s, src, src, MUL).then_inc(dve_step, dve.sends(dve_step))
                dve_eng.wait_ge(dve.last, dve.value)
                v.tensor_reduce(dst, s, AX, ADD).then_inc(dve_step, dve.sends(dve_step))

            def mean_eps(at, n, width, eps, last):
                ins = v.tensor_scalar(S_VAR[:, at:at + n], S_VAR[:, at:at + n], 1.0 / width, eps, MUL, ADD)
                if last:
                    ins.then_inc(sem("var_ready"), dve.sends(sem("var_ready")))
                else:
                    ins.then_inc(dve_step, dve.sends(dve_step))

            def scaled(view, r, gain, a, n):
                v.tensor_tensor(view, view, per_channel(r, n), MUL).then_inc(dve_step, dve.sends(dve_step))
                dve_eng.wait_ge(dve.last, dve.value)
                v.tensor_tensor(view, view, per_column(gain, a), MUL).then_inc(dve_step, dve.sends(dve_step))
                dve_eng.wait_ge(dve.last, dve.value)

            def rope(src, dst, nh):
                cos = bc(v3(cst[:, C_COS:C_COS + TT * HALF], TT).unsqueeze(2), P, TT, nh, HALF)
                sin = bc(v3(cst[:, C_SIN:C_SIN + TT * HALF], TT).unsqueeze(2), P, TT, nh, HALF)
                n = TT * nh * HALF
                t = [v4(sq[:, k * n:(k + 1) * n], TT, nh) for k in range(4)]
                lo, hi = src[:, :, :, 0:HALF], src[:, :, :, HALF:ROPE]
                v.tensor_tensor(t[0], lo, cos, MUL).then_inc(dve_step, dve.sends(dve_step))
                v.tensor_tensor(t[1], hi, sin, MUL).then_inc(dve_step, dve.sends(dve_step))
                v.tensor_tensor(t[2], hi, cos, MUL).then_inc(dve_step, dve.sends(dve_step))
                v.tensor_tensor(t[3], lo, sin, MUL).then_inc(dve_step, dve.sends(dve_step))
                dve_eng.wait_ge(dve.last, dve.value)
                if nh != NH:
                    t = [bc(s, P, TT, NH, HALF) for s in t]
                v.tensor_tensor(dst[:, :, :, 0:HALF], t[0], t[1], SUB).then_inc(dve_step, dve.sends(dve_step))
                return v.tensor_tensor(dst[:, :, :, HALF:ROPE], t[2], t[3], ADD)

            def flat3(ap):
                return ap.rearrange("p a b c -> p (a b) c")

            def shift(l, first, tiles, dcol=dcol):
                dve_eng.wait_ge(sem("shift_in"), dve.next("shift_in"))
                v.tensor_tensor(dcol[:, 0:tiles, :], pcol[:, 0:tiles, 0:T], pcol[:, 0:tiles, 1:T + 1], SUB).then_inc(dve_step, dve.sends(dve_step))
                dve_eng.wait_ge(dve.last, dve.value)
                for m in range(tiles):
                    mu = 12 + l * CP_LAYER + first + m
                    ins = v.scalar_tensor_tensor(sh[:, first + m, :], dcol[:, m, :], col[:, mu:mu + 1], pcol[:, m, 1:T + 1], MUL, ADD)
                    if m == tiles - 1:
                        ins.then_inc(sem("shift_done"), dve.sends(sem("shift_done")))
                    else:
                        ins.then_inc(dve_step, dve.sends(dve_step))

            def turned_qk(kdim):
                for dst, g, b in ((qTt, 0, 0), (qTt, 1, 1), (kTt, 0, 2), (kTt, 1, 3)):
                    copy_out(dst[0:kdim, 4 * g:4 * g + 4, 0:P], b, v3(banks[b][0:kdim, :], 4))

            def softmax(scale):
                for half in range(2):
                    for h in range(4 * half, 4 * half + 4):
                        b = h % NDB
                        dve_eng.wait_ge(bank_full[b], dve.next(("full", b)))
                        v.scalar_tensor_tensor(Pm[:, h, :], banks[b][:, 0:3 * P], scale, cst[:, C_CAUSAL:C_CAUSAL + 3 * P], MUL, ADD).then_inc(bank_free[b], dve.sends(bank_free[b]))
                    dve_eng.wait_ge(dve.last, dve.value)
                    hs, at = slice(4 * half, 4 * half + 4), 8 * half
                    v.tensor_reduce(S_MX[:, at:at + 4], Pm[:, hs, 0:P], AX, MAX).then_inc(dve_step, dve.sends(dve_step))
                    v.tensor_reduce(S_MX[:, at + 4:at + 8], Pm[:, hs, P:3 * P], AX, MAX).then_inc(dve_step, dve.sends(dve_step))
                    dve_eng.wait_ge(dve.last, dve.value)
                    v.tensor_scalar(S_NM[:, at:at + 8], S_MX[:, at:at + 8], -1.0, None, MUL).then_inc(sem("max_ready"), dve.sends(sem("max_ready")))

            def normalise():
                for half in range(2):
                    hs, at = slice(4 * half, 4 * half + 4), 8 * half
                    dve_eng.wait_ge(sem("exp_done"), dve.next("exp_done"))
                    v.reciprocal(S_RS[:, at:at + 8], S_SUM[:, at:at + 8]).then_inc(dve_step, dve.sends(dve_step))
                    dve_eng.wait_ge(dve.last, dve.value)
                    v.tensor_tensor(Pm[:, hs, 0:P], Pm[:, hs, 0:P], per_channel(S_RS[:, at:at + 4], P), MUL).then_inc(dve_step, dve.sends(dve_step))
                    v.tensor_tensor(Pm[:, hs, P:3 * P], Pm[:, hs, P:3 * P], per_channel(S_RS[:, at + 4:at + 8], T), MUL).then_inc(sem("p_ready"), dve.sends(sem("p_ready")))

            def gated_out(g):
                for j in range(4):
                    dve_eng.wait_ge(bank_full[j], dve.next(("full", j)))
                    v.tensor_tensor(oT[:, j, :], banks[j][:, 0:T], gates[:, g, j, :], MUL).then_inc(bank_free[j], dve.sends(bank_free[j]))

            def merge_half(n):
                half = slice(n * 512, (n + 1) * 512)
                dve_eng.wait_ge(sem("sgm_ready"), dve.next("sgm_ready"))
                for tt, b in ((0, 3), (1, 4)):
                    dve_eng.wait_ge(bank_full[b], dve.next(("full", b)))
                    v.tensor_tensor(sgm_half[:, tt, :], banks[b][:, :], sgm_half[:, tt, :], MUL).then_inc(bank_free[b], dve.sends(bank_free[b]))
                dve_eng.wait_ge(dve.last, dve.value)
                v.tensor_tensor(merged[:, :, half], merged[:, :, half], sgm_half, ADD).then_inc(sem("half_merged"), dve.sends(sem("half_merged")))

            def gated_y(tt):
                tok = slice(tt * P, (tt + 1) * P)
                dve_eng.wait_ge(bank_full[0], dve.next(("full", 0)))
                v.tensor_tensor(oT_c[:, :, tok], v3(banks[0][:, :], 4), gates[:, 0, :, tok], MUL).then_inc(bank_free[0], dve.sends(bank_free[0]))

            def merge(first):
                dve_eng.wait_ge(sem("sgm_ready"), dve.next("sgm_ready"))
                for n in range(2):
                    for tt in range(TT):
                        b = n + 2 * tt
                        dve_eng.wait_ge(bank_full[b], dve.next(("full", b)))
                        half = slice(n * 512, (n + 1) * 512)
                        o = merged[:, tt, half] if first else sgm[:, tt, half]
                        v.tensor_tensor(o, banks[b][:, :], sgm[:, tt, half], MUL).then_inc(bank_free[b], dve.sends(bank_free[b]))
                dve_eng.wait_ge(dve.last, dve.value)
                if not first:
                    v.tensor_tensor(merged, merged, sgm, ADD).then_inc(dve_step, dve.sends(dve_step))

            for l in range(DEPTH):
                v.tensor_tensor_reduce(out=y_nat[:, 1, :], in0=x_nat[:, 1, :], in1=x_nat[:, 1, :], scale=1.0, scalar=0.0,
                                       op0=MUL, op1=ADD, accum_out=S_VAR[:, 1:2]).then_inc(dve_step, dve.sends(dve_step))
                dve_eng.wait_ge(dve.last, dve.value)
                dve_eng.wait_ge(sem("first_squares"), l + 1)
                mean_eps(0, TT, D, RMS_EPS, True)
                roots(TT)
                dve_eng.wait_ge(sem("norm_loaded"), 16 * (l + 1))
                for tt in range(TT):
                    ins = v.scalar_tensor_tensor(y_nat[:, tt, :], x_nat[:, tt, :], S_RSTD[:, tt:tt + 1], norm_row, MUL, MUL)
                    if tt:
                        ins.then_inc(sem("h_ready2"), dve.sends(sem("h_ready2")))
                    else:
                        ins.then_inc(sem("h_first"), dve.sends(sem("h_first")))
                turned_x()
                dve_eng.wait_ge(sem("rows_loaded"), 16 * (2 * DEPTH + l + 1))
                for tt in range(TT):
                    copy_out(cnat[:, tt, :], tt, banks[tt][:, 0:LAT])
                dve_eng.wait_ge(dve.last, dve.value)
                for at, a, n in ((0, 0, 256), (2, 256, 128), (4, 384, ROPE)):
                    squares(cnat[:, :, a:a + n], TT, n, S_VAR[:, at:at + 2])
                    dve_eng.wait_ge(dve.last, dve.value)
                mean_eps(0, 2, 256, RMS_EPS, False)
                mean_eps(2, 2, 128, RMS_EPS, False)
                mean_eps(4, 2, ROPE, RMS_EPS, True)
                roots(6)
                scaled(cnat[:, :, 384:LAT], S_RSTD[:, 4:6], rowv("kr"), TT, ROPE)
                scaled(cnat[:, :, 0:256], S_RSTD[:, 0:2], rowv("qa"), TT, 256)
                v.tensor_tensor(cnat[:, :, 256:384], cnat[:, :, 256:384], per_channel(S_RSTD[:, 2:4], 128), MUL).then_inc(dve_step, dve.sends(dve_step))
                dve_eng.wait_ge(dve.last, dve.value)
                v.tensor_tensor(cnat[:, :, 256:384], cnat[:, :, 256:384], per_column(rowv("kva"), TT), MUL).then_inc(sem("lat_ready"), dve.sends(sem("lat_ready")))
                n = TT * NH
                lf, lfe, neg = ffn[:, 0:n], ffn[:, n:2 * n], ffn[:, 2 * n:3 * n]
                dve_eng.wait_ge(bank_full[4], dve.next(("full", 4)))
                v.tensor_tensor(v3(lf, TT), v3(banks[4][:, 0:n], TT), per_column(rowv("bf"), TT), ADD).then_inc(bank_free[4], dve.sends(bank_free[4]))
                dve_eng.wait_ge(dve.last, dve.value)
                v.tensor_scalar(neg, lf, -1.0, None, MUL).then_inc(dve_step, dve.sends(dve_step))
                dve_eng.wait_ge(dve.last, dve.value)
                v.tensor_tensor(lfe, lf, neg, MIN).then_inc(sem("gates_neg"), dve.sends(sem("gates_neg")))
                v.tensor_scalar(lf, lf, 0.0, None, MIN).then_inc(dve_step, dve.sends(dve_step))
                dve_eng.wait_ge(dve.last, dve.value)
                v.memset(pcol[:, :, 0:1], 0.0).then_inc(dve_step, dve.sends(dve_step))
                dve_eng.wait_ge(dve.last, dve.value)
                for t in range(0, 4, 2):
                    shift(l, t, 2, v3(sq[:, 0:2 * T], 2))
                copy_out(cT[:, 0:2, :], 2, v3(banks[2][:, :], 2))
                copy_out(cT[:, 2, :], 3, banks[3][:, 0:T])
                dve_eng.wait_ge(dve.last, dve.value)
                dve_eng.wait_ge(sem("gates_ln"), dve.next("gates_ln"))
                v.tensor_tensor(lf, lf, lfe, SUB).then_inc(sem("logf_ready"), dve.sends(sem("logf_ready")))
                for n4 in range(2):
                    for tt in range(TT):
                        b = 2 * n4 + tt
                        copy_out(qn[:, tt, 4 * n4:4 * n4 + 4, :], b, v3(banks[b][:, 0:4 * QK], 4))
                dve_eng.wait_ge(dve.last, dve.value)
                dve_eng.wait_ge(sem("kv_ready"), dve.next("kv_ready"))
                qf, kf = flat3(qn), flat3(kn)
                squares(qf, TT * NH, QK, S_VAR[:, 0:16])
                dve_eng.wait_ge(dve.last, dve.value)
                squares(kf[:, :, 0:NOPE], TT * NH, NOPE, S_VAR[:, 16:32])
                dve_eng.wait_ge(dve.last, dve.value)
                mean_eps(0, 16, QK, RMS_EPS, False)
                mean_eps(16, 16, NOPE, RMS_EPS, True)
                roots(32)
                scaled(qf, S_RSTD[:, 0:16], rowv("q"), TT * NH, QK)
                scaled(kf[:, :, 0:NOPE], S_RSTD[:, 16:32], rowv("kn"), TT * NH, NOPE)
                rope(qn[:, :, :, NOPE:QK], qn[:, :, :, NOPE:QK], NH).then_inc(dve_step, dve.sends(dve_step))
                dve_eng.wait_ge(dve.last, dve.value)
                krope = rope(cnat[:, :, 384:LAT].unsqueeze(2), kn[:, :, :, NOPE:QK], 1)
                krope.then_inc(sem("qk_ready"), dve.sends(sem("qk_ready")))
                for t in range(4, 8, 2):
                    shift(l, t, 2)
                turned_qk(QK)
                softmax(QK ** -0.5)
                cum_sb = neg
                copy_out(cum_sb, 4, banks[4][:, 0:TT * NH])
                for tt in range(TT):
                    copy_out(qn[:, tt, :, 0:HC], tt, v3(banks[tt][:, :], NH))
                for tt in range(TT):
                    copy_out(kn[:, tt, :, 0:HC], 2 + tt, v3(banks[2 + tt][:, :], NH))
                normalise()
                dve_eng.wait_ge(dve.last, dve.value)
                sqf = flat2(sgm)
                for src, at in ((qf, 0), (kf, 16)):
                    s = v3(sqf[:, 0:TT * NH * HC], TT * NH)
                    v.tensor_tensor(s, src[:, :, 0:HC], src[:, :, 0:HC], MUL).then_inc(dve_step, dve.sends(dve_step))
                    dve_eng.wait_ge(dve.last, dve.value)
                    v.tensor_reduce(S_VAR[:, at:at + 16], s, AX, ADD).then_inc(dve_step, dve.sends(dve_step))
                    dve_eng.wait_ge(dve.last, dve.value)
                mean_eps(0, 32, HC, RMS_EPS, True)
                roots(32)
                scaled(qf[:, :, 0:HC], S_RSTD[:, 0:16], rowv("fq"), TT * NH, HC)
                scaled(kf[:, :, 0:HC], S_RSTD[:, 16:32], rowv("fk"), TT * NH, HC)
                v.tensor_scalar(qf[:, :, 0:HC], qf[:, :, 0:HC], HC ** -0.5, None, MUL).then_inc(dve_step, dve.sends(dve_step))
                cum3 = cum_sb.unsqueeze(2)
                v.tensor_copy(qf[:, :, HC:HC + 1], cum3).then_inc(dve_step, dve.sends(dve_step))
                v.memset(qf[:, :, HC + 1:HC + 2], 1.0).then_inc(dve_step, dve.sends(dve_step))
                v.memset(kf[:, :, HC:HC + 1], 1.0).then_inc(dve_step, dve.sends(dve_step))
                v.tensor_scalar(kf[:, :, HC + 1:HC + 2], cum3, -1.0, None, MUL).then_inc(sem("qk_ready"), dve.sends(sem("qk_ready")))
                gated_out(0)
                for t in range(8, 12, 2):
                    shift(l, t, 2)
                shift(l, 12, 1)
                dve_eng.wait_ge(dve.last, dve.value)
                if l:
                    v.tensor_copy(S_BIG[:, 0:1], sh[:, 12, 0:1]).then_inc(sem("shift_ready"), dve.sends(sem("shift_ready")))
                turned_qk(FOXK)
                softmax(1.0)
                merge(True)
                if l:
                    copy_out(v_mid, 4, banks[4][0:32, 0:T])
                normalise()
                if l == 0:
                    v.tensor_copy(vfirst, vlT).then_inc(dve_step, dve.sends(dve_step))
                else:
                    for g in range(2):
                        dve_eng.wait_ge(bank_full[g], dve.next(("full", g)))
                        v.tensor_tensor(nuT[:, 2 * g:2 * g + 2, :], v3(banks[g][:, :], 2), per_channel(colv(l, V0)[:, 2 * g:2 * g + 2], T), ADD).then_inc(bank_free[g], dve.sends(bank_free[g]))
                    dve_eng.wait_ge(dve.last, dve.value)
                    v.tensor_tensor(vdiff, vfirst, vlT, SUB).then_inc(sem("nu_in"), dve.sends(sem("nu_in")))
                    dve_eng.wait_ge(sem("nu_ready"), dve.next("nu_ready"))
                    dve_eng.wait_ge(dve.last, dve.value)
                    v.tensor_tensor(vdiff, vdiff, nuT, MUL).then_inc(dve_step, dve.sends(dve_step))
                    dve_eng.wait_ge(dve.last, dve.value)
                    v.tensor_tensor(vlT, vlT, vdiff, ADD).then_inc(dve_step, dve.sends(dve_step))
                gated_out(1)
                dve_eng.wait_ge(dve.last, dve.value)
                for tt in range(TT):
                    tok = slice(tt * P, (tt + 1) * P)
                    r_, k_, v_ = rlT[:, :, tok], klT[:, :, tok], vlT[:, :, tok]
                    v.tensor_copy(S_BIG[:, 0:1], sh[:, 12, 0:1]).then_inc(sem("shift_all"), dve.sends(sem("shift_all")))
                    v.tensor_tensor(kk, k_, per_channel(colv(l, KK), P), MUL).then_inc(dve_step, dve.sends(dve_step))
                    dve_eng.wait_ge(dve.last, dve.value)
                    v.tensor_tensor(t1, kk, kk, MUL).then_inc(sem("ksq_ready"), dve.sends(sem("ksq_ready")))
                    if tt:
                        gated_y(0)
                    dve_eng.wait_ge(bank_full[0], dve.next(("full", 0)))
                    v.tensor_tensor(lw, v3(banks[0][:, :], 4), per_channel(colv(l, W0), P), ADD).then_inc(bank_free[0], dve.sends(bank_free[0]))
                    dve_eng.wait_ge(bank_full[1], dve.next(("full", 1)))
                    v.tensor_tensor(aa, v3(banks[1][:, :], 4), per_channel(colv(l, A0), P), ADD).then_inc(bank_free[1], dve.sends(bank_free[1]))
                    dve_eng.wait_ge(dve.last, dve.value)
                    v.tensor_copy(S_BIG[:, 0:1], sh[:, 12, 0:1]).then_inc(sem("wa_in"), dve.sends(sem("wa_in")))
                    dve_eng.wait_ge(bank_full[2], dve.next(("full", 2)))
                    v.tensor_scalar(flat2(t1), banks[2][:, :], 1e-24, None, MAX).then_inc(bank_free[2], dve.sends(bank_free[2]))
                    dve_eng.wait_ge(dve.last, dve.value)
                    v.tensor_copy(S_BIG[:, 0:1], sh[:, 12, 0:1]).then_inc(sem("ksum_ready"), dve.sends(sem("ksum_ready")))
                    dve_eng.wait_ge(sem("wa_ready"), dve.next("wa_ready"))
                    v.tensor_scalar(flat2(lw), flat2(lw), DECAY, None, MUL).then_inc(dve_step, dve.sends(dve_step))
                    dve_eng.wait_ge(dve.last, dve.value)
                    v.tensor_tensor_scan(flat2(cum), cst[:, C_SCAN:C_SCAN + 4 * P], flat2(lw), 0.0, MUL, ADD).then_inc(dve_step, dve.sends(dve_step))
                    dve_eng.wait_ge(dve.last, dve.value)
                    v.tensor_tensor(pex, cum, lw, SUB).then_inc(sem("cum_ready"), dve.sends(sem("cum_ready")))
                    dve_eng.wait_ge(sem("knorm_ready"), dve.next("knorm_ready"))
                    v.reciprocal(flat2(t1), flat2(t1)).then_inc(dve_step, dve.sends(dve_step))
                    dve_eng.wait_ge(dve.last, dve.value)
                    v.tensor_tensor(kk, kk, t1, MUL).then_inc(dve_step, dve.sends(dve_step))
                    dve_eng.wait_ge(dve.last, dve.value)
                    v.tensor_scalar(flat2(t1), flat2(aa), -1.0, None, ADD).then_inc(dve_step, dve.sends(dve_step))
                    dve_eng.wait_ge(dve.last, dve.value)
                    v.tensor_tensor(t1, t1, per_channel(colv(l, KA), P), MUL).then_inc(dve_step, dve.sends(dve_step))
                    dve_eng.wait_ge(dve.last, dve.value)
                    v.tensor_scalar(flat2(t1), flat2(t1), 1.0, None, ADD).then_inc(dve_step, dve.sends(dve_step))
                    dve_eng.wait_ge(dve.last, dve.value)
                    v.tensor_tensor(km, t1, k_, MUL).then_inc(dve_step, dve.sends(dve_step))
                    dve_eng.wait_ge(dve.last, dve.value)
                    v.tensor_scalar(flat2(aa), flat2(aa), -1.0, None, MUL).then_inc(dve_step, dve.sends(dve_step))
                    dve_eng.wait_ge(sem("decay_ready"), dve.next("decay_ready"))
                    v.tensor_copy(pcs.unsqueeze(2), pp.rearrange("p a (c t) -> p (a c) t", c=2)[:, :, CH - 1:CH]).then_inc(dve_step, dve.sends(dve_step))
                    dve_eng.wait_ge(dve.last, dve.value)
                    v.tensor_tensor(aa, aa, kk, MUL).then_inc(dve_step, dve.sends(dve_step))
                    dve_eng.wait_ge(dve.last, dve.value)
                    v.tensor_tensor(pex, pex, kk, MUL).then_inc(dve_step, dve.sends(dve_step))
                    v.tensor_tensor(aa, aa, pinv, MUL).then_inc(dve_step, dve.sends(dve_step))
                    dve_eng.wait_ge(dve.last, dve.value)
                    v.tensor_tensor(pinv, pinv, km, MUL).then_inc(dve_step, dve.sends(dve_step))
                    dve_eng.wait_ge(dve.last, dve.value)

                    def to_end(dst, src):
                        return v.tensor_tensor(dst.rearrange("p a (c t) -> p (a c) t", c=2), src.rearrange("p a (c t) -> p (a c) t", c=2),
                                               per_channel(pcs, CH), MUL)

                    v.tensor_tensor(pp, pp, r_, MUL).then_inc(sem("rows_ready"), dve.sends(sem("rows_ready")))
                    to_end(cum, aa).then_inc(dve_step, dve.sends(dve_step))
                    to_end(lw, pinv).then_inc(dve_step, dve.sends(dve_step))
                    v.tensor_tensor(rk, km, r_, MUL).then_inc(dve_step, dve.sends(dve_step))
                    dve_eng.wait_ge(dve.last, dve.value)
                    v.tensor_tensor(rk, rk, per_channel(colv(l, RK), P), MUL).then_inc(sem("ends_ready"), dve.sends(sem("ends_ready")))
                    merge_half(tt)
                    for par in range(2):
                        copy_out(NTm[:, par, :, :], 0, v3(banks[0][:, :], 4))
                        for b, dst, mask in ((1, MTm, C_STRICT), (2, AkT, C_INCL), (3, AbT, C_INCL)):
                            dve_eng.wait_ge(bank_full[b], dve.next(("full", b)))
                            v.tensor_tensor(dst[:, par, :, :], v3(banks[b][:, :], 4), mat4(mask), MUL).then_inc(bank_free[b], dve.sends(bank_free[b]))
                    dve_eng.wait_ge(bank_full[4], dve.next(("full", 4)))
                    v.tensor_copy(S_RS[:, 0:NH], banks[4][:, 0:NH]).then_inc(dve_step, dve.sends(dve_step))
                    v.tensor_copy(pc0[0:64, :], banks[4][0:64, 64:80]).then_inc(bank_free[4], dve.sends(bank_free[4]))
                    copy_out(Kp, 3, banks[3][:, :])
                    dve_eng.wait_ge(dve.last, dve.value)
                    for par in range(2):
                        v.tensor_tensor(Nl[:, par, :, :], NTm[:, par, :, :], mat4(C_LEV), MUL).then_inc(dve_step, dve.sends(dve_step))
                        dve_eng.wait_ge(dve.last, dve.value)
                        v.tensor_tensor(TTm[:, par, :, :], Nl[:, par, :, :], mat4(C_ID), ADD).then_inc(sem("level_ready"), dve.sends(sem("level_ready")))
                    for par in range(2):
                        copy_out(Tm[:, par, :, :], par, v3(banks[par][:, :], 4))
                        dve_eng.wait_ge(dve.last, dve.value)
                        v.tensor_tensor(Nl[:, par, :, :], NTm[:, par, :, :], mat4(C_LEV + P), MUL).then_inc(sem("level_ready"), dve.sends(sem("level_ready")))
                    for lev in range(1, LEVELS):
                        for par in range(2):
                            if lev < LEVELS - 1:
                                dve_eng.wait_ge(bank_full[2 * par], dve.next(("full", 2 * par)))
                                v.tensor_tensor(Tm[:, par, :, :], Tm[:, par, :, :], v3(banks[2 * par][:, :], 4), ADD).then_inc(bank_free[2 * par], dve.sends(bank_free[2 * par]))
                            dve_eng.wait_ge(bank_full[2 * par + 1], dve.next(("full", 2 * par + 1)))
                            v.tensor_tensor(TTm[:, par, :, :], TTm[:, par, :, :], v3(banks[2 * par + 1][:, :], 4), ADD).then_inc(bank_free[2 * par + 1], dve.sends(bank_free[2 * par + 1]))
                            if lev < LEVELS - 1:
                                v.tensor_tensor(Nl[:, par, :, :], NTm[:, par, :, :], mat4(C_LEV + (lev + 1) * P), MUL).then_inc(sem("level_ready"), dve.sends(sem("level_ready")))
                    copy_out(Wn, 2, banks[2][:, :])
                    copy_out(mv, 3, banks[3][:, :])
                    copy_out(uv, 4, banks[4][:, :])
                    chunks = (0, 1) if tt == 0 else (0,)
                    for c in chunks:
                        g = 2 * tt + c
                        if g:
                            shape = [64, 4, 2, HC]
                            diag = ysq[0:64, :]
                            dec = pc0[0:64, :].rearrange("p (b a c) -> p a b c", b=2, c=2)[:, :, :, c:c + 1]
                            v.tensor_tensor(v4(diag, 4, 2), bc(mat(C_ID)[0:64, 0:64].unsqueeze(1).unsqueeze(1), *shape), bc(dec, *shape), MUL).then_inc(dve_step, dve.sends(dve_step))
                            dve_eng.wait_ge(dve.last, dve.value)
                            dve_eng.wait_ge(bank_full[c], dve.next(("full", c)))
                            v.tensor_tensor(GT[0:64, c, :, :], v3(banks[c][0:64, :], NH), v3(diag, NH), ADD).then_inc(bank_free[c], dve.sends(bank_free[c]))
                            copy_out(Hs[0:64, c, :], 2 + c, banks[2 + c][0:64, :])
                        else:
                            copy_out(states[0][0:64, :], 2, banks[2][0:64, :])
                    dve_eng.wait_ge(dve.last, dve.value)
                    for c in chunks:
                        g = 2 * tt + c
                        if g:
                            dve_eng.wait_ge(bank_full[4], dve.next(("full", 4)))
                            v.tensor_tensor(states[g][0:64, :], banks[4][0:64, :], Hs[0:64, c, :], ADD).then_inc(bank_free[4], dve.sends(bank_free[4]))
                    copy_out(yv, 4, banks[4][:, :])
                    dve_eng.wait_ge(dve.last, dve.value)
                    y3, q3 = v3(yv, NH), v3(ysq, NH)
                    v.tensor_reduce(S_MX[:, 0:NH], y3, AX, ADD).then_inc(dve_step, dve.sends(dve_step))
                    dve_eng.wait_ge(dve.last, dve.value)
                    v.tensor_scalar(S_MX[:, 0:NH], S_MX[:, 0:NH], 1.0 / HC, None, MUL).then_inc(dve_step, dve.sends(dve_step))
                    dve_eng.wait_ge(dve.last, dve.value)
                    v.tensor_tensor(y3, y3, per_channel(S_MX[:, 0:NH], HC), SUB).then_inc(dve_step, dve.sends(dve_step))
                    dve_eng.wait_ge(dve.last, dve.value)
                    v.tensor_tensor(ysq, yv, yv, MUL).then_inc(dve_step, dve.sends(dve_step))
                    dve_eng.wait_ge(dve.last, dve.value)
                    v.tensor_reduce(S_VAR[:, 0:NH], q3, AX, ADD).then_inc(dve_step, dve.sends(dve_step))
                    dve_eng.wait_ge(dve.last, dve.value)
                    mean_eps(0, NH, HC, GN_EPS, True)
                    roots(NH)
                    v.tensor_tensor(y3, y3, per_channel(S_RSTD[:, 0:NH], HC), MUL).then_inc(dve_step, dve.sends(dve_step))
                    dve_eng.wait_ge(dve.last, dve.value)
                    v.tensor_tensor(yv, yv, rowv("lg"), MUL).then_inc(dve_step, dve.sends(dve_step))
                    dve_eng.wait_ge(dve.last, dve.value)
                    v.tensor_tensor(q3, v3(Vn, NH), per_channel(S_RS[:, 0:NH], HC), MUL).then_inc(dve_step, dve.sends(dve_step))
                    v.tensor_tensor(yv, yv, rowv("lb"), ADD).then_inc(dve_step, dve.sends(dve_step))
                    dve_eng.wait_ge(dve.last, dve.value)
                    v.tensor_tensor(yv, yv, ysq, ADD).then_inc(sem("y_ready"), dve.sends(sem("y_ready")))
                gated_y(1)
                merge(False)
                dve_eng.wait_ge(dve.last, dve.value)
                v.tensor_copy(S_BIG[:, 0:1], merged[:, 1, D - 1:D]).then_inc(sem("merged_ready"), dve.sends(sem("merged_ready")))
                turned_x()
                for n in range(2):
                    for tt in range(TT):
                        b = n + 2 * tt
                        dve_eng.wait_ge(bank_full[b], dve.next(("full", b)))
                        half = slice(n * 512, (n + 1) * 512)
                        v.tensor_tensor(x_nat[:, tt, half], x_nat[:, tt, half], banks[b][:, :], ADD).then_inc(bank_free[b], dve.sends(bank_free[b]))
                        if n and tt == 0 and l + 1 < DEPTH:
                            dve_eng.wait_ge(dve.last, dve.value)
                            v.tensor_copy(S_BIG2[:, 0:1], x_nat[:, 0, D - 1:D]).then_inc(sem("x_first"), dve.sends(sem("x_first")))
                dve_eng.wait_ge(dve.last, dve.value)
                v.tensor_copy(S_BIG[:, 0:1], x_nat[:, 1, D - 1:D]).then_inc(sem("x_ready"), dve.sends(sem("x_ready")))


def constants():
    import numpy as np
    c = np.zeros((P, NCONST), np.float32)
    i, t = np.arange(P)[:, None], np.arange(P)[None, :]
    same = i // CH == t // CH
    c[:, C_ID:C_ID + P] = i == t
    c[:, C_STRICT:C_STRICT + P] = (i < t) & same
    c[:, C_INCL:C_INCL + P] = (i <= t) & same
    c[:, C_BLOCK:C_BLOCK + P] = same
    c[:, C_TRI:C_TRI + P] = i <= t
    c[:, C_ONES:C_ONES + P] = 1
    for n in range(LEVELS):
        b = 1 << n
        c[:, C_LEV + n * P:C_LEV + (n + 1) * P] = (i // (2 * b) == t // (2 * b)) & (i % (2 * b) < b) & (t % (2 * b) >= b)
    causal = np.where(t <= i, 0.0, -1e30)
    c[:, C_CAUSAL:C_CAUSAL + P] = causal
    c[:, C_CAUSAL + 2 * P:C_CAUSAL + 3 * P] = causal
    c[:, C_SCAN:C_SCAN + 4 * P] = np.arange(4 * P)[None, :] % CH != 0
    inv = np.float32(10000.0) ** (-np.arange(0, ROPE, 2, dtype=np.float32) / ROPE)
    ang = np.arange(T, dtype=np.float32)[:, None] * inv[None, :].astype(np.float32)
    for at, f in ((C_COS, np.cos), (C_SIN, np.sin)):
        c[:, at:at + TT * HALF] = f(ang).reshape(TT, P, HALF).transpose(1, 0, 2).reshape(P, -1)
    for j in range(4):
        for m in range(2):
            c[64 * m:64 * m + 64, C_SEL + j * NH + 2 * j + m] = 1
    own, other = np.arange(GS)[:, None], np.arange(GS)[None, :]
    c[:, C_TIE:C_TIE + GS * GS] = (other < own).reshape(1, -1)
    c[:, C_IOTA:C_IOTA + T] = np.arange(1, T + 1)[None, :]
    return c


def kernel(**inputs):
    import numpy as np
    import concourse.bacc as bacc
    from concourse import mybir
    from concourse.bass_utils import run_bass_kernel_spmd

    a = {k: np.asarray(v) for k, v in inputs.items()}

    def tiles(w):
        k, n = w.shape
        return w.reshape(k // P, P, n).transpose(1, 0, 2).reshape(P, -1)

    def cut(w, edges):
        return [tiles(w[:, lo:hi]) for lo, hi in zip(edges[:-1], edges[1:])]

    def chan(w):
        return w.reshape(-1, P).T

    def cat(parts):
        return np.ascontiguousarray(np.concatenate(parts, axis=1))

    halves, half3, half4 = (0, 512, 1024), (0, 512, 1024, 1536), (0, 512, 1024, 1536, 2048)
    w_kv, w_in = [cut(w, halves) for w in a["w_kv"]], [cut(a["w_in_a"][0], half3), cut(a["w_in_b"][0], half4)]
    w_o = [cut(w, halves) for w in a["w_out"]]
    first = [cat([w_kv[0][0], w_in[0][2], w_in[0][0], w_in[0][1], w_kv[0][1], w_kv[1][0]] + w_o[0] + [w_kv[1][1]]),
             cat([w_in[1][3]] + w_in[1][0:3] + w_o[1])]
    moe = np.empty((DEPTH, NG, GS * PER_EXPERT, P, SLOT), np.float32)
    for s, (name, e) in enumerate(GROUP_SLOTS):
        w = a["w_" + name][:, e::GS]
        moe[:, :, s] = w.reshape(DEPTH, NG, -1, P, w.shape[-1]).transpose(0, 1, 3, 2, 4).reshape(DEPTH, NG, P, SLOT)

    at = np.cumsum([0, LAT, MIX, MIX, MIX, MIX, NH, MIX, MIX, MIX, MIX, 128, MIX])
    c_lat, c_ga, c_fq, c_fk, c_fv, c_ff, c_gb, c_r, c_k, c_v, c_wa, c_gc, c_mg = at
    second, ff, lora, cols, rows2 = [], [], [], [], []
    colp = [a["conv_w"][0].reshape(3, 4, P).transpose(2, 1, 0).reshape(P, 12)]
    for l in range(DEPTH):
        w = a["w_in_2"][l]

        def c(lo, n=MIX):
            return tiles(w[:, lo:lo + n])

        parts = [c(c_lat, LAT), c(c_ga), c(c_r), tiles(a["mla_w_uq_2"][l]), tiles(a["mla_w_ukv_2"][l]), c(c_k), c(c_fq), c(c_fk),
                 c(c_fv), c(c_gb), c(c_v), c(c_wa, P)]
        parts += [tiles(a["w_pa_2"][l]), c(c_mg), c(c_mg + 512), c(c_gc)]
        pb = cut(a["w_pb_2"][l], halves)
        parts += [pb[0], c(c_mg + 1024), pb[1], c(c_mg + 1536), c(c_mg + 2048), c(c_mg + 2560), tiles(a["w_pc_2"][l])] + cut(a["w_out_2"][l], halves)
        assert [p.shape[1] for p in parts] == LOADS_SECOND
        second.append(cat(parts))
        ff.append(c(c_ff, NH).reshape(P, KD, NH))
        lo = np.zeros((P, 1152), np.float32)
        lo[0:64, 0:512], lo[64:128, 0:512] = a["rwkv_w_up_2"][l], a["rwkv_a_up_2"][l]
        lo[:, 512:640] = tiles(a["rwkv_v_down_2"][0])
        lo[0:32, 640:1152] = a["rwkv_v_up_2"][0]
        lora.append(lo)
        colp += [chan(a[n + "_2"][l].reshape(-1)) for n in ("rwkv_mu", "rwkv_w0", "rwkv_a0", "rwkv_k_k", "rwkv_k_a", "rwkv_r_k")]
        colp.append(chan(a["rwkv_v0_2"][0]))
        rows2.append(np.concatenate([a[n + "_2"][l] for n in ("norm_g", "mla_qa_g", "mla_kva_g", "mla_q_g", "mla_knope_g", "mla_krope_g",
                                                             "fox_q_g", "fox_k_g", "fox_b_f", "rwkv_lnx_g", "rwkv_lnx_b")]))
    tokens = a["x"][0]
    arrays = {
        "x0": tokens.reshape(TT, P, D).transpose(1, 0, 2), "x0T": tokens.T.reshape(KD, P, T).transpose(1, 0, 2),
        "memT0": a["mem"][0].T.reshape(KD, P, T).transpose(1, 0, 2), "sguT": a["sgu_w"][0].transpose(2, 0, 1),
        "wfirst0": first[0], "wfirst1": first[1], "wmoe": moe.reshape(DEPTH, NG // 2, 2 * GS * PER_EXPERT, P, SLOT), "wsecond": np.stack(second), "wff": np.stack(ff),
        "lora": np.stack(lora), "rw": tiles(a["router_w"]).reshape(P, KD, NE), "consts": constants(), "colp": np.concatenate(colp, axis=1),
        "rowa": np.concatenate([a["sgu_ln_g"][0], a["sgu_ln_b"][0], a["sgu_b"][0].reshape(-1), a["router_b"]])[None],
        "lnrows": np.stack([np.concatenate([a[g][i], a[b][i]]) for i in range(DEPTH) for g, b in (("ln1_g", "ln1_b"), ("ln2_g", "ln2_b"))]),
        "rows2": np.stack(rows2),
    }
    arrays = {k: np.ascontiguousarray(v) for k, v in arrays.items()}
    nc = bacc.Bacc("TRN2", target_bir_lowering=False, num_devices=1)
    aps = [nc.dram_tensor(k, v.shape, mybir.dt.float32, kind="ExternalInput").ap() for k, v in arrays.items()]
    out = nc.dram_tensor("out", (P, TT, D), mybir.dt.float32, kind="ExternalOutput").ap()
    two_blocks(nc, *aps, out)
    r = run_bass_kernel_spmd(nc, [arrays], core_ids=[0])
    got = r.results[0]["out"]
    return got.transpose(1, 0, 2).reshape(1, T, D)
```
